# Optimizing a Trainium2 kernel written in Bass

```python
import math
import jax, jax.numpy as jnp
from jax import lax
import numpy as np

D_MODEL = 1024
BATCH = 1
SEQ = 1024
DEPTH = 1
DEC_BATCH = 8
DEC_SEQ = 4
PAST_LEN = 256
PAGE_SIZE = 128

MIX_WIDTH = D_MODEL
M_HEADS = 4
M_HEAD_DIM = MIX_WIDTH // 2 // M_HEADS
M_WIDTH = M_HEADS * M_HEAD_DIM
M_CHUNK = 64
A_HEADS = 8
A_HEAD_DIM = (MIX_WIDTH - M_WIDTH) // A_HEADS
A_WIDTH = A_HEADS * A_HEAD_DIM
IDX_HEADS = 8
IDX_DIM = 64
TOPK_MAX = 256
Q_BLOCK = 128
ROPE_THETA = 500000.0
ROT_FRACTION = 4
D_FF = -(-8 * D_MODEL // (3 * 256)) * 256
ALPHA = (2 * DEPTH) ** 0.25
BETA = (8 * DEPTH) ** -0.25
LN_EPS = 1e-5
IN_SPLITS = (M_WIDTH, M_WIDTH, M_WIDTH, M_WIDTH, M_HEADS, M_HEADS,
             A_WIDTH, A_WIDTH, A_WIDTH,
             IDX_HEADS * IDX_DIM, IDX_DIM, IDX_HEADS)
IN_DIM = sum(IN_SPLITS)

kernel_name = "hymba_mlstm_dsa_deepnorm_step"

def layer_norm(x, g, b):
    xf = x.astype(jnp.float32)
    mu = xf.mean(-1, keepdims=True)
    var = jnp.square(xf - mu).mean(-1, keepdims=True)
    return ((xf - mu) * lax.rsqrt(var + LN_EPS) * g.astype(jnp.float32) + b.astype(jnp.float32)).astype(x.dtype)

def partial_rope(x, pos):
    rot = x.shape[-1] // ROT_FRACTION
    half = rot // 2
    inv = ROPE_THETA ** (-jnp.arange(half, dtype=jnp.float32) / half)
    ang = pos.astype(jnp.float32)[:, None] * inv[None, :]
    cos = jnp.cos(ang)[:, None, :]
    sin = jnp.sin(ang)[:, None, :]
    x1 = x[..., :half]
    x2 = x[..., half:rot]
    return jnp.concatenate([x1 * cos - x2 * sin, x2 * cos + x1 * sin, x[..., rot:]], axis=-1)

def mixer_streams(x, pos, w_in, b_gate):
    B, T, _ = x.shape
    z = jnp.einsum('btd,de->bte', x, w_in).astype(jnp.float32)
    split_points = np.cumsum(IN_SPLITS)[:-1].tolist()
    mq, mk, mv, mo, mi, mf, aq, ak, av, iq, ik, iw = jnp.split(z, split_points, axis=-1)
    heads = lambda a, h: a.reshape(B, T, h, -1)
    bg = b_gate.astype(jnp.float32)
    i_pre = mi + bg[:M_HEADS]
    log_f = jax.nn.log_sigmoid(mf + bg[M_HEADS:])
    mlstm = (heads(mq, M_HEADS), heads(mk, M_HEADS) * (M_HEAD_DIM ** -0.5), heads(mv, M_HEADS), mo, i_pre, log_f)
    q = partial_rope(heads(aq, A_HEADS), pos)
    k = partial_rope(heads(ak, A_HEADS), pos)
    v = heads(av, A_HEADS)
    qi = partial_rope(heads(iq, IDX_HEADS), pos) * (IDX_DIM ** -0.5)
    ki = partial_rope(ik[:, :, None, :], pos)[:, :, 0, :]
    wi = iw * (IDX_HEADS ** -0.5)
    return mlstm, (q, k, v, qi, ki, wi)

def mlstm_mixer(streams, C0, n0, m0):
    q, k, v, o_pre, i_pre, log_f = streams
    B, T, H, Dh = q.shape
    c = math.gcd(T, M_CHUNK)
    nc = T // c

    def to_chunks(a):
        a = a.reshape((B, nc, c) + a.shape[2:])
        return jnp.moveaxis(jnp.moveaxis(a, 1, 0), 3, 2)

    causal = jnp.tril(jnp.ones((c, c), dtype=bool))

    def step(carry, inp):
        C, n, m = carry
        qc, kc, vc, ic, fc = inp
        F = jnp.cumsum(fc, axis=-1)
        Dlog = jnp.where(causal, F[..., :, None] - F[..., None, :] + ic[..., None, :], -jnp.inf)
        inter = m[..., None] + F
        m_t = jnp.maximum(Dlog.max(-1), inter)
        W = jnp.exp(Dlog - m_t[..., None])
        g = jnp.exp(inter - m_t)
        S = jnp.einsum('bhtd,bhsd->bhts', qc, kc) * W
        num = jnp.einsum('bhts,bhse->bhte', S, vc) + g[..., None] * jnp.einsum('bhtd,bhde->bhte', qc, C)
        den = S.sum(-1) + g * jnp.einsum('bhtd,bhd->bht', qc, n)
        h = num / jnp.maximum(jnp.abs(den), jnp.exp(-m_t))[..., None]
        FL = F[..., -1]
        a = FL[..., None] - F + ic
        m_new = jnp.maximum(m + FL, a.max(-1))
        wk = jnp.exp(a - m_new[..., None])
        gC = jnp.exp(m + FL - m_new)
        C_new = gC[..., None, None] * C + jnp.einsum('bhs,bhsd,bhse->bhde', wk, kc, vc)
        n_new = gC[..., None] * n + jnp.einsum('bhs,bhsd->bhd', wk, kc)
        return (C_new, n_new, m_new), h

    init = (C0.astype(jnp.float32), n0.astype(jnp.float32), m0.astype(jnp.float32))
    (C, n, m), h = lax.scan(step, init, (to_chunks(q), to_chunks(k), to_chunks(v), to_chunks(i_pre), to_chunks(log_f)))
    h = jnp.moveaxis(jnp.moveaxis(h, 2, 3), 0, 1).reshape(B, T, H * Dh)
    return h * jax.nn.sigmoid(o_pre), (C, n, m)

def index_scores(qi, wi, ki):
    r = jax.nn.relu(jnp.einsum('bthd,bsd->bths', qi, ki.astype(jnp.float32)))
    return jnp.einsum('bths,bth->bts', r, wi)

def sparse_attend(q, k_sel, v_sel, valid):
    s = jnp.einsum('bthd,btkhd->bthk', q, k_sel.astype(jnp.float32)) * (q.shape[-1] ** -0.5)
    p = jax.nn.softmax(jnp.where(valid[:, :, None, :], s, -jnp.inf), axis=-1)
    return jnp.einsum('bthk,btkhd->bthd', p, v_sel.astype(jnp.float32))

def dsa_prompt(q, k, v, qi, ki, wi):
    B, S, H, D = q.shape
    topk = min(TOPK_MAX, S // 4)
    nb = S // Q_BLOCK
    pos = jnp.arange(S, dtype=jnp.int32)
    blocks = lambda a: jnp.moveaxis(a.reshape((B, nb, Q_BLOCK) + a.shape[2:]), 1, 0)
    gather = jax.vmap(lambda rows, idx: rows[idx])

    def one_block(inp):
        qb, qib, wib, pb = inp
        sc = index_scores(qib, wib, ki)
        sc = jnp.where(pos[None, None, :] <= pb[None, :, None], sc, -jnp.inf)
        _, idx = lax.top_k(sc, topk)
        valid = idx <= pb[None, :, None]
        return sparse_attend(qb, gather(k, idx), gather(v, idx), valid)

    out = lax.map(one_block, (blocks(q), blocks(qi), blocks(wi), pos.reshape(nb, Q_BLOCK)))
    return jnp.moveaxis(out, 0, 1).reshape(B, S, H * D)

def dsa_sample(q, k_new, v_new, qi, ki_new, wi, cache_k, cache_v, cache_kidx, page_table):
    Bd, T, H, D = q.shape
    past = page_table.shape[1] * PAGE_SIZE
    L = past + T
    topk = min(TOPK_MAX, L // 4)
    ki_past = cache_kidx[page_table].reshape(Bd, past, -1)
    ki_all = jnp.concatenate([ki_past.astype(jnp.float32), ki_new], axis=1)
    pos_q = past + jnp.arange(T, dtype=jnp.int32)
    sc = index_scores(qi, wi, ki_all)
    sc = jnp.where(jnp.arange(L, dtype=jnp.int32)[None, None, :] <= pos_q[None, :, None], sc, -jnp.inf)
    _, idx = lax.top_k(sc, topk)
    valid = idx <= pos_q[None, :, None]
    in_past = (idx < past)[..., None, None]
    bidx = jnp.arange(Bd)[:, None, None]
    ip = jnp.minimum(idx, past - 1)
    phys = page_table[bidx, ip // PAGE_SIZE]
    off = ip % PAGE_SIZE
    inew = jnp.clip(idx - past, 0, T - 1)
    k_sel = jnp.where(in_past, cache_k[phys, off].astype(jnp.float32), k_new[bidx, inew])
    v_sel = jnp.where(in_past, cache_v[phys, off].astype(jnp.float32), v_new[bidx, inew])
    return sparse_attend(q, k_sel, v_sel, valid).reshape(Bd, T, H * D)

def block_output(x, h_m, h_a, w_out, ln1_g, ln1_b, w_gate, w_up, w_down, ln2_g, ln2_b):
    mix = jnp.concatenate([h_m, h_a], axis=-1).astype(x.dtype)
    x = layer_norm(ALPHA * x + mix @ w_out, ln1_g, ln1_b)
    ff = (jax.nn.silu(x @ w_gate) * (x @ w_up)) @ w_down
    return layer_norm(ALPHA * x + ff, ln2_g, ln2_b)

def setup_inputs(seed: int = 0) -> dict:
    key = jax.random.key(seed)
    ks = jax.random.split(key, 24)
    n_pages = PAST_LEN // PAGE_SIZE
    n_used = DEC_BATCH * n_pages
    n_pool = n_used + n_used // 4
    nrm = lambda k, shape, scale: jax.random.normal(k, shape, jnp.float32) * scale
    f_bias = jnp.linspace(3.0, 6.0, M_HEADS, dtype=jnp.float32)
    b_gate = jnp.concatenate([nrm(ks[10], (DEPTH, M_HEADS), 0.1),
                              f_bias[None, :] + nrm(ks[11], (DEPTH, M_HEADS), 0.1)], axis=-1)
    return {
        "x_prompt": nrm(ks[0], (BATCH, SEQ, D_MODEL), 1.0),
        "x_sample": nrm(ks[1], (DEC_BATCH, DEC_SEQ, D_MODEL), 1.0),
        "cache_k": nrm(ks[2], (DEPTH, n_pool, PAGE_SIZE, A_HEADS, A_HEAD_DIM), 1.0),
        "cache_v": nrm(ks[3], (DEPTH, n_pool, PAGE_SIZE, A_HEADS, A_HEAD_DIM), 1.0),
        "cache_kidx": nrm(ks[4], (DEPTH, n_pool, PAGE_SIZE, IDX_DIM), 1.0),
        "state_C": nrm(ks[5], (DEPTH, DEC_BATCH, M_HEADS, M_HEAD_DIM, M_HEAD_DIM), 0.1),
        "state_n": nrm(ks[6], (DEPTH, DEC_BATCH, M_HEADS, M_HEAD_DIM), 0.1),
        "state_m": nrm(ks[7], (DEPTH, DEC_BATCH, M_HEADS), 1.0),
        "page_table": jax.random.permutation(ks[8], n_pool)[:n_used].reshape(DEC_BATCH, n_pages).astype(jnp.int32),
        "w_in": nrm(ks[9], (DEPTH, D_MODEL, IN_DIM), D_MODEL ** -0.5),
        "b_gate": b_gate,
        "w_out": nrm(ks[12], (DEPTH, MIX_WIDTH, D_MODEL), MIX_WIDTH ** -0.5 * BETA),
        "ln1_g": 1.0 + nrm(ks[13], (DEPTH, D_MODEL), 0.05),
        "ln1_b": nrm(ks[14], (DEPTH, D_MODEL), 0.02),
        "w_gate": nrm(ks[15], (DEPTH, D_MODEL, D_FF), D_MODEL ** -0.5),
        "w_up": nrm(ks[16], (DEPTH, D_MODEL, D_FF), D_MODEL ** -0.5),
        "w_down": nrm(ks[17], (DEPTH, D_FF, D_MODEL), D_FF ** -0.5 * BETA),
        "ln2_g": 1.0 + nrm(ks[18], (DEPTH, D_MODEL), 0.05),
        "ln2_b": nrm(ks[19], (DEPTH, D_MODEL), 0.02),
    }

def reference(x_prompt, x_sample, cache_k, cache_v, cache_kidx, state_C, state_n, state_m, page_table,
              w_in, b_gate, w_out, ln1_g, ln1_b, w_gate, w_up, w_down, ln2_g, ln2_b):
    Bp, Sp, _ = x_prompt.shape
    Bs, Ts, _ = x_sample.shape
    past = page_table.shape[1] * PAGE_SIZE
    pos_p = jnp.arange(Sp, dtype=jnp.int32)
    pos_s = past + jnp.arange(Ts, dtype=jnp.int32)
    xp, xs = x_prompt, x_sample
    kp_l, vp_l, kip_l, Cp_l, np_l, mp_l = [], [], [], [], [], []
    ks_l, vs_l, kis_l, Cs_l, ns_l, ms_l = [], [], [], [], [], []
    for l in range(DEPTH):
        ffn = (ln1_g[l], ln1_b[l], w_gate[l], w_up[l], w_down[l], ln2_g[l], ln2_b[l])
        m_str, a_str = mixer_streams(xp, pos_p, w_in[l], b_gate[l])
        h_m, (Cp, n_p, m_p) = mlstm_mixer(m_str, jnp.zeros((Bp, M_HEADS, M_HEAD_DIM, M_HEAD_DIM), jnp.float32),
                                          jnp.zeros((Bp, M_HEADS, M_HEAD_DIM), jnp.float32),
                                          jnp.zeros((Bp, M_HEADS), jnp.float32))
        q, k, v, qi, ki, wi = a_str
        h_a = dsa_prompt(q, k, v, qi, ki, wi)
        xp = block_output(xp, h_m, h_a, w_out[l], *ffn)
        kp_l.append(k); vp_l.append(v); kip_l.append(ki); Cp_l.append(Cp); np_l.append(n_p); mp_l.append(m_p)
        m_str, a_str = mixer_streams(xs, pos_s, w_in[l], b_gate[l])
        h_m, (Cs, n_s, m_s) = mlstm_mixer(m_str, state_C[l], state_n[l], state_m[l])
        q, k, v, qi, ki, wi = a_str
        h_a = dsa_sample(q, k, v, qi, ki, wi, cache_k[l], cache_v[l], cache_kidx[l], page_table)
        xs = block_output(xs, h_m, h_a, w_out[l], *ffn)
        ks_l.append(k); vs_l.append(v); kis_l.append(ki); Cs_l.append(Cs); ns_l.append(n_s); ms_l.append(m_s)
    k_prompt = jnp.stack(kp_l); v_prompt = jnp.stack(vp_l); kidx_prompt = jnp.stack(kip_l)
    C_prompt = jnp.stack(Cp_l); n_prompt = jnp.stack(np_l); m_prompt = jnp.stack(mp_l)
    k_sample = jnp.stack(ks_l); v_sample = jnp.stack(vs_l); kidx_sample = jnp.stack(kis_l)
    C_sample = jnp.stack(Cs_l); n_sample = jnp.stack(ns_l); m_sample = jnp.stack(ms_l)
    return (xp, xs, k_prompt, v_prompt, kidx_prompt, C_prompt, n_prompt, m_prompt,
            k_sample, v_sample, kidx_sample, C_sample, n_sample, m_sample)


_drawn_inputs = setup_inputs


def setup_inputs(seed=0):
    import zlib

    import numpy as np

    out = dict(_drawn_inputs(seed))
    spreads = {}
    factors = {'ln1_b': 2.748, 'ln2_b': 2.846}
    for name, (base, spread) in spreads.items():
        noise = np.random.default_rng([zlib.crc32(name.encode()), seed]).standard_normal(out[name].shape)
        drawn = base * np.exp(spread * noise) if base else spread * noise
        out[name] = __import__('jax').numpy.asarray(drawn.astype(out[name].dtype))
    for name, factor in factors.items():
        out[name] = (out[name] * factor).astype(out[name].dtype)
    return out
```

```python
import concourse.bass as bass
from concourse import mybir
from contextlib import ExitStack

F32 = mybir.dt.float32
I32 = mybir.dt.int32
ALU = mybir.AluOpType
ACT = mybir.ActivationFunctionType

P = 128
D = 1024
KD = D // P
SEQ = 1024
NB, NT = 8, 4
SMP = NB * NT
T = SEQ + SMP
TILES = SEQ // P + 1
LAST = TILES - 1
CH = T // 3
MH = 4
AH, AD = 8, 64
AW = AH * AD
PAGES = 2
PAST = PAGES * P
SC_W = PAST + SMP
TOPK, TOPK_S = 256, (PAST + NT) // 4
FF = 2816
MF = FF // P
ALPHA = 2 ** 0.25
EPS = 1e-5
NEG = -1e30
TAKEN = -3e38
MQ, MK, MV, MO, MI, AQ, AK, AV, IQ, IK = 0, 512, 1024, 1536, 2048, 2056, 2568, 3080, 3592, 4104
IDX_D = 64
NSM = IDX_D + AH
RING = 6
STG = 4
FIRST_SPARSE = TOPK // P


def rows(i):
    return SMP if i == LAST else P


def build(nc, x_prompt, x_sample, cache_k, cache_v, cache_kidx, state_C, state_n, state_m, page_table,
          w_in, b_gate, w_out, ln1_g, ln1_b, w_gate, w_up, w_down, ln2_g, ln2_b,
          c_square, c_rope, c_small, c_rows,
          y_prompt, y_sample, k_prompt, v_prompt, kidx_prompt, C_prompt, n_prompt, m_prompt,
          k_sample, v_sample, kidx_sample, C_sample, n_sample, m_sample,
          mv_dram, iw_dram):
    ctx = ExitStack()
    with ctx:
        def sem(name):
            return ctx.enter_context(nc.semaphore(name))

        A = ctx.enter_context(nc.sbuf_tensor("arena", [P, 52600], F32))
        top = [0]

        def take(n):
            top[0] += n
            assert top[0] <= 52600, top[0]
            return A[:, top[0] - n:top[0]]

        sq = take(6 * P).rearrange("p (c n) -> p c n", n=P)
        ident, causal, causal_t, ones = (sq[:, c, :] for c in range(4))
        expand = sq[0:SMP, 4:6, :]
        rope = take(TILES * 32).rearrange("p (i c n) -> p i c n", c=2, n=16)
        small = take(64 + SMP * 2)
        wsel_mask = small[:, 0:64].rearrange("p (g n) -> p g n", g=2)
        new_mask, new_mask_t = small[0:SMP, 64:96], small[0:SMP, 96:128]
        crow = take(T + MH * P)
        not_first = crow[0:MH, 0:T]
        head_row = crow[0:MH, T:T + MH * P].rearrange("q (h n) -> q h n", h=MH)
        iw = take(TILES * AH).rearrange("p (i h) -> p i h", h=AH)
        wcol = take(2)
        wsel = take(2 * SMP).rearrange("p (g n) -> p g n", g=2)
        gate_b = take(2)
        ptab = ctx.enter_context(nc.sbuf_tensor("ptab", [1, NB * PAGES], I32))
        m8 = take(32)
        scd = take(SC_W)
        qbd = take(NB * 4 * SMP).rearrange("p (q b n) -> p q b n", q=4, b=NB)
        gates = take(2 * T).rearrange("p (w t) -> p w t", w=2)
        mixT = take(8 * T).rearrange("p (k t) -> p k t", t=T)
        qT = mixT[:, 4:8, :]
        after_mix = top[0]
        kT_flat = take(4 * T)
        kT = kT_flat.rearrange("p (k t) -> p k t", t=T)
        mkT_flat = take(4 * T)
        mkT = mkT_flat.rearrange("p (k t) -> p k t", t=T)
        iqT = take(4 * T).rearrange("p (k t) -> p k t", t=T)
        moT = iqT
        kiT = take(T)
        widths = [(i + 1) * P for i in range(TILES - 1)]
        score_flat = take(sum(widths[FIRST_SPARSE:]))
        score, at = {}, 0
        for i in range(FIRST_SPARSE, TILES - 1):
            score[i] = score_flat[:, at:at + widths[i]]
            at += widths[i]
        stage = take(STG * AW).rearrange("p (s n) -> p s n", s=STG)
        ropet = take(AH * 32)
        work0 = top[0]
        xT = take(KD * T).rearrange("p (k t) -> p k t", t=T)
        wslot = take(2 * KD * 512).rearrange("p (s k n) -> p s k n", s=2, k=KD)
        wsm = take(KD * 80).rearrange("p (k n) -> p k n", k=KD)
        end_phase1 = top[0]
        xin = score_flat[:, 0:3 * D].rearrange("p (s n) -> p s n", s=3)
        kix = mkT_flat[:, 0:2048].rearrange("p (j n) -> p j n", n=P)
        kixT = mkT_flat[:, 2048:4096].rearrange("p (j n) -> p j n", n=P)
        relu = kT_flat[:, 0:4 * 512].rearrange("p (s n) -> p s n", s=4)
        relud = relu[:, 0:2, 0:SC_W]
        top[0] = work0
        v_tm = take(TILES * AW).rearrange("p (i n) -> p i n", n=AW)
        mv_tm = take(TILES * 512).rearrange("p (i n) -> p i n", n=512)
        work1 = top[0]

        PS = [ctx.enter_context(nc.psum_tensor(f"bank{i}", [P, 512], F32)) for i in range(8)]

        square_in = sem("square_in")
        const_in = sem("const_in")
        x_in = [sem(f"x_in{s}") for s in range(3)]
        w_in_s = [sem(f"w_in{s}") for s in range(2)]
        wsm_in = sem("wsm_in")
        kix_in = sem("kix_in")
        wcol_in = sem("wcol_in")
        filled, freed = sem("filled"), sem("freed")
        roped, rope_step = sem("roped"), sem("rope_step")
        stored = [sem(f"stored{s}") for s in range(STG)]
        scored = sem("scored")
        causal_done = sem("causal_done")
        topk_step, topk_turn = sem("topk_step"), sem("topk_turn")
        zeroed = sem("zeroed")
        wsel_done = sem("wsel_done")
        masks_done = sem("masks_done")

        big = ["iq", "ak", "aq", "av", "mv", "mk", "mq", "mo"]
        col = dict(iq=IQ, ak=AK, aq=AQ, av=AV, mv=MV, mk=MK, mq=MQ, mo=MO)
        jobs = [("xT", i, j) for i in range(TILES) for j in range(2)]

        def tm_jobs(g, turned):
            out = []
            for i in range(TILES):
                out.append(("tm", g, i))
                if turned and i >= 2:
                    out.append(("tr", g, i - 2))
            return out + ([("tr", g, TILES - 2), ("tr", g, TILES - 1)] if turned else [])

        jobs += tm_jobs("iq", True) + tm_jobs("ik", True)
        for i in range(FIRST_SPARSE, TILES - 1):
            jobs += [("idx", i, h, c) for h in range(AH) for c in range(-(-widths[i] // 512))]
        jobs += [("kxT", q) for q in range(4)] + [("idxd", g) for g in range(2)] + [("scd",)]
        jobs += tm_jobs("ak", True) + tm_jobs("aq", True) + tm_jobs("av", False) + tm_jobs("mv", False)
        for g in ("mk", "mq"):
            jobs += [("fm", g, m, c) for m in range(4) for c in range(3)]
        jobs += [("gate", w, c) for w in range(2) for c in range(3)]
        jobs += [("fm", "mo", m, c) for m in range(4) for c in range(3)]
        pos = {job: n for n, job in enumerate(jobs)}
        staged = [j for j in jobs if j[0] == "tm"]
        stage_no = {j: s for s, j in enumerate(staged)}
        rope_jobs = [j for j in staged if j[1] in ("iq", "ik", "ak", "aq")]
        rope_no = {j: r for r, j in enumerate(rope_jobs)}
        store_jobs = [j for j in staged if j[1] in ("ik", "ak", "av", "mv")]
        store_no, seen = {}, [0] * STG
        for j in store_jobs:
            seen[stage_no[j] % STG] += 1
            store_no[j] = seen[stage_no[j] % STG]
        idx_jobs = [j for j in jobs if j[0] == "idx"]
        idx_no = {j: r for r, j in enumerate(idx_jobs)}
        turned_into = dict(iq=iqT, ik=kiT, ak=kT, aq=qT)

        def tile_cols(i):
            return slice(i * P, i * P + rows(i))

        n_sparse = LAST - FIRST_SPARSE
        top[0] = work1
        masked = take(2 * SEQ).rearrange("p (s n) -> p s n", s=2)
        probT = take(2 * SEQ).rearrange("p (s j n) -> p s j n", s=2, j=LAST)
        att_out = take(2 * AW).rearrange("p (s n) -> p s n", s=2)
        kraw = take(2 * PAGES * AW).rearrange("p (s j n) -> p s j n", s=2, j=PAGES)
        prob_s = take(SC_W)
        probT_s = take(3 * P).rearrange("p (j n) -> p j n", n=P)
        negmax = take(4)
        rowsum = take(2 * AH).rearrange("p (s h) -> p s h", s=2)
        rinv = take(2 * AH).rearrange("p (s h) -> p s h", s=2)
        vpage = score_flat[:, 0:4 * PAGES * AW].rearrange("p (b j n) -> p b j n", b=4, j=PAGES)
        kpT = masked.rearrange("p s n -> p (s n)")[:, 0:2 * 4 * PAST].rearrange("p (s q n) -> p s q n", s=2, q=4)
        top[0] += 0
        dense01 = stage.rearrange("p s n -> p (s n)")[:, 0:3 * P]

        steps2 = [(i, h) for i in range(LAST) for h in range(AH)]
        N2 = len(steps2)
        wide = [0] * (N2 + 1)
        for n, (i, h) in enumerate(steps2):
            wide[n + 1] = wide[n] + (widths[i] > 512)

        def mask_of(i):
            if i >= FIRST_SPARSE:
                return score[i]
            return dense01[:, 0:P] if i == 0 else dense01[:, P:3 * P]

        v_loaded = sem("v_loaded")
        dense_ready = sem("dense_ready")
        att_scores, att_masked, att_exp = sem("att_scores"), sem("att_masked"), sem("att_exp")
        att_turned, att_left, att_right = sem("att_turned"), sem("att_left"), sem("att_right")
        att_values, att_scaled, att_oT, att_put = sem("att_values"), sem("att_scaled"), sem("att_oT"), sem("att_put")
        neg_step = sem("neg_step")
        turned_before = [0] * (N2 + 1)
        for n, (i, h) in enumerate(steps2):
            turned_before[n + 1] = turned_before[n] + 1 + (widths[i] > 512)

        def pe_attention(pe):
            pe.wait_ge(freed, len(jobs))
            pe.wait_ge(v_loaded, 16 * TILES)

            def scores(n):
                i, h = steps2[n]
                lo = 64 * (h % 2)
                if n >= 2:
                    pe.wait_ge(att_masked, n - 1)
                for c in range(-(-widths[i] // 512)):
                    wd = min(512, widths[i] - 512 * c)
                    mm = pe.matmul(PS[2 * (n % 2) + c][:, 0:wd], qT[lo:lo + 64, h // 2, tile_cols(i)],
                                   kT[lo:lo + 64, h // 2, 512 * c:512 * c + wd], start=True, stop=True)
                mm.then_inc(att_scores, 1)

            def turn(n):
                i, h = steps2[n]
                pe.wait_ge(att_exp, n + 1)
                for c in range(-(-widths[i] // 512)):
                    if c == 0 and n >= 1:
                        pe.wait_ge(att_left, n)
                    if c == 1 and wide[n] >= 1:
                        pe.wait_ge(att_right, wide[n])
                    for j in range(4 * c, min(4 * c + 4, i + 1)):
                        mm = pe.transpose(PS[4 + c][:, (j % 4) * P:(j % 4 + 1) * P],
                                          masked[:, n % 2, j * P:(j + 1) * P], ident)
                    mm.then_inc(att_turned, 1)

            def values(n):
                i, h = steps2[n]
                pe.wait_ge(att_left, n + 1)
                if wide[n + 1] > wide[n]:
                    pe.wait_ge(att_right, wide[n + 1])
                if h == 0 and i:
                    pe.wait_ge(att_scaled, i)
                for j in range(i + 1):
                    mm = pe.matmul(PS[6][:, h * AD:(h + 1) * AD], probT[:, n % 2, j, :],
                                   v_tm[:, j, h * AD:(h + 1) * AD], start=(j == 0), stop=(j == i))
                mm.then_inc(att_values, 1)

            def out_turn(i):
                pe.wait_ge(att_scaled, i + 1)
                if i:
                    pe.wait_ge(att_put, i)
                for k in range(4):
                    mm = pe.transpose(PS[7][:, k * P:(k + 1) * P], att_out[:, i % 2, k * P:(k + 1) * P], ident)
                mm.then_inc(att_oT, 1)

            for n in range(N2 + 3):
                if n < N2:
                    scores(n)
                if 1 <= n <= N2:
                    turn(n - 1)
                if n >= 3 and steps2[n - 3][1] == AH - 1:
                    out_turn(steps2[n - 3][0])
                if 2 <= n < N2 + 2:
                    values(n - 2)

        def dve_attention(dve):
            dve.wait_ge(stored[0], 16 * seen[0])
            dve.memset(dense01[:, P:2 * P], 0.0).then_inc(dense_ready, 1)
            dve.tensor_copy(dense01[:, 0:P], causal).then_inc(dense_ready, 1)
            dve.tensor_copy(dense01[:, 2 * P:3 * P], causal).then_inc(dense_ready, 1)
            dve.wait_ge(dense_ready, 3)
            dve.wait_ge(masks_done, n_sparse + 1)
            for n in range(N2 + 3):
                if n < N2:
                    i, h = steps2[n]
                    dve.wait_ge(att_scores, n + 1)
                    if n >= 2:
                        dve.wait_ge(att_turned, turned_before[n - 1])
                        dve.wait_ge(att_exp, n - 1)
                    nc_ = -(-widths[i] // 512)
                    for c in range(nc_):
                        wd = min(512, widths[i] - 512 * c)
                        dve.tensor_tensor_reduce(masked[:, n % 2, 512 * c:512 * c + wd], PS[2 * (n % 2) + c][:, 0:wd],
                                                 mask_of(i)[:, 512 * c:512 * c + wd], 1.0, -3e38, ALU.add, ALU.max,
                                                 m8[:, c:c + 1]).then_inc(neg_step, 1)
                    base = sum(-(-widths[a] // 512) + 1 for a, _ in steps2[:n])
                    dve.wait_ge(neg_step, base + nc_)
                    if nc_ == 2:
                        dve.scalar_tensor_tensor(out=m8[:, 2:3], in0=m8[:, 0:1], scalar=1.0, in1=m8[:, 1:2],
                                                 op0=ALU.mult, op1=ALU.max).then_inc(neg_step, 1)
                    else:
                        dve.tensor_copy(m8[:, 2:3], m8[:, 0:1]).then_inc(neg_step, 1)
                    dve.wait_ge(neg_step, base + nc_ + 1)
                    dve.tensor_scalar(negmax[:, n % 2:n % 2 + 1], m8[:, 2:3], -(AD ** -0.5), None, ALU.mult)\
                        .then_inc(att_masked, 1)
                if 1 <= n <= N2 and wide[n] > wide[n - 1]:
                    i, h = steps2[n - 1]
                    dve.wait_ge(att_turned, turned_before[n])
                    if n >= 3:
                        dve.wait_ge(att_values, n - 2)
                    dve.tensor_copy(probT[:, (n - 1) % 2, 4:i + 1, :],
                                    PS[5][:, 0:(i - 3) * P].rearrange("p (j n) -> p j n", n=P)).then_inc(att_right, 1)
                if n >= 2 and n < N2 + 2 and steps2[n - 2][1] == AH - 1:
                    i = steps2[n - 2][0]
                    dve.wait_ge(att_values, n - 1)
                    dve.reciprocal(rinv[:, i % 2, :], rowsum[:, i % 2, :]).then_inc(dense_ready, 1)
                    dve.wait_ge(dense_ready, 4 + i)
                    if i >= 2:
                        dve.wait_ge(att_oT, i - 1)
                    dve.tensor_tensor(att_out[:, i % 2, :].rearrange("p (h n) -> p h n", h=AH),
                                      PS[6][:, :].rearrange("p (h n) -> p h n", h=AH),
                                      rinv[:, i % 2, :].unsqueeze(2).to_broadcast([P, AH, AD]), ALU.mult)\
                        .then_inc(att_scaled, 1)

        def act_attention(act):
            for n in range(N2 + 3):
                if n < N2:
                    i, h = steps2[n]
                    act.wait_ge(att_masked, n + 1)
                    if h == 0 and i >= 2:
                        act.wait_ge(att_scaled, i - 1)
                    act.activation(masked[:, n % 2, 0:widths[i]], masked[:, n % 2, 0:widths[i]], ACT.Exp,
                                   bias=negmax[:, n % 2:n % 2 + 1], scale=float(AD ** -0.5),
                                   accum_out=rowsum[:, i % 2, h:h + 1]).then_inc(att_exp, 1)
                if 1 <= n <= N2:
                    i, h = steps2[n - 1]
                    k = min(4, i + 1)
                    act.wait_ge(att_turned, turned_before[n - 1] + 1)
                    if n >= 3:
                        act.wait_ge(att_values, n - 2)
                    act.activation(probT[:, (n - 1) % 2, 0:k, :],
                                   PS[4][:, 0:k * P].rearrange("p (j n) -> p j n", n=P), ACT.Copy).then_inc(att_left, 1)
                if n >= 3 and steps2[n - 3][1] == AH - 1:
                    i = steps2[n - 3][0]
                    act.wait_ge(att_oT, i + 1)
                    act.activation(qT[:, :, tile_cols(i)], PS[7][:, :].rearrange("p (k n) -> p k n", k=4), ACT.Copy)\
                        .then_inc(att_put, 1)

        def sp_attention(sp):
            sp.wait_ge(filled, len(jobs))
            for i in range(TILES):
                r = rows(i)
                src = v_prompt[0, 0, i * P:(i + 1) * P].rearrange("t h n -> t (h n)") if i < LAST else \
                    v_sample[0].rearrange("b t h n -> (b t) (h n)")
                sp.dma_start(v_tm[0:r, i, :], src).then_inc(v_loaded, 16)
            for i in range(TILES):
                sp.dma_start(mv_tm[0:rows(i), i, :], mv_dram[i * P:i * P + rows(i), :]).then_inc(mv_loaded, 16)

        kpage_in = [sem(f"kpage_in{s}") for s in range(2)]
        vpage_in = sem("vpage_in")
        mv_loaded = sem("mv_loaded")
        smp_kT, smp_kput = sem("smp_kT"), sem("smp_kput")
        smp_mask, smp_scores, smp_exp, smp_norm = sem("smp_mask"), sem("smp_scores"), sem("smp_exp"), sem("smp_norm")
        smp_turned, smp_put, smp_values, smp_out = sem("smp_turned"), sem("smp_put"), sem("smp_values"), sem("smp_out")
        smp_step = sem("smp_step")

        def sp_samples(sp):
            for g in range(2):
                for b4 in range(4):
                    b = 4 * g + b4
                    if b >= 2:
                        sp.wait_ge(smp_kT, 2 * (b - 1))
                    for j in range(PAGES):
                        page = sp.value_load(ptab[0:1, b * PAGES + j:b * PAGES + j + 1], min_val=0,
                                             max_val=cache_k.shape[1] - 1)
                        sp.dma_start(kraw[:, b % 2, j, :],
                                     cache_k[0, bass.ds(page, 1)].rearrange("a p h n -> (a p) (h n)"))\
                            .then_inc(kpage_in[b % 2], 16)
                        if b == 0 and j == 0:
                            sp.wait_ge(att_masked, N2)
                        if b4 == 0 and j == 0 and g:
                            sp.wait_ge(smp_values, 4 * g)
                        sp.dma_start(vpage[:, b4, j, :],
                                     cache_v[0, bass.ds(page, 1)].rearrange("a p h n -> (a p) (h n)"))\
                            .then_inc(vpage_in, 16)

        def pe_samples(pe):
            pe.wait_ge(att_put, LAST)
            pe.wait_ge(att_left, N2)
            pe.wait_ge(att_right, wide[N2])
            for g in range(2):
                S = PS[4 + g]
                pe.wait_ge(masks_done, n_sparse + 1)
                pe.matmul(S[:, 0:SC_W], expand[:, g, :], scd[0:SMP, :], start=True, stop=False, skip_group_check=True)
                for b4 in range(4):
                    b = 4 * g + b4
                    pe.wait_ge(kpage_in[b % 2], 16 * PAGES * (b // 2 + 1))
                    for j in range(PAGES):
                        n = PAGES * b + j
                        if n >= 2:
                            pe.wait_ge(smp_kput, n - 1)
                        for q in range(4):
                            mm = pe.transpose(PS[n % 2][:, q * P:(q + 1) * P], kraw[:, b % 2, j, q * P:(q + 1) * P], ident)
                        mm.then_inc(smp_kT, 1)
                    pe.wait_ge(smp_kput, PAGES * (b + 1))
                    o = S[32 * b4:32 * b4 + 32]
                    for q in range(4):
                        pe.matmul(o[:, 0:PAST], qbd[:, q, b, :], kpT[:, b % 2, q, :], start=False, stop=False,
                                  skip_group_check=True, tile_position=(0, 32 * b4))
                    for q in range(4):
                        mm = pe.matmul(o[:, PAST:SC_W], qbd[:, q, b, :], kT[:, q, SEQ:T], start=False, stop=(q == 3),
                                       skip_group_check=True, tile_position=(0, 32 * b4))
                    mm.then_inc(smp_scores, 1)
                pe.wait_ge(smp_norm, g + 1)
                if g:
                    pe.wait_ge(smp_put, g)
                for j in range(PAGES):
                    pe.transpose(PS[2][:, j * P:(j + 1) * P], prob_s[:, j * P:(j + 1) * P], ident)
                pe.transpose(PS[2][0:SMP, PAGES * P:3 * P], prob_s[:, PAST:SC_W], ident).then_inc(smp_turned, 1)
                pe.wait_ge(smp_put, g + 1)
                pe.wait_ge(vpage_in, 16 * PAGES * 4 * (g + 1))
                for b4 in range(4):
                    for q in range(4):
                        o = PS[6 + g][:, (4 * b4 + q) * SMP:(4 * b4 + q + 1) * SMP]
                        cols, hp = slice(32 * b4, 32 * b4 + 32), slice(q * P, (q + 1) * P)
                        for j in range(PAGES):
                            pe.matmul(o, vpage[:, b4, j, hp], probT_s[:, j, cols], start=(j == 0), stop=False)
                        mm = pe.matmul(o, v_tm[0:SMP, LAST, hp], probT_s[0:SMP, 2, cols], start=False, stop=True)
                    mm.then_inc(smp_values, 1)

        def act_samples(act):
            act.wait_ge(att_turned, turned_before[N2])
            for g in range(2):
                for b4 in range(4):
                    b = 4 * g + b4
                    for j in range(PAGES):
                        act.wait_ge(smp_kT, PAGES * b + j + 1)
                        if b >= 2:
                            act.wait_ge(smp_scores, b - 1)
                        act.activation(kpT[:, b % 2, :, j * P:(j + 1) * P],
                                       PS[(PAGES * b + j) % 2][:, :].rearrange("p (q n) -> p q n", q=4), ACT.Copy)\
                            .then_inc(smp_kput, 1)
                act.wait_ge(smp_mask, g + 1)
                act.activation(prob_s, PS[4 + g][:, 0:SC_W], ACT.Exp, bias=negmax[:, 2:3], scale=float(AD ** -0.5),
                               accum_out=negmax[:, 3:4]).then_inc(smp_exp, 1)
                act.wait_ge(smp_turned, g + 1)
                if g:
                    act.wait_ge(smp_values, 4 * g)
                act.activation(probT_s[:, 0:2, :], PS[2][:, 0:2 * P].rearrange("p (j n) -> p j n", j=2), ACT.Copy)
                act.activation(probT_s[0:SMP, 2, :], PS[2][0:SMP, 2 * P:3 * P], ACT.Copy).then_inc(smp_put, 1)

        def dve_samples(dve):
            for g in range(2):
                dve.wait_ge(smp_scores, 4 * (g + 1))
                if g:
                    dve.wait_ge(smp_exp, g)
                dve.tensor_reduce(m8[:, 0:1], PS[4 + g][:, 0:SC_W], mybir.AxisListType.X, ALU.max).then_inc(smp_step, 1)
                dve.wait_ge(smp_step, 3 * g + 1)
                dve.tensor_scalar(negmax[:, 2:3], m8[:, 0:1], -(AD ** -0.5), None, ALU.mult).then_inc(smp_mask, 1)
                dve.wait_ge(smp_exp, g + 1)
                dve.reciprocal(m8[:, 1:2], negmax[:, 3:4]).then_inc(smp_step, 1)
                dve.wait_ge(smp_step, 3 * g + 2)
                dve.tensor_scalar(prob_s, prob_s, m8[:, 1:2], None, ALU.mult).then_inc(smp_norm, 1)
                dve.wait_ge(smp_values, 4 * (g + 1))
                for h in range(AH):
                    lo = 64 * (h % 2)
                    src = PS[6 + g][lo:lo + 64, :].rearrange("p (b q n) -> p b q n", b=4, q=4)
                    c = dve.tensor_copy(qT[lo:lo + 64, h // 2, SEQ + 16 * g:SEQ + 16 * g + 16]
                                        .rearrange("p (b t) -> p b t", b=4), src[:, :, h // 2, NT * h:NT * h + NT])
                c.then_inc(smp_step, 1)
            dve.wait_ge(smp_step, 6)

        CK = TILES
        top[0] = work1
        qg = take(T)
        st = take(2 * P).rearrange("p (s n) -> p s n", s=2)
        kw = take(2 * P).rearrange("p (s n) -> p s n", s=2)
        hden = take(P)
        hinv = take(P)
        state = take(2 * 2 * P).rearrange("p (s n) -> p s n", s=2)
        c_smp = take(2 * NB * P).rearrange("p (s b n) -> p s b n", s=2, b=NB)
        kw_smp = take(NB * P).rearrange("p (b n) -> p b n", b=NB)
        acol = take(CK * MH).rearrange("p (c h) -> p c h", h=MH)
        qn = take(SMP)
        n_all = take(NB * MH + MH)
        m_prev = take(LAST + NB)
        n_rows = take(P)
        n_out = take(P)
        one_col = take(1)
        lf, ig = gates[0:MH, 1, :], gates[0:MH, 0, :]
        b_row, m_row, a_row, g_row = (score_flat[0:MH, r * T:(r + 1) * T] for r in range(4))
        e_row = kiT[0:MH, :]
        bb, gb, eb, wt = (kT[:, r, :] for r in range(4))

        m_in, nst_in = sem("m_in"), sem("nst_in")
        c_in = [sem(f"c_in{s}") for s in range(2)]
        row_step, row_act = sem("row_step"), sem("row_act")
        a_turned, a_put = sem("a_turned"), sem("a_put")
        n_turned, n_put = sem("n_turned"), sem("n_put")
        bc_filled, bc_freed = sem("bc_filled"), sem("bc_freed")
        wt_arg, wt_exp, qg_done, qn_done = sem("wt_arg"), sem("wt_exp"), sem("qg_done"), sem("qn_done")
        st_ps, st_done, kw_done = sem("st_ps"), sem("st_done"), sem("kw_done")
        nd_ps, cs_ps, cs_done, h_done = sem("nd_ps"), sem("cs_ps"), sem("cs_done"), sem("h_done")
        h_step, gated = sem("h_step"), sem("gated")
        c_stored = [sem(f"c_stored{s}") for s in range(2)]
        cp_stored = sem("cp_stored")
        m_stored = sem("m_stored")
        n_final, n_back, n_out_put, n_stored = sem("n_final"), sem("n_back"), sem("n_out_put"), sem("n_stored")

        def sp_mlstm(sp):
            sp.wait_ge(mp_zero, 1)
            sp.dma_start(m_prev[0:MH, LAST:LAST + NB], state_m[0].rearrange("b h -> h b"),
                         allow_slow_non_contiguous=True).then_inc(m_in, 16)
            sp.dma_start(n_rows[0:NB * MH, :], state_n[0].rearrange("b h d -> (b h) d")).then_inc(nst_in, 16)

            def load_c(h):
                sp.dma_start(c_smp[:, h % 2, :, :], state_C[0, :, h].rearrange("b d e -> d b e"))\
                    .then_inc(c_in[h % 2], 16)

            load_c(0)
            load_c(1)
            sp.wait_ge(row_step, 3 + NB)
            sp.dma_start(m_prompt[0, 0, :].rearrange("(h n) -> h n", n=1), m_row[:, SEQ - 1:SEQ]).then_inc(m_stored, 16)
            sp.dma_start(m_sample[0].rearrange("b h -> h b"),
                         m_row[:, SEQ:T].rearrange("h (b t) -> h b t", b=NB)[:, :, NT - 1],
                         allow_slow_non_contiguous=True).then_inc(m_stored, 16)
            for h in range(MH):
                sp.wait_ge(cs_done, CK * h + LAST)
                sp.dma_start(C_prompt[0, 0, h], state[:, 0, 0:P]).then_inc(cp_stored, 16)
                sp.wait_ge(cs_done, CK * h + CK)
                sp.dma_start(C_sample[0, :, h].rearrange("b d e -> d b e"), c_smp[:, h % 2, :, :])\
                    .then_inc(c_stored[h % 2], 16)
                if h + 2 < MH:
                    sp.wait_ge(c_stored[h % 2], 16)
                    load_c(h + 2)
            sp.wait_ge(n_out_put, 1)
            sp.dma_start(n_sample[0].rearrange("b h d -> (b h) d"), n_out[0:NB * MH, :]).then_inc(n_stored, 16)
            sp.dma_start(n_prompt[0, 0], n_out[NB * MH:NB * MH + MH, :]).then_inc(n_stored, 16)
            sp.wait_ge(n_stored, 32)
            sp.wait_ge(m_stored, 32)
            sp.wait_ge(cp_stored, 16 * MH)
            for s in range(2):
                sp.wait_ge(c_stored[s], 32)

        def dve_rows(dve):
            dve.wait_ge(smp_values, 8)
            dve.wait_ge(smp_scores, 8)
            dve.memset(m_prev[0:MH, 0:1], 0.0)
            dve.memset(one_col, 1.0).then_inc(mp_zero, 1)
            dve.scalar_tensor_tensor(out=a_row, in0=lf, scalar=-1.0, in1=lf, op0=ALU.mult, op1=ALU.max)\
                .then_inc(row_step, 1)
            dve.wait_ge(row_act, 1)
            dve.scalar_tensor_tensor(out=lf, in0=lf, scalar=0.0, in1=g_row, op0=ALU.min, op1=ALU.subtract)\
                .then_inc(row_step, 1)
            dve.wait_ge(row_step, 2)
            dve.tensor_tensor_scan(b_row, not_first, lf, 0.0, ALU.mult, ALU.add)
            dve.tensor_tensor_scan(m_row[:, 0:SEQ], lf[:, 0:SEQ], ig[:, 0:SEQ], 0.0, ALU.add, ALU.max)\
                .then_inc(row_step, 1)
            dve.wait_ge(m_in, 16)
            for b in range(NB):
                c = slice(SEQ + NT * b, SEQ + NT * b + NT)
                dve.tensor_tensor_scan(m_row[:, c], lf[:, c], ig[:, c], m_prev[0:MH, LAST + b:LAST + b + 1],
                                       ALU.add, ALU.max).then_inc(row_step, 1)
            step = 3 + NB
            dve.wait_ge(row_step, step)
            dve.tensor_copy(m_prev[0:MH, 1:LAST],
                            m_row[:, 0:SEQ].rearrange("h (c t) -> h c t", t=P)[:, 0:LAST - 1, P - 1])
            dve.tensor_tensor(a_row, ig, b_row, ALU.subtract).then_inc(row_step, 1)
            dve.wait_ge(row_step, step + 1)
            dve.tensor_tensor(b_row, b_row, m_row, ALU.subtract).then_inc(row_step, 1)
            dve.wait_ge(row_step, step + 2)
            dve.tensor_tensor(g_row[:, 0:SEQ].rearrange("h (c t) -> h c t", t=P),
                              b_row[:, 0:SEQ].rearrange("h (c t) -> h c t", t=P),
                              m_prev[0:MH, 0:LAST].unsqueeze(2).to_broadcast([MH, LAST, P]), ALU.add)
            dve.tensor_tensor(g_row[:, SEQ:T].rearrange("h (c t) -> h c t", t=NT),
                              b_row[:, SEQ:T].rearrange("h (c t) -> h c t", t=NT),
                              m_prev[0:MH, LAST:LAST + NB].unsqueeze(2).to_broadcast([MH, NB, NT]), ALU.add)\
                .then_inc(row_step, 1)

        ROWS_DONE = 3 + NB + 3

        def act_rows(act):
            act.wait_ge(row_step, 1)
            act.activation(e_row, a_row, ACT.Exp, scale=-1.0).then_inc(e_tmp, 1)
            act.wait_ge(e_tmp, 1)
            act.activation(g_row, e_row, ACT.Ln, bias=one_col[0:MH, :]).then_inc(row_act, 1)
            act.wait_ge(row_step, ROWS_DONE)
            act.activation(g_row, g_row, ACT.Exp)
            act.activation(e_row, m_row, ACT.Exp, scale=-1.0).then_inc(row_act, 1)
            act.wait_ge(a_turned, 1)
            act.activation(acol[:, 0:LAST, :], PS[3][:, 0:LAST * MH].rearrange("p (c h) -> p c h", h=MH), ACT.Copy)
            act.activation(acol[0:SMP, LAST, :], PS[3][0:SMP, LAST * MH:CK * MH], ACT.Copy)
            act.activation(n_all[:, 0:NB * MH], PS[3][:, 64:64 + NB * MH], ACT.Copy).then_inc(a_put, 1)

        def pe_rows(pe):
            pe.wait_ge(row_step, ROWS_DONE)
            pe.wait_ge(nst_in, 16)
            for c in range(CK):
                pe.transpose(PS[3][0:rows(c), c * MH:(c + 1) * MH], a_row[:, tile_cols(c)], ident[0:MH, 0:MH])
            pe.transpose(PS[3][:, 64:64 + NB * MH], n_rows[0:NB * MH, :], ident[0:NB * MH, 0:NB * MH])\
                .then_inc(a_turned, 1)
            pe.wait_ge(a_put, 1)
            pe.wait_ge(row_act, 2)

        def pe_mlstm(pe):
            def scores(q):
                h, c = divmod(q, CK)
                r = rows(c)
                if q:
                    pe.wait_ge(st_done, q)
                    pe.wait_ge(kw_done, q)
                pe.matmul(PS[3][0:r, 0:r], mkT[:, h, tile_cols(c)], mixT[:, h, tile_cols(c)], start=True, stop=True)
                pe.transpose(PS[4][0:r, 0:P], mkT[:, h, tile_cols(c)], ident).then_inc(st_ps, 1)

            def outputs(q):
                h, c = divmod(q, CK)
                r = rows(c)
                hs = slice(h * P, (h + 1) * P)
                ND = PS[5 + q % 2]
                w = st[0:r, q % 2, 0:r]
                pe.wait_ge(st_done, q + 1)
                pe.wait_ge(kw_done, q + 1)
                pe.wait_ge(qg_done, h + 1)
                if q >= 2:
                    pe.wait_ge(h_done, q - 1)
                if q:
                    pe.wait_ge(cs_done, q)
                qc = qg[:, tile_cols(c)]
                if c < LAST:
                    pe.matmul(ND[:, 0:P], mv_tm[:, c, hs], w, start=True, stop=(c == 0))
                    if c:
                        pe.matmul(ND[:, 0:P], state[:, c % 2, 0:P], qc, start=False, stop=True)
                    mm = pe.matmul(ND[:, P:2 * P], ones, w, start=True, stop=(c == 0))
                    if c:
                        mm = pe.matmul(ND[:, P:2 * P], state[:, c % 2, P:2 * P], qc, start=False, stop=True)
                    mm.then_inc(nd_ps, 1)
                    pe.matmul(PS[7][:, 0:P], kw[:, q % 2, :], mv_tm[:, c, hs], start=True, stop=True)
                    pe.matmul(PS[7][:, P:2 * P], kw[:, q % 2, :], ones, start=True, stop=True).then_inc(cs_ps, 1)
                else:
                    pe.wait_ge(c_in[h % 2], 16 * (h // 2 + 1))
                    pe.wait_ge(qn_done, h + 1)
                    pe.matmul(ND[:, 0:SMP], mv_tm[0:SMP, c, hs], w, start=True, stop=False, skip_group_check=True)
                    for b in range(NB):
                        pe.matmul(ND[:, NT * b:NT * b + NT], c_smp[:, h % 2, b, :], qc[:, NT * b:NT * b + NT],
                                  start=False, stop=True, skip_group_check=True)
                    pe.matmul(ND[:, P:P + SMP], ones[0:SMP, :], w, start=True, stop=False)
                    pe.matmul(ND[:, P:P + SMP], ones, qn, start=False, stop=True)
                    for b in range(NB):
                        mm = pe.matmul(ND[:, 2 * P + b:2 * P + b + 1], kw_smp[0:SMP, b, :], ones[0:SMP, 0:1],
                                       start=True, stop=True)
                    mm.then_inc(nd_ps, 1)
                    for b in range(NB):
                        mm = pe.matmul(PS[7 if b < 4 else 2][:, (b % 4) * P:(b % 4 + 1) * P], kw_smp[0:SMP, b, :],
                                       mv_tm[0:SMP, c, hs], start=True, stop=True)
                    mm.then_inc(cs_ps, 1)

            pe.wait_ge(mv_loaded, 16 * TILES)
            for h in range(MH):
                for n in range(9):
                    N = 9 * h + n
                    if N >= 2:
                        pe.wait_ge(bc_freed, N - 1)
                    row = (b_row, g_row, e_row)[n // 3]
                    c = n % 3
                    pe.matmul(PS[N % 2][:, 0:CH], head_row[:, h, :], row[:, c * CH:(c + 1) * CH], start=True, stop=True)\
                        .then_inc(bc_filled, 1)
                scores(CK * h)
                for c in range(CK):
                    if c + 1 < CK:
                        scores(CK * h + c + 1)
                    outputs(CK * h + c)
            pe.wait_ge(n_final, 2 * MH)
            pe.transpose(PS[0][0:NB * MH + MH, 0:P], n_all, ident).then_inc(n_back, 1)

        def act_mlstm(act):
            for h in range(MH):
                if h:
                    act.wait_ge(h_done, CK * h)
                    act.wait_ge(cs_done, CK * h)
                    act.wait_ge(qg_done, h)
                for n in range(9):
                    act.wait_ge(bc_filled, 9 * h + n + 1)
                    c = n % 3
                    act.activation((bb, gb, eb)[n // 3][:, c * CH:(c + 1) * CH], PS[(9 * h + n) % 2][:, 0:CH], ACT.Copy)\
                        .then_inc(bc_freed, 1)
                act.wait_ge(wt_arg, h + 1)
                for c in range(CK):
                    r = rows(c)
                    e = act.activation(wt[0:r, tile_cols(c)], wt[0:r, tile_cols(c)], ACT.Exp, bias=acol[0:r, c, h:h + 1])
                e.then_inc(wt_exp, 1)
                act.wait_ge(wt_exp, h + 1)
                for c in range(CK):
                    q = CK * h + c
                    r = rows(c)
                    act.wait_ge(st_ps, q + 1)
                    if c < LAST:
                        if q >= 2:
                            act.wait_ge(cs_ps, q - 1)
                        act.activation(kw[:, q % 2, :], PS[4][:, 0:P], ACT.Copy, scale=wt[:, (c + 1) * P - 1:(c + 1) * P])\
                            .then_inc(kw_done, 1)
                    else:
                        if h:
                            act.wait_ge(cs_ps, q)
                        for b in range(NB):
                            t = SEQ + NT * b + NT - 1
                            e = act.activation(kw_smp[0:SMP, b, :], PS[4][0:SMP, 0:P], ACT.Copy, scale=wt[0:SMP, t:t + 1])
                        e.then_inc(kw_done, 1)
            act.wait_ge(n_back, 1)
            act.activation(n_out[0:NB * MH + MH, :], PS[0][0:NB * MH + MH, 0:P], ACT.Copy).then_inc(n_out_put, 1)

        def pool_mlstm(pool):
            for h in range(MH):
                pool.wait_ge(bc_freed, 9 * h + 6)
                if h:
                    pool.wait_ge(nd_ps, CK * h)
                    pool.wait_ge(gated, h)
                pool.tensor_tensor(qg, mixT[:, h, :], gb, ALU.mult).then_inc(qg_done, 1)
                pool.wait_ge(qg_done, h + 1)
                if h == 0:
                    pool.wait_ge(a_put, 1)
                pool.tensor_tensor(qn.rearrange("p (b t) -> p b t", b=NB),
                                   qg[:, SEQ:T].rearrange("p (b t) -> p b t", b=NB),
                                   n_all[:, h:NB * MH:MH].unsqueeze(2).to_broadcast([P, NB, NT]), ALU.mult)\
                    .then_inc(qn_done, 1)
                pool.wait_ge(h_done, CK * (h + 1))
                pool.tensor_tensor(mixT[:, h, :], mixT[:, h, :], moT[:, h, :], ALU.mult).then_inc(gated, 1)

        def dve_mlstm(dve):
            steps = 0
            for h in range(MH):
                dve.wait_ge(bc_freed, 9 * h + 3)
                if h:
                    dve.wait_ge(kw_done, CK * h)
                dve.tensor_tensor(wt[:, 0:SEQ].rearrange("p (c t) -> p c t", t=P),
                                  bb[:, 0:SEQ].rearrange("p (c t) -> p c t", t=P),
                                  causal_t.unsqueeze(1).to_broadcast([P, LAST, P]), ALU.add)
                dve.tensor_tensor(wt[0:SMP, SEQ:T], bb[0:SMP, SEQ:T], new_mask_t, ALU.add).then_inc(wt_arg, 1)
                dve.wait_ge(bc_freed, 9 * h + 9)
                for c in range(CK):
                    q = CK * h + c
                    r = rows(c)
                    cols = tile_cols(c)
                    dve.wait_ge(st_ps, q + 1)
                    dve.wait_ge(wt_exp, h + 1)
                    if q >= 2:
                        dve.wait_ge(nd_ps, q - 1)
                    dve.tensor_tensor(st[0:r, q % 2, 0:r], PS[3][0:r, 0:r], wt[0:r, cols], ALU.mult)\
                        .then_inc(st_done, 1)
                    dve.wait_ge(nd_ps, q + 1)
                    ND = PS[5 + q % 2]
                    if steps:
                        dve.wait_ge(h_done, q)
                    dve.scalar_tensor_tensor(out=hden[:, 0:r], in0=ND[:, P:P + r], scalar=-1.0, in1=eb[:, cols],
                                             op0=ALU.mult, op1=ALU.max).then_inc(h_step, 1)
                    dve.wait_ge(h_step, 3 * steps + 1)
                    dve.tensor_tensor(hden[:, 0:r], ND[:, P:P + r], hden[:, 0:r], ALU.max).then_inc(h_step, 1)
                    dve.wait_ge(h_step, 3 * steps + 2)
                    dve.reciprocal(hinv[:, 0:r], hden[:, 0:r]).then_inc(h_step, 1)
                    dve.wait_ge(h_step, 3 * steps + 3)
                    steps += 1
                    if c == LAST:
                        n_h = n_all[:, h:NB * MH:MH]
                        g_last = gb[:, SEQ:T].rearrange("p (b t) -> p b t", b=NB)[:, :, NT - 1]
                        dve.wait_ge(qn_done, h + 1)
                        dve.tensor_tensor(n_h, n_h, g_last, ALU.mult).then_inc(n_final, 1)
                        dve.wait_ge(n_final, 2 * h + 1)
                        dve.tensor_tensor(n_h, n_h, ND[:, 2 * P:2 * P + NB], ALU.add).then_inc(n_final, 1)
                    dve.tensor_tensor(mixT[:, h, cols], ND[:, 0:r], hinv[:, 0:r], ALU.mult).then_inc(h_done, 1)
                    dve.wait_ge(cs_ps, q + 1)
                    if c == 0:
                        dve.tensor_copy(state[:, 1, :], PS[7][:, 0:2 * P]).then_inc(cs_done, 1)
                    elif c < LAST:
                        dve.wait_ge(cs_done, q)
                        if c == 1 and h:
                            dve.wait_ge(cp_stored, 16 * h)
                        u = dve.scalar_tensor_tensor(out=state[:, (c + 1) % 2, :], in0=state[:, c % 2, :],
                                                     scalar=gb[:, (c + 1) * P - 1:(c + 1) * P], in1=PS[7][:, 0:2 * P],
                                                     op0=ALU.mult, op1=ALU.add)
                        u.then_inc(cs_done, 1)
                        if c == LAST - 1:
                            dve.wait_ge(cs_done, q + 1)
                            dve.tensor_copy(n_all[:, NB * MH + h:NB * MH + h + 1], state[:, 0, P:P + 1])
                    else:
                        for b in range(NB):
                            t = SEQ + NT * b + NT - 1
                            u = dve.scalar_tensor_tensor(
                                out=c_smp[:, h % 2, b, :], in0=c_smp[:, h % 2, b, :], scalar=gb[:, t:t + 1],
                                in1=PS[7 if b < 4 else 2][:, (b % 4) * P:(b % 4 + 1) * P], op0=ALU.mult, op1=ALU.add)
                        u.then_inc(cs_done, 1)
        e_tmp, mp_zero = sem("e_tmp"), sem("mp_zero")

        top[0] = after_mix
        x_tm = take(TILES * D).rearrange("p (i n) -> p i n", n=D)
        hT_flat = take(MF * T)
        hT = hT_flat.rearrange("p (m t) -> p m t", t=T)
        wgu_flat = take(2 * 2 * KD * P)
        wgu = wgu_flat.rearrange("p (s w k n) -> p s w k n", s=2, w=2, k=KD)
        silu = take(2 * CH).rearrange("p (s n) -> p s n", s=2)
        stats = take(TILES * 12).rearrange("p (i n) -> p i n", n=12)
        moments = take(TILES * 2).rearrange("p (i n) -> p i n", n=2)
        rstd = take(TILES)
        end5 = top[0]
        assert end5 <= 52600
        x1T = mixT
        hf, mf, gf = hT_flat, mixT.rearrange("p k t -> p (k t)"), wgu_flat
        proj = {
            "out": dict(k=KD, w=hf[:, 0:2 * KD * P].rearrange("p (s k n) -> p s k n", s=2, k=KD),
                        y=hf[:, 4096:4096 + 2 * T].rearrange("p (s t) -> p s t", s=2), rhs=mixT, dram=w_out[0],
                        g=hf[:, 8192:8192 + D], b=hf[:, 8192 + D:8192 + 2 * D], dg=ln1_g, db=ln1_b),
            "down": dict(k=MF, w=mf[:, 0:2 * MF * P].rearrange("p (s k n) -> p s k n", s=2, k=MF),
                         y=mf[:, 2 * MF * P:2 * MF * P + 2 * T].rearrange("p (s t) -> p s t", s=2), rhs=hT,
                         dram=w_down[0], g=gf[:, 0:D], b=gf[:, D:2 * D], dg=ln2_g, db=ln2_b),
        }
        for name, pr in proj.items():
            for s in ("w0", "w1", "y_ps", "y_put", "turned", "added", "gb_in", "stat", "var_in", "std", "centred",
                      "normed", "nT", "nput"):
                pr[s] = sem(f"{name}_{s}")
        x_back = sem("x_back")
        gu_in = [sem("gu_in0"), sem("gu_in1")]
        gu_ps, silu_done, h_made = sem("gu_ps"), sem("silu_done"), sem("h_made")
        y_stored = sem("y_stored")
        MD = D // P

        def sp_proj(sp, pr):
            src = pr["dram"].rearrange("(k p) n -> p k n", p=P)
            with sp.Fori(0, MD // 2) as j:
                for u in range(2):
                    sp.wait_ge(pr["y_ps"], j * 6 + (3 * u + 3))
                    sp.dma_start(pr["w"][:, u], src[:, :, bass.ds(j * (2 * P) + u * P, P)]).then_inc(pr[f"w{u}"], 16)

        def pe_proj(pe, pr):
            pe.sem_inc(pr["y_ps"], 6)
            pe.sem_inc(pr["turned"], 6)

            def product(j, u):
                pe.wait_ge(pr[f"w{u}"], j * 16 + 16)
                for c in range(3):
                    pe.wait_ge(pr["y_put"], j * 6 + (3 * u + c + 1))
                    for k in range(pr["k"]):
                        mm = pe.matmul(PS[3 * u + c][:, 0:CH], pr["w"][:, u, k, :], pr["rhs"][:, k, c * CH:(c + 1) * CH],
                                       start=(k == 0), stop=(k == pr["k"] - 1))
                    mm.then_inc(pr["y_ps"], 1)

            def turn(j, u):
                pe.wait_ge(pr["y_put"], j * 6 + (6 + 3 * u + 3))
                for g in range(3):
                    pe.wait_ge(pr["added"], j * 6 + (3 * u + g + 1))
                    for i in range(4 * g, min(4 * g + 4, TILES)):
                        mm = pe.transpose(PS[6 + (3 * u + g) % 2][0:rows(i), (i % 4) * P:(i % 4 + 1) * P],
                                          pr["y"][:, u, tile_cols(i)], ident)
                    mm.then_inc(pr["turned"], 1)

            product(0, 0)
            with pe.Fori(0, MD // 2 - 1) as j:
                product(j, 1)
                turn(j, 0)
                product(j + 1, 0)
                turn(j, 1)
            product(MD // 2 - 1, 1)
            turn(MD // 2 - 1, 0)
            turn(MD // 2 - 1, 1)

        def act_proj(act, pr):
            act.sem_inc(pr["y_put"], 6)
            with act.Fori(0, MD // 2) as j:
                for u in range(2):
                    for c in range(3):
                        act.wait_ge(pr["y_ps"], j * 6 + (6 + 3 * u + c + 1))
                        if c == 0:
                            act.wait_ge(pr["turned"], j * 6 + (3 * u + 3))
                        act.activation(pr["y"][:, u, c * CH:(c + 1) * CH], PS[3 * u + c][:, 0:CH], ACT.Copy)\
                            .then_inc(pr["y_put"], 1)

        def dve_proj(dve, pr):
            dve.sem_inc(pr["added"], 2)
            with dve.Fori(0, MD // 2) as j:
                for u in range(2):
                    for g in range(3):
                        bank = PS[6 + (3 * u + g) % 2]
                        dve.wait_ge(pr["turned"], j * 6 + (6 + 3 * u + g + 1))
                        if g < 2:
                            x = x_tm[:, 4 * g:4 * g + 4, bass.ds(j * (2 * P) + u * P, P)]
                            y = bank[:, :].rearrange("p (i n) -> p i n", i=4)
                        else:
                            x = x_tm[0:SMP, LAST, bass.ds(j * (2 * P) + u * P, P)]
                            y = bank[0:SMP, 0:P]
                        dve.scalar_tensor_tensor(out=x, in0=x, scalar=float(ALPHA), in1=y, op0=ALU.mult, op1=ALU.add)\
                            .then_inc(pr["added"], 1)

        def dve_norm(dve, pr):
            dve.memset(moments, 1.0).then_inc(pr["stat"], 1)
            dve.wait_ge(pr["added"], 2 + 3 * MD)
            dve.wait_ge(pr["stat"], 1)
            for i in range(TILES):
                r = rows(i)
                for c in range(2):
                    s = dve.bn_stats(stats[0:r, i, 6 * c:6 * c + 6], x_tm[0:r, i, 512 * c:512 * c + 512])
            s.then_inc(pr["stat"], 1)
            dve.wait_ge(pr["stat"], 2)
            for i in range(TILES):
                r = rows(i)
                s = dve.bn_aggr(moments[0:r, i, :], stats[0:r, i, :])
            s.then_inc(pr["stat"], 1)
            dve.wait_ge(pr["stat"], 3)
            dve.tensor_scalar(rstd, moments[:, :, 1], float(EPS), None, ALU.add).then_inc(pr["var_in"], 1)
            dve.wait_ge(pr["std"], 1)
            dve.reciprocal(rstd, rstd).then_inc(pr["stat"], 1)
            dve.wait_ge(pr["stat"], 4)
            dve.wait_ge(pr["gb_in"], 32)
            for i in range(TILES):
                r = rows(i)
                x = x_tm[0:r, i, :]
                dve.tensor_scalar(x, x, moments[0:r, i, 0:1], rstd[0:r, i:i + 1], ALU.subtract, ALU.mult)\
                    .then_inc(pr["stat"], 1)
                dve.wait_ge(pr["stat"], 5 + i)
                dve.tensor_tensor(x, x, pr["g"][0:r, :], ALU.mult).then_inc(pr["centred"], 1)

        def act_std(act, pr):
            act.wait_ge(pr["var_in"], 1)
            act.activation(rstd, rstd, ACT.Sqrt).then_inc(pr["std"], 1)

        def pool_norm(pool, pr):
            for i in range(TILES):
                r = rows(i)
                pool.wait_ge(pr["centred"], i + 1)
                x = x_tm[0:r, i, :]
                pool.tensor_tensor(x, x, pr["b"][0:r, :], ALU.add).then_inc(pr["normed"], 1)

        def pe_x1(pe):
            pr = proj["out"]
            for i in range(TILES):
                r = rows(i)
                pe.wait_ge(pr["normed"], i + 1)
                for g in range(2):
                    n = 2 * i + g
                    if n >= 4:
                        pe.wait_ge(pr["nput"], n - 3)
                    for k in range(4):
                        mm = pe.transpose(PS[n % 4][:, k * P:k * P + r], x_tm[0:r, i, (4 * g + k) * P:(4 * g + k + 1) * P],
                                          ident[0:r, 0:r])
                    mm.then_inc(pr["nT"], 1)

        def act_x1(act):
            pr = proj["out"]
            for i in range(TILES):
                for g in range(2):
                    n = 2 * i + g
                    act.wait_ge(pr["nT"], n + 1)
                    act.activation(x1T[:, 4 * g:4 * g + 4, tile_cols(i)],
                                   PS[n % 4][:, :].rearrange("p (k n) -> p k n", k=4)[:, :, 0:rows(i)], ACT.Copy)\
                        .then_inc(pr["nput"], 1)

        def sp_gate_up(sp):
            wg = w_gate[0].rearrange("(k p) n -> p k n", p=P)
            wu = w_up[0].rearrange("(k p) n -> p k n", p=P)
            with sp.Fori(0, MF // 2) as j:
                for u in range(2):
                    sp.wait_ge(gu_ps, j * 6 + (3 * u + 3))
                    sp.dma_start(wgu[:, u, 0], wg[:, :, bass.ds(j * (2 * P) + u * P, P)]).then_inc(gu_in[u], 16)
                    sp.dma_start(wgu[:, u, 1], wu[:, :, bass.ds(j * (2 * P) + u * P, P)]).then_inc(gu_in[u], 16)

        def pe_gate_up(pe):
            pe.wait_ge(proj["out"]["nput"], 2 * TILES)
            with pe.Fori(0, MF // 2) as j:
                for u in range(2):
                    pe.wait_ge(gu_in[u], j * 32 + 32)
                    for c in range(3):
                        pe.wait_ge(h_made, j * 6 + (3 * u + c + 1))
                        for w in range(2):
                            for k in range(KD):
                                mm = pe.matmul(PS[2 * c + w][:, 0:CH], wgu[:, u, w, k, :], x1T[:, k, c * CH:(c + 1) * CH],
                                               start=(k == 0), stop=(k == KD - 1))
                        mm.then_inc(gu_ps, 1)

        def act_gate_up(act):
            with act.Fori(0, MF // 2) as j:
                for u in range(2):
                    for c in range(3):
                        n = 3 * u + c
                        act.wait_ge(gu_ps, j * 6 + (6 + n + 1))
                        act.wait_ge(h_made, j * 6 + (n + 2))
                        act.activation(silu[:, n % 2, :], PS[2 * c][:, 0:CH], ACT.Silu).then_inc(silu_done, 1)

        def dve_gate_up(dve):
            with dve.Fori(0, MF // 2) as j:
                for u in range(2):
                    for c in range(3):
                        n = 3 * u + c
                        dve.wait_ge(silu_done, j * 6 + (n + 1))
                        dve.tensor_tensor(hT_flat[:, bass.ds(j * (2 * T) + (u * T + c * CH), CH)], silu[:, n % 2, :],
                                          PS[2 * c + 1][:, 0:CH], ALU.mult).then_inc(h_made, 1)

        def sp_phase5(sp):
            sp.wait_ge(gated, MH)
            for i in range(TILES):
                src = x_prompt[0, i * P:(i + 1) * P, :] if i < LAST else x_sample.rearrange("b t d -> (b t) d")
                sp.dma_start(x_tm[0:rows(i), i, :], src).then_inc(x_back, 16)
            pr = proj["out"]
            sp.dma_start(pr["g"], pr["dg"][0].partition_broadcast(P)).then_inc(pr["gb_in"], 16)
            sp.dma_start(pr["b"], pr["db"][0].partition_broadcast(P)).then_inc(pr["gb_in"], 16)
            sp_proj(sp, pr)
            sp_gate_up(sp)
            pr = proj["down"]
            sp.wait_ge(gu_ps, 6 + 3 * MF)
            sp.dma_start(pr["g"], pr["dg"][0].partition_broadcast(P)).then_inc(pr["gb_in"], 16)
            sp.dma_start(pr["b"], pr["db"][0].partition_broadcast(P)).then_inc(pr["gb_in"], 16)
            sp_proj(sp, pr)
            for i in range(TILES):
                sp.wait_ge(pr["normed"], i + 1)
                dst = y_prompt[0, i * P:(i + 1) * P, :] if i < LAST else y_sample.rearrange("b t d -> (b t) d")
                sp.dma_start(dst, x_tm[0:rows(i), i, :]).then_inc(y_stored, 16)
            sp.wait_ge(y_stored, 16 * TILES)

        def pe_phase5(pe):
            pe.wait_ge(gated, MH)
            pe.sem_inc(gu_ps, 6)
            pe_proj(pe, proj["out"])
            pe_x1(pe)
            pe_gate_up(pe)
            pe.wait_ge(h_made, 3 + 3 * MF)
            pe_proj(pe, proj["down"])

        def act_phase5(act):
            act_proj(act, proj["out"])
            act_std(act, proj["out"])
            act_x1(act)
            act_gate_up(act)
            act_proj(act, proj["down"])
            act_std(act, proj["down"])

        def dve_phase5(dve):
            dve.wait_ge(x_back, 16 * TILES)
            dve.sem_inc(h_made, 3)
            dve_proj(dve, proj["out"])
            dve_norm(dve, proj["out"])
            dve_gate_up(dve)
            dve_proj(dve, proj["down"])
            dve_norm(dve, proj["down"])

        def sp_rest(sp):
            sp_attention(sp)
            sp_samples(sp)
            sp_mlstm(sp)
            sp_phase5(sp)

        def pe_rest(pe):
            pe_attention(pe)
            pe_samples(pe)
            pe_rows(pe)
            pe_mlstm(pe)
            pe_phase5(pe)

        def act_rest(act):
            act_attention(act)
            act_samples(act)
            act_rows(act)
            act_mlstm(act)
            act_phase5(act)

        def pool_rest(pool):
            pool_mlstm(pool)
            pool_norm(pool, proj["out"])
            pool_norm(pool, proj["down"])

        def dve_rest(dve):
            dve_attention(dve)
            dve_samples(dve)
            dve_rows(dve)
            dve_mlstm(dve)
            dve_phase5(dve)

        block = ctx.enter_context(nc.Block())

        @block.sync
        def _(sp):
            sp.dma_start(sq, c_square).then_inc(square_in, 16)

            def load_x(i):
                if i >= 3:
                    sp.wait_ge(filled, pos["xT", i - 3, 1] + 1)
                src = x_prompt[0, i * P:(i + 1) * P, :] if i < LAST else x_sample.rearrange("b t d -> (b t) d")
                sp.dma_start(xin[0:rows(i), i % 3, :], src).then_inc(x_in[i % 3], 16)

            def load_w(g):
                s = big.index(g)
                if s >= 2:
                    before = max(n for n, j in enumerate(jobs) if j[0] in ("tm", "fm") and j[1] == big[s - 2])
                    sp.wait_ge(filled, before + 1)
                src = w_in[0, :, col[g]:col[g] + 512].rearrange("(k p) n -> p k n", p=P)
                for k in range(0, KD, 4):
                    sp.dma_start(wslot[:, s % 2, k:k + 4, :], src[:, k:k + 4, :]).then_inc(w_in_s[s % 2], 16)

            for i in range(3):
                load_x(i)
            load_w("iq")
            for i in range(3, TILES):
                load_x(i)
            sp.dma_start(rope, c_rope).then_inc(const_in, 16)
            sp.dma_start(small, c_small).then_inc(const_in, 16)
            sp.dma_start(crow[0:MH, :], c_rows).then_inc(const_in, 16)
            sp.dma_start(ptab[:, :], page_table.rearrange("(a b) n -> a (b n)", a=1)).then_inc(const_in, 16)
            sp.dma_start(gate_b[0:MH, :], b_gate[0, :].rearrange("(w h) -> h w", w=2),
                         allow_slow_non_contiguous=True).then_inc(const_in, 16)
            win = w_in[0].rearrange("(k p) n -> p k n", p=P)
            sp.dma_start(wsm[:, :, 0:NSM], win[:, :, IK:IK + NSM]).then_inc(wsm_in, 16)
            sp.dma_start(wsm[:, :, NSM:80], win[:, :, MI:MI + 8]).then_inc(wsm_in, 16)
            load_w("ak")
            sp.wait_ge(const_in, 16 * 5)
            with sp.Fori(0, NB * PAGES) as j:
                page = sp.value_load(ptab[0:1, bass.ds(j, 1)], min_val=0, max_val=cache_kidx.shape[1] - 1)
                for twin in range(2):
                    sp.dma_start(mkT_flat[:, bass.ds(j * P + twin * IDX_D, IDX_D)],
                                 cache_kidx[0, bass.ds(page, 1)].rearrange("a p n -> (a p) n")).then_inc(kix_in, 16)

            def store(g, i):
                j = ("tm", g, i)
                s = stage_no[j] % STG
                if g in ("ak", "ik"):
                    sp.wait_ge(roped, rope_no[j] + 1)
                else:
                    sp.wait_ge(freed, pos[j] + 1)
                smp, prm, w = dict(ak=(k_sample, k_prompt, AW), av=(v_sample, v_prompt, AW),
                                   ik=(kidx_sample, kidx_prompt, IDX_D), mv=(None, None, 512))[g]
                if g == "mv":
                    dst = mv_dram[i * P:i * P + rows(i), :]
                elif i == LAST:
                    dst = smp[0].rearrange("b t h n -> (b t) (h n)") if g != "ik" else smp[0].rearrange("b t n -> (b t) n")
                else:
                    dst = prm[0, 0, i * P:(i + 1) * P]
                    if g != "ik":
                        dst = dst.rearrange("t h n -> t (h n)")
                sp.dma_start(dst, stage[0:rows(i), s, 0:w]).then_inc(stored[s], 16)

            for i in range(TILES):
                store("ik", i)
            sp.dma_start(iw_dram, iw[0:SMP, LAST, :]).then_inc(wcol_in, 16)
            sp.wait_ge(wcol_in, 16)
            for b in range(NB):
                sp.dma_start(wcol[32 * (b % 4):32 * (b % 4) + 32, b // 4:b // 4 + 1],
                             iw_dram[NT * b:NT * b + NT, :].rearrange("t h -> h t"),
                             allow_slow_non_contiguous=True).then_inc(wcol_in, 16)
            for i in range(TILES):
                store("ak", i)
            load_w("aq")
            load_w("av")
            for i in range(TILES):
                store("av", i)
            load_w("mv")
            load_w("mk")
            for i in range(TILES):
                store("mv", i)
            load_w("mq")
            load_w("mo")
            for s in range(STG):
                sp.wait_ge(stored[s], 16 * seen[s])
            sp_rest(sp)

        @block.tensor
        def _(pe):
            pe.wait_ge(square_in, 16)
            for n, job in enumerate(jobs):
                kind = job[0]
                bank = PS[n % RING]
                if n >= RING:
                    pe.wait_ge(freed, n - RING + 1)
                if kind == "xT":
                    _, i, j = job
                    r = rows(i)
                    if j == 0:
                        pe.wait_ge(x_in[i % 3], 16 * (i // 3 + 1))
                    for k in range(4):
                        mm = pe.transpose(bank[:, k * P:k * P + r], xin[0:r, i % 3, (4 * j + k) * P:(4 * j + k + 1) * P],
                                          ident[0:r, 0:r])
                elif kind == "tm":
                    _, g, i = job
                    if g == "ik":
                        pe.wait_ge(wsm_in, 32)
                        w, wd = wsm, NSM
                    else:
                        s = big.index(g)
                        pe.wait_ge(w_in_s[s % 2], 32 * (s // 2 + 1))
                        w, wd = wslot[:, s % 2], 512
                    pe.wait_ge(freed, pos["xT", i, 1] + 1)
                    for k in range(KD):
                        mm = pe.matmul(bank[0:rows(i), 0:wd], xT[:, k, tile_cols(i)], w[:, k, 0:wd],
                                       start=(k == 0), stop=(k == KD - 1))
                elif kind == "tr":
                    _, g, i = job
                    r = rows(i)
                    pe.wait_ge(roped, rope_no["tm", g, i] + 1)
                    s = stage_no["tm", g, i] % STG
                    for k in range(1 if g == "ik" else 4):
                        mm = pe.transpose(bank[:, k * P:k * P + r], stage[0:r, s, k * P:(k + 1) * P], ident[0:r, 0:r])
                elif kind == "idx":
                    _, i, h, c = job
                    wd = min(512, widths[i] - 512 * c)
                    if h == 0 and c == 0:
                        pe.wait_ge(freed, pos["tr", "ik", i] + 1)
                    lo = 64 * (h % 2)
                    mm = pe.matmul(bank[:, 0:wd], iqT[lo:lo + 64, h // 2, tile_cols(i)],
                                   kiT[lo:lo + 64, 512 * c:512 * c + wd], start=True, stop=True)
                elif kind == "kxT":
                    _, q = job
                    if q == 0:
                        pe.wait_ge(kix_in, 2 * 16 * NB * PAGES)
                    for j in range(4):
                        mm = pe.transpose(bank[:, j * P:(j + 1) * P], kix[:, 4 * q + j, :], ident)
                elif kind == "idxd":
                    _, g = job
                    pe.wait_ge(freed, pos["kxT", 3] + 1)
                    for b4 in range(4):
                        b = 4 * g + b4
                        o = bank[32 * b4:32 * b4 + 32]
                        for q in range(4):
                            mm = pe.matmul(o[:, 0:PAST], qbd[:, q, b, :],
                                           kixT[:, PAGES * b:PAGES * b + PAGES, :].rearrange("p j n -> p (j n)"),
                                           start=(q == 0), stop=(q == 3), tile_position=(0, 32 * b4))
                        for q in range(4):
                            mm = pe.matmul(o[:, PAST:SC_W], qbd[:, q, b, :], kiT[:, SEQ:T],
                                           start=(q == 0), stop=(q == 3), tile_position=(0, 32 * b4))
                elif kind == "scd":
                    pe.wait_ge(freed, pos["idxd", 1] + 1)
                    pe.wait_ge(wsel_done, 2)
                    for g in range(2):
                        mm = pe.matmul(bank[0:SMP, 0:SC_W], wsel[:, g, :], relud[:, g, :], start=(g == 0), stop=(g == 1))
                elif kind == "fm":
                    _, g, m, c = job
                    s = big.index(g)
                    pe.wait_ge(w_in_s[s % 2], 32 * (s // 2 + 1))
                    for k in range(KD):
                        mm = pe.matmul(bank[:, 0:CH], wslot[:, s % 2, k, m * P:(m + 1) * P],
                                       xT[:, k, c * CH:(c + 1) * CH], start=(k == 0), stop=(k == KD - 1))
                elif kind == "gate":
                    _, w, c = job
                    for k in range(KD):
                        mm = pe.matmul(bank[0:MH, 0:CH], wsm[:, k, NSM + 4 * w:NSM + 4 * w + 4],
                                       xT[:, k, c * CH:(c + 1) * CH], start=(k == 0), stop=(k == KD - 1))
                mm.then_inc(filled, 1)
            pe_rest(pe)

        @block.scalar
        def _(act):
            for n, job in enumerate(jobs):
                kind = job[0]
                bank = PS[n % RING]
                if kind == "tm":
                    _, g, i = job
                    s = stage_no[job]
                    if s >= STG:
                        last = staged[s - STG]
                        if last[1] in ("iq", "ik", "ak", "aq"):
                            act.wait_ge(filled, pos["tr", last[1], last[2]] + 1)
                        if last in store_no:
                            act.wait_ge(stored[s % STG], 16 * store_no[last])
                if kind == "idx" and idx_no[job] >= 4:
                    act.wait_ge(scored, idx_no[job] - 3)
                act.wait_ge(filled, n + 1)
                if kind == "xT":
                    _, i, j = job
                    out = act.activation(xT[:, 4 * j:4 * j + 4, tile_cols(i)],
                                         bank[:, :].rearrange("p (k n) -> p k n", k=4)[:, :, 0:rows(i)], ACT.Copy)
                elif kind == "tm":
                    _, g, i = job
                    r, st = rows(i), stage[:, stage_no[job] % STG, :]
                    if g == "ik":
                        act.activation(iw[0:r, i, :], bank[0:r, IDX_D:NSM], ACT.Copy,
                                       scale=float(AH ** -0.5 * IDX_D ** -0.5))
                        act.activation(st[0:r, IDX_D:2 * IDX_D], bank[0:r, 0:IDX_D], ACT.Copy)
                        out = act.activation(st[0:r, 0:IDX_D], bank[0:r, 0:IDX_D], ACT.Copy)
                    else:
                        out = act.activation(st[0:r, :], bank[0:r, :], ACT.Copy)
                elif kind == "tr":
                    _, g, i = job
                    r = rows(i)
                    if g == "ik":
                        out = act.activation(kiT[:, tile_cols(i)], bank[:, 0:r], ACT.Copy)
                    else:
                        dst = turned_into[g]
                        if i == LAST and g in ("iq", "aq"):
                            act.wait_ge(zeroed, 1)
                            if g == "aq":
                                act.wait_ge(filled, pos["idxd", 1] + 1)
                            for h in range(AH):
                                lo = 64 * (h % 2)
                                act.activation(
                                    qbd[lo:lo + 64, h // 2, :, NT * h:NT * h + NT],
                                    bank[lo:lo + 64, (h // 2) * P:(h // 2) * P + SMP].rearrange("p (b t) -> p b t", b=NB),
                                    ACT.Copy)
                        out = act.activation(dst[:, :, tile_cols(i)],
                                             bank[:, :].rearrange("p (k n) -> p k n", k=4)[:, :, 0:r], ACT.Copy)
                elif kind == "idx":
                    _, i, h, c = job
                    wd = min(512, widths[i] - 512 * c)
                    out = act.activation(relu[:, idx_no[job] % 4, 0:wd], bank[:, 0:wd], ACT.Relu)
                elif kind == "kxT":
                    _, q = job
                    out = act.activation(kixT[:, 4 * q:4 * q + 4, :],
                                         bank[:, :].rearrange("p (k n) -> p k n", k=4), ACT.Copy)
                elif kind == "idxd":
                    if job[1] == 0:
                        act.wait_ge(scored, len(idx_jobs))
                    out = act.activation(relud[:, job[1], :], bank[:, 0:SC_W], ACT.Relu)
                elif kind == "scd":
                    out = act.activation(scd[0:SMP, :], bank[0:SMP, 0:SC_W], ACT.Copy)
                elif kind == "fm":
                    _, g, m, c = job
                    cols = slice(c * CH, (c + 1) * CH)
                    if g == "mq":
                        out = act.activation(mixT[:, m, cols], bank[:, 0:CH], ACT.Copy)
                    elif g == "mk":
                        out = act.activation(mkT[:, m, cols], bank[:, 0:CH], ACT.Copy, scale=float(P ** -0.5))
                    else:
                        out = act.activation(moT[:, m, cols], bank[:, 0:CH], ACT.Sigmoid)
                elif kind == "gate":
                    _, w, c = job
                    if w == 0 and c == 0:
                        act.wait_ge(const_in, 16 * 5)
                    out = act.activation(gates[0:MH, w, c * CH:(c + 1) * CH], bank[0:MH, 0:CH], ACT.Identity,
                                         bias=gate_b[0:MH, w:w + 1])
                out.then_inc(freed, 1)
            act_rest(act)

        @block.gpsimd
        def _(pool):
            pool.memset(qbd, 0.0).then_inc(zeroed, 1)
            pool.wait_ge(const_in, 16 * 5)
            steps = 0

            def rope_tile(job):
                nonlocal steps
                _, g, i = job
                r, hn = rows(i), 2 if g == "ik" else AH
                s = stage[0:r, stage_no[job] % STG, 0:hn * AD].rearrange("p (h n) -> p h n", h=hn)
                t = ropet[0:r, 0:hn * 32].rearrange("p (h n) -> p h n", h=hn)
                cos = rope[0:r, i, 0, :].unsqueeze(1).to_broadcast([r, hn, 16])
                sin = rope[0:r, i, 1, :].unsqueeze(1).to_broadcast([r, hn, 16])
                pool.wait_ge(freed, pos[job] + 1)
                if steps:
                    pool.wait_ge(roped, steps)
                pool.tensor_tensor(t[:, :, 0:16], s[:, :, 0:16], cos, ALU.mult)
                pool.tensor_tensor(t[:, :, 16:24], s[:, :, 8:16], sin[:, :, 0:8], ALU.mult)
                pool.tensor_tensor(t[:, :, 24:32], s[:, :, 0:8], sin[:, :, 8:16], ALU.mult).then_inc(rope_step, 1)
                pool.wait_ge(rope_step, steps + 1)
                pool.tensor_tensor(s[:, :, 0:16], t[:, :, 0:16], t[:, :, 16:32], ALU.add).then_inc(roped, 1)
                steps += 1

            for job in rope_jobs:
                rope_tile(job)
                if job == ("tm", "ik", LAST):
                    pool.wait_ge(wcol_in, 16 * (NB + 1))
                    for g in range(2):
                        pool.tensor_scalar(wsel[:, g, :], wsel_mask[:, g, :], wcol[:, g:g + 1], None, ALU.mult)\
                            .then_inc(wsel_done, 1)
            pool_rest(pool)

        @block.vector
        def _(dve):
            dve.wait_ge(square_in, 16)
            dve.wait_ge(const_in, 16 * 5)
            for job in idx_jobs:
                _, i, h, c = job
                r = idx_no[job]
                wd = min(512, widths[i] - 512 * c)
                cols = slice(512 * c, 512 * c + wd)
                dve.wait_ge(freed, pos[job] + 1)
                src = relu[:, r % 4, 0:wd]
                w = iw[:, i, h:h + 1]
                if h == 0:
                    dve.tensor_scalar(score[i][:, cols], src, w, None, ALU.mult).then_inc(scored, 1)
                else:
                    dve.wait_ge(scored, idx_no["idx", i, h - 1, c] + 1)
                    dve.scalar_tensor_tensor(out=score[i][:, cols], in0=src, scalar=w, in1=score[i][:, cols],
                                             op0=ALU.mult, op1=ALU.add).then_inc(scored, 1)
                if h == AH - 1 and 512 * c + wd == widths[i]:
                    dve.wait_ge(scored, r + 1)
                    diag = score[i][:, widths[i] - P:widths[i]]
                    dve.tensor_tensor(diag, diag, causal, ALU.add).then_inc(causal_done, 1)
            step = 0
            for a in range(FIRST_SPARSE, TILES - 1, 2):
                if step == 0:
                    dve.wait_ge(causal_done, n_sparse)
                with dve.Fori(0, TOPK // 8) as rnd:
                    for u in range(2):
                        dve.max(m8[:, 8 * u:8 * u + 8], score[a + u]).then_inc(topk_step, 1)
                    for u in range(2):
                        dve.wait_ge(topk_step, rnd * 4 + (step + 1 + u))
                        dve.sem_inc(topk_turn, 1)
                        dve.match_replace(score[a + u], m8[:, 8 * u:8 * u + 8], score[a + u], TAKEN)\
                            .then_inc(topk_step, 1)
                    dve.wait_ge(topk_step, rnd * 4 + (step + 4))
                step += 4 * (TOPK // 8)
            for i in range(FIRST_SPARSE, TILES - 1):
                dve.tensor_scalar(score[i], score[i], -2e38, NEG, ALU.is_gt, ALU.mult).then_inc(masks_done, 1)
            dve.wait_ge(freed, pos["scd",] + 1)
            sd, m8d = scd[0:SMP, :], m8[0:SMP, 16:24]
            dve.memset(m8[0:SMP, 24:32], TAKEN).then_inc(topk_step, 1)
            dve.tensor_tensor(sd[:, PAST:SC_W], sd[:, PAST:SC_W], new_mask, ALU.add).then_inc(topk_step, 1)
            step += 2
            dve.wait_ge(topk_step, step)
            with dve.Fori(0, TOPK_S // 8) as rnd:
                dve.max(m8d, sd).then_inc(topk_step, 1)
                dve.wait_ge(topk_step, rnd * 2 + (step + 1))
                dve.sem_inc(topk_turn, 1)
                dve.match_replace(sd, m8d, sd, TAKEN).then_inc(topk_step, 1)
                dve.wait_ge(topk_step, rnd * 2 + (step + 2))
            step += 2 * (TOPK_S // 8)
            dve.max(m8d, sd).then_inc(topk_step, 1)
            dve.wait_ge(topk_step, step + 1)
            dve.tensor_copy(m8[0:SMP, 24:25], m8d[:, 0:1]).then_inc(topk_step, 1)
            dve.wait_ge(topk_step, step + 2)
            dve.match_replace(sd, m8[0:SMP, 24:32], sd, TAKEN).then_inc(topk_step, 1)
            dve.wait_ge(topk_step, step + 3)
            dve.tensor_scalar(sd, sd, -2e38, NEG, ALU.is_gt, ALU.mult).then_inc(masks_done, 1)
            dve_rest(dve)


_INS = ['x_prompt', 'x_sample', 'cache_k', 'cache_v', 'cache_kidx', 'state_C', 'state_n', 'state_m', 'page_table',
        'w_in', 'b_gate', 'w_out', 'ln1_g', 'ln1_b', 'w_gate', 'w_up', 'w_down', 'ln2_g', 'ln2_b']
_OUTS = [(1, SEQ, D), (NB, NT, D), (1, 1, SEQ, AH, AD), (1, 1, SEQ, AH, AD), (1, 1, SEQ, IDX_D),
         (1, 1, MH, P, P), (1, 1, MH, P), (1, 1, MH),
         (1, NB, NT, AH, AD), (1, NB, NT, AH, AD), (1, NB, NT, IDX_D), (1, NB, MH, P, P), (1, NB, MH, P), (1, NB, MH)]
_SCRATCH = [(T, 512), (SMP, AH)]


def shape_constants():
    import numpy as np
    f = np.float32
    r = np.arange(P)
    square = np.zeros((P, 6, P), f)
    square[:, 0] = np.eye(P)
    square[:, 1] = np.where(r[None, :] <= r[:, None], 0, NEG)
    square[:, 2] = np.where(r[:, None] <= r[None, :], 0, NEG)
    square[:, 3] = 1
    bt = np.arange(SMP)
    for g in range(2):
        square[bt, 4 + g] = ((bt // NT)[:, None] == 4 * g + (r // 32)[None, :]) & ((bt % NT)[:, None] == (r % NT)[None, :])
    half = AD // 4 // 2
    pos = np.zeros((TILES, P), f)
    pos[:LAST] = np.arange(SEQ).reshape(LAST, P)
    pos[LAST] = PAST + r % NT
    inv = f(500000.0) ** (-(np.arange(half, dtype=f) / f(half)))
    ang = pos[:, :, None] * inv
    cos, sin = np.cos(ang), np.sin(ang)
    rope = np.stack([np.concatenate([cos, cos], -1), np.concatenate([-sin, sin], -1)], 2)
    small = np.zeros((P, 64 + 2 * SMP), f)
    small[:, 0:64] = square[0:SMP, 4:6].transpose(2, 1, 0).reshape(P, 64)
    own = ((bt // NT)[:, None] == (bt // NT)[None, :]) & (bt[None, :] <= bt[:, None])
    small[0:SMP, 64:96] = np.where(own, 0, NEG)
    small[0:SMP, 96:128] = np.where(own.T, 0, NEG)
    first = np.ones(T, f)
    first[0:SEQ:P] = 0
    first[SEQ:T:NT] = 0
    rows_ = np.concatenate([np.tile(first, (MH, 1)), np.repeat(np.eye(MH, dtype=f), P, axis=1)], 1)
    return [square.reshape(P, -1), np.ascontiguousarray(rope.transpose(1, 0, 2, 3)).reshape(P, -1), small,
            rows_.astype(f)]


def kernel(**inputs):
    import numpy as _np
    import concourse.bacc as _bacc
    from concourse import mybir as _mybir
    from concourse.bass_utils import run_bass_kernel_spmd as _run

    nc = _bacc.Bacc("TRN2", target_bir_lowering=False, num_devices=1)
    arrays, args = {}, []
    given = [(name, _np.ascontiguousarray(inputs[name])) for name in _INS]
    given += [(f"shape_constant_{n}", _np.ascontiguousarray(a)) for n, a in enumerate(shape_constants())]
    for name, a in given:
        arrays[f"in_{name}_dram"] = a
        args.append(nc.dram_tensor(f"in_{name}_dram", a.shape, _mybir.dt.from_np(a.dtype), kind="ExternalInput").ap())
    for i, shape in enumerate(_OUTS):
        args.append(nc.dram_tensor(f"out_{i}_dram", shape, F32, kind="ExternalOutput").ap())
    for i, shape in enumerate(_SCRATCH):
        args.append(nc.dram_tensor(f"scratch_{i}_dram", shape, F32, kind="Internal").ap())
    build(nc, *args)
    r = _run(nc, [arrays], core_ids=[0])
    return tuple(r.results[0][f"out_{i}_dram"] for i in range(len(_OUTS)))
```

```python
import concourse.bass as bass
from concourse import mybir
from contextlib import ExitStack

F32 = mybir.dt.float32
I32 = mybir.dt.int32
ALU = mybir.AluOpType
ACT = mybir.ActivationFunctionType

P = 128
D = 1024
KD = D // P
SEQ = 1024
NB, NT = 8, 4
SMP = NB * NT
T = SEQ + SMP
TILES = SEQ // P + 1
LAST = TILES - 1
CH = T // 3
MH = 4
AH, AD = 8, 64
AW = AH * AD
PAGES = 2
PAST = PAGES * P
SC_W = PAST + SMP
TOPK, TOPK_S = 256, (PAST + NT) // 4
FF = 2816
MF = FF // P
ALPHA = 2 ** 0.25
EPS = 1e-5
NEG = -1e30
TAKEN = -3e38
MQ, MK, MV, MO, MI, AQ, AK, AV, IQ, IK = 0, 512, 1024, 1536, 2048, 2056, 2568, 3080, 3592, 4104
IDX_D = 64
NSM = IDX_D + AH
RING = 6
ARENA = 52600
STG = 4
FIRST_SPARSE = TOPK // P


def rows(i):
    return SMP if i == LAST else P


def build(nc, x_prompt, x_sample, cache_k, cache_v, cache_kidx, state_C, state_n, state_m, page_table,
          w_in, b_gate, w_out, ln1_g, ln1_b, w_gate, w_up, w_down, ln2_g, ln2_b,
          c_square, c_rope, c_small, c_rows,
          y_prompt, y_sample, k_prompt, v_prompt, kidx_prompt, C_prompt, n_prompt, m_prompt,
          k_sample, v_sample, kidx_sample, C_sample, n_sample, m_sample,
          mv_dram, iw_dram):
    ctx = ExitStack()
    with ctx:
        def sem(name):
            return ctx.enter_context(nc.semaphore(name))

        arena_base = -(-nc.sbuf_base // 32) * 32
        ctx.enter_context(nc.sbuf_tensor("arena", [P, ARENA], F32))
        top = [0]

        def put(name, word, n, dt=F32):
            return nc.alloc_sbuf_tensor_at(name, [P, n], dt, offset=arena_base + 4 * word)[:, :]

        def take(n, name="buffer"):
            word = -(-top[0] // 8) * 8
            top[0] = word + n
            assert top[0] <= ARENA, top[0]
            return put(name, word, n)

        sq = take(6 * P).rearrange("p (c n) -> p c n", n=P)
        ident, causal, causal_t, ones = (sq[:, c, :] for c in range(4))
        expand = sq[0:SMP, 4:6, :]
        rope = take(TILES * 32).rearrange("p (i c n) -> p i c n", c=2, n=16)
        small = take(64 + SMP * 2)
        wsel_mask = small[:, 0:64].rearrange("p (g n) -> p g n", g=2)
        new_mask, new_mask_t = small[0:SMP, 64:96], small[0:SMP, 96:128]
        crow = take(T + MH * P)
        not_first = crow[0:MH, 0:T]
        head_row = crow[0:MH, T:T + MH * P].rearrange("q (h n) -> q h n", h=MH)
        iw = take(TILES * AH).rearrange("p (i h) -> p i h", h=AH)
        wcol = take(2)
        wsel = take(2 * SMP).rearrange("p (g n) -> p g n", g=2)
        gate_b = take(2)
        ptab = ctx.enter_context(nc.sbuf_tensor("ptab", [1, NB * PAGES], I32))
        m8 = take(32)
        scd = take(SC_W)
        qbd = take(NB * 4 * SMP).rearrange("p (q b n) -> p q b n", q=4, b=NB)
        gates = take(2 * T).rearrange("p (w t) -> p w t", w=2)
        mixT = take(8 * T).rearrange("p (k t) -> p k t", t=T)
        qT = mixT[:, 4:8, :]
        after_mix = top[0]
        kT_flat = take(4 * T)
        kT = kT_flat.rearrange("p (k t) -> p k t", t=T)
        mkT_flat = take(4 * T)
        mkT = mkT_flat.rearrange("p (k t) -> p k t", t=T)
        iqT = take(4 * T).rearrange("p (k t) -> p k t", t=T)
        moT = iqT
        kiT = take(T)
        widths = [(i + 1) * P for i in range(TILES - 1)]
        score_flat = take(sum(widths[FIRST_SPARSE:]))
        score, at = {}, 0
        for i in range(FIRST_SPARSE, TILES - 1):
            score[i] = score_flat[:, at:at + widths[i]]
            at += widths[i]
        stage = take(STG * AW).rearrange("p (s n) -> p s n", s=STG)
        ropet = take(AH * 32)
        work0 = top[0]
        xT = take(KD * T).rearrange("p (k t) -> p k t", t=T)
        wslot = take(2 * KD * 512).rearrange("p (s k n) -> p s k n", s=2, k=KD)
        wsm = take(KD * 80).rearrange("p (k n) -> p k n", k=KD)
        end_phase1 = top[0]
        xin = score_flat[:, 0:3 * D].rearrange("p (s n) -> p s n", s=3)
        kix = mkT_flat[:, 0:2048].rearrange("p (j n) -> p j n", n=P)
        kixT = mkT_flat[:, 2048:4096].rearrange("p (j n) -> p j n", n=P)
        relu = kT_flat[:, 0:4 * 512].rearrange("p (s n) -> p s n", s=4)
        relud = relu[:, 0:2, 0:SC_W]
        top[0] = work0
        v_tm = take(TILES * AW).rearrange("p (i n) -> p i n", n=AW)
        mv_tm = take(TILES * 512).rearrange("p (i n) -> p i n", n=512)
        work1 = top[0]

        PS = [ctx.enter_context(nc.psum_tensor(f"bank{i}", [P, 512], F32)) for i in range(8)]

        square_in = sem("square_in")
        const_in = sem("const_in")
        x_in = [sem(f"x_in{s}") for s in range(3)]
        w_in_s = [sem(f"w_in{s}") for s in range(2)]
        wsm_in = sem("wsm_in")
        kix_in = sem("kix_in")
        wcol_in = sem("wcol_in")
        filled, freed = sem("filled"), sem("freed")
        roped, rope_step = sem("roped"), sem("rope_step")
        stored = [sem(f"stored{s}") for s in range(STG)]
        scored = sem("scored")
        causal_done = sem("causal_done")
        topk_step, topk_turn = sem("topk_step"), sem("topk_turn")
        zeroed = sem("zeroed")
        wsel_done = sem("wsel_done")
        masks_done = sem("masks_done")

        big = ["iq", "ak", "aq", "av", "mv", "mk", "mq", "mo"]
        col = dict(iq=IQ, ak=AK, aq=AQ, av=AV, mv=MV, mk=MK, mq=MQ, mo=MO)
        jobs = [("xT", i, j) for i in range(TILES) for j in range(2)]

        def tm_jobs(g, turned):
            out = []
            for i in range(TILES):
                out.append(("tm", g, i))
                if turned and i >= 2:
                    out.append(("tr", g, i - 2))
            return out + ([("tr", g, TILES - 2), ("tr", g, TILES - 1)] if turned else [])

        jobs += tm_jobs("iq", True) + tm_jobs("ik", True)
        for i in range(FIRST_SPARSE, TILES - 1):
            jobs += [("idx", i, h, c) for h in range(AH) for c in range(-(-widths[i] // 512))]
        jobs += [("kxT", q) for q in range(4)] + [("idxd", g) for g in range(2)] + [("scd",)]
        jobs += tm_jobs("ak", True) + tm_jobs("aq", True) + tm_jobs("av", False) + tm_jobs("mv", False)
        for g in ("mk", "mq"):
            jobs += [("fm", g, m, c) for m in range(4) for c in range(3)]
        jobs += [("gate", w, c) for w in range(2) for c in range(3)]
        jobs += [("fm", "mo", m, c) for m in range(4) for c in range(3)]
        pos = {job: n for n, job in enumerate(jobs)}
        staged = [j for j in jobs if j[0] == "tm"]
        stage_no = {j: s for s, j in enumerate(staged)}
        rope_jobs = [j for j in staged if j[1] in ("iq", "ik", "ak", "aq")]
        rope_no = {j: r for r, j in enumerate(rope_jobs)}
        store_jobs = [j for j in staged if j[1] in ("ik", "ak", "av", "mv")]
        store_no, seen = {}, [0] * STG
        for j in store_jobs:
            seen[stage_no[j] % STG] += 1
            store_no[j] = seen[stage_no[j] % STG]
        idx_jobs = [j for j in jobs if j[0] == "idx"]
        idx_no = {j: r for r, j in enumerate(idx_jobs)}
        turned_into = dict(iq=iqT, ik=kiT, ak=kT, aq=qT)

        def tile_cols(i):
            return slice(i * P, i * P + rows(i))

        n_sparse = LAST - FIRST_SPARSE
        top[0] = work1
        masked = take(2 * SEQ).rearrange("p (s n) -> p s n", s=2)
        probT = take(2 * SEQ).rearrange("p (s j n) -> p s j n", s=2, j=LAST)
        att_out = take(2 * AW).rearrange("p (s n) -> p s n", s=2)
        kraw = take(2 * PAGES * AW).rearrange("p (s j n) -> p s j n", s=2, j=PAGES)
        prob_s = take(SC_W)
        probT_s = take(3 * P).rearrange("p (j n) -> p j n", n=P)
        negmax = take(4)
        rowsum = take(2 * AH).rearrange("p (s h) -> p s h", s=2)
        rinv = take(2 * AH).rearrange("p (s h) -> p s h", s=2)
        vpage = score_flat[:, 0:4 * PAGES * AW].rearrange("p (b j n) -> p b j n", b=4, j=PAGES)
        kpT = masked.rearrange("p s n -> p (s n)")[:, 0:2 * 4 * PAST].rearrange("p (s q n) -> p s q n", s=2, q=4)
        top[0] += 0
        dense01 = stage.rearrange("p s n -> p (s n)")[:, 0:3 * P]

        steps2 = [(i, h) for i in range(LAST) for h in range(AH)]
        N2 = len(steps2)
        wide = [0] * (N2 + 1)
        for n, (i, h) in enumerate(steps2):
            wide[n + 1] = wide[n] + (widths[i] > 512)

        def mask_of(i):
            if i >= FIRST_SPARSE:
                return score[i]
            return dense01[:, 0:P] if i == 0 else dense01[:, P:3 * P]

        v_loaded = sem("v_loaded")
        dense_ready = sem("dense_ready")
        att_scores, att_masked, att_exp = sem("att_scores"), sem("att_masked"), sem("att_exp")
        att_turned, att_left, att_right = sem("att_turned"), sem("att_left"), sem("att_right")
        att_values, att_scaled, att_oT, att_put = sem("att_values"), sem("att_scaled"), sem("att_oT"), sem("att_put")
        neg_step = sem("neg_step")
        turned_before = [0] * (N2 + 1)
        for n, (i, h) in enumerate(steps2):
            turned_before[n + 1] = turned_before[n] + 1 + (widths[i] > 512)

        def pe_attention(pe):
            pe.wait_ge(freed, len(jobs))
            pe.wait_ge(v_loaded, 16 * TILES)

            def scores(n):
                i, h = steps2[n]
                lo = 64 * (h % 2)
                if n >= 2:
                    pe.wait_ge(att_masked, n - 1)
                for c in range(-(-widths[i] // 512)):
                    wd = min(512, widths[i] - 512 * c)
                    mm = pe.matmul(PS[2 * (n % 2) + c][:, 0:wd], qT[lo:lo + 64, h // 2, tile_cols(i)],
                                   kT[lo:lo + 64, h // 2, 512 * c:512 * c + wd], start=True, stop=True)
                mm.then_inc(att_scores, 1)

            def turn(n):
                i, h = steps2[n]
                pe.wait_ge(att_exp, n + 1)
                for c in range(-(-widths[i] // 512)):
                    if c == 0 and n >= 1:
                        pe.wait_ge(att_left, n)
                    if c == 1 and wide[n] >= 1:
                        pe.wait_ge(att_right, wide[n])
                    for j in range(4 * c, min(4 * c + 4, i + 1)):
                        mm = pe.transpose(PS[4 + c][:, (j % 4) * P:(j % 4 + 1) * P],
                                          masked[:, n % 2, j * P:(j + 1) * P], ident)
                    mm.then_inc(att_turned, 1)

            def values(n):
                i, h = steps2[n]
                pe.wait_ge(att_left, n + 1)
                if wide[n + 1] > wide[n]:
                    pe.wait_ge(att_right, wide[n + 1])
                if h == 0 and i:
                    pe.wait_ge(att_scaled, i)
                for j in range(i + 1):
                    mm = pe.matmul(PS[6][:, h * AD:(h + 1) * AD], probT[:, n % 2, j, :],
                                   v_tm[:, j, h * AD:(h + 1) * AD], start=(j == 0), stop=(j == i))
                mm.then_inc(att_values, 1)

            def out_turn(i):
                pe.wait_ge(att_scaled, i + 1)
                if i:
                    pe.wait_ge(att_put, i)
                for k in range(4):
                    mm = pe.transpose(PS[7][:, k * P:(k + 1) * P], att_out[:, i % 2, k * P:(k + 1) * P], ident)
                mm.then_inc(att_oT, 1)

            for n in range(N2 + 3):
                if n < N2:
                    scores(n)
                if 1 <= n <= N2:
                    turn(n - 1)
                if n >= 3 and steps2[n - 3][1] == AH - 1:
                    out_turn(steps2[n - 3][0])
                if 2 <= n < N2 + 2:
                    values(n - 2)

        def dve_attention(dve):
            dve.wait_ge(stored[0], 16 * seen[0])
            dve.memset(dense01[:, P:2 * P], 0.0).then_inc(dense_ready, 1)
            dve.tensor_copy(dense01[:, 0:P], causal).then_inc(dense_ready, 1)
            dve.tensor_copy(dense01[:, 2 * P:3 * P], causal).then_inc(dense_ready, 1)
            dve.wait_ge(dense_ready, 3)
            dve.wait_ge(masks_done, n_sparse + 1)
            for n in range(N2 + 3):
                if n < N2:
                    i, h = steps2[n]
                    dve.wait_ge(att_scores, n + 1)
                    if n >= 2:
                        dve.wait_ge(att_turned, turned_before[n - 1])
                        dve.wait_ge(att_exp, n - 1)
                    nc_ = -(-widths[i] // 512)
                    for c in range(nc_):
                        wd = min(512, widths[i] - 512 * c)
                        dve.tensor_tensor_reduce(masked[:, n % 2, 512 * c:512 * c + wd], PS[2 * (n % 2) + c][:, 0:wd],
                                                 mask_of(i)[:, 512 * c:512 * c + wd], 1.0, -3e38, ALU.add, ALU.max,
                                                 m8[:, c:c + 1]).then_inc(neg_step, 1)
                    base = sum(-(-widths[a] // 512) + 1 for a, _ in steps2[:n])
                    dve.wait_ge(neg_step, base + nc_)
                    if nc_ == 2:
                        dve.scalar_tensor_tensor(out=m8[:, 2:3], in0=m8[:, 0:1], scalar=1.0, in1=m8[:, 1:2],
                                                 op0=ALU.mult, op1=ALU.max).then_inc(neg_step, 1)
                    else:
                        dve.tensor_copy(m8[:, 2:3], m8[:, 0:1]).then_inc(neg_step, 1)
                    dve.wait_ge(neg_step, base + nc_ + 1)
                    dve.tensor_scalar(negmax[:, n % 2:n % 2 + 1], m8[:, 2:3], -(AD ** -0.5), None, ALU.mult)\
                        .then_inc(att_masked, 1)
                if 1 <= n <= N2 and wide[n] > wide[n - 1]:
                    i, h = steps2[n - 1]
                    dve.wait_ge(att_turned, turned_before[n])
                    if n >= 3:
                        dve.wait_ge(att_values, n - 2)
                    dve.tensor_copy(probT[:, (n - 1) % 2, 4:i + 1, :],
                                    PS[5][:, 0:(i - 3) * P].rearrange("p (j n) -> p j n", n=P)).then_inc(att_right, 1)
                if n >= 2 and n < N2 + 2 and steps2[n - 2][1] == AH - 1:
                    i = steps2[n - 2][0]
                    dve.wait_ge(att_values, n - 1)
                    dve.reciprocal(rinv[:, i % 2, :], rowsum[:, i % 2, :]).then_inc(dense_ready, 1)
                    dve.wait_ge(dense_ready, 4 + i)
                    if i >= 2:
                        dve.wait_ge(att_oT, i - 1)
                    dve.tensor_tensor(att_out[:, i % 2, :].rearrange("p (h n) -> p h n", h=AH),
                                      PS[6][:, :].rearrange("p (h n) -> p h n", h=AH),
                                      rinv[:, i % 2, :].unsqueeze(2).to_broadcast([P, AH, AD]), ALU.mult)\
                        .then_inc(att_scaled, 1)

        def act_attention(act):
            for n in range(N2 + 3):
                if n < N2:
                    i, h = steps2[n]
                    act.wait_ge(att_masked, n + 1)
                    if h == 0 and i >= 2:
                        act.wait_ge(att_scaled, i - 1)
                    act.activation(masked[:, n % 2, 0:widths[i]], masked[:, n % 2, 0:widths[i]], ACT.Exp,
                                   bias=negmax[:, n % 2:n % 2 + 1], scale=float(AD ** -0.5),
                                   accum_out=rowsum[:, i % 2, h:h + 1]).then_inc(att_exp, 1)
                if 1 <= n <= N2:
                    i, h = steps2[n - 1]
                    k = min(4, i + 1)
                    act.wait_ge(att_turned, turned_before[n - 1] + 1)
                    if n >= 3:
                        act.wait_ge(att_values, n - 2)
                    act.activation(probT[:, (n - 1) % 2, 0:k, :],
                                   PS[4][:, 0:k * P].rearrange("p (j n) -> p j n", n=P), ACT.Copy).then_inc(att_left, 1)
                if n >= 3 and steps2[n - 3][1] == AH - 1:
                    i = steps2[n - 3][0]
                    act.wait_ge(att_oT, i + 1)
                    act.activation(qT[:, :, tile_cols(i)], PS[7][:, :].rearrange("p (k n) -> p k n", k=4), ACT.Copy)\
                        .then_inc(att_put, 1)

        def sp_attention(sp):
            sp.wait_ge(filled, len(jobs))
            for i in range(TILES):
                r = rows(i)
                src = v_prompt[0, 0, i * P:(i + 1) * P].rearrange("t h n -> t (h n)") if i < LAST else \
                    v_sample[0].rearrange("b t h n -> (b t) (h n)")
                sp.dma_start(v_tm[0:r, i, :], src).then_inc(v_loaded, 16)
            for i in range(TILES):
                sp.dma_start(mv_tm[0:rows(i), i, :], mv_dram[i * P:i * P + rows(i), :]).then_inc(mv_loaded, 16)

        kpage_in = [sem(f"kpage_in{s}") for s in range(2)]
        vpage_in = sem("vpage_in")
        mv_loaded = sem("mv_loaded")
        smp_kT, smp_kput = sem("smp_kT"), sem("smp_kput")
        smp_mask, smp_scores, smp_exp, smp_norm = sem("smp_mask"), sem("smp_scores"), sem("smp_exp"), sem("smp_norm")
        smp_turned, smp_put, smp_values, smp_out = sem("smp_turned"), sem("smp_put"), sem("smp_values"), sem("smp_out")
        smp_step = sem("smp_step")

        def sp_samples(sp):
            for g in range(2):
                for b4 in range(4):
                    b = 4 * g + b4
                    if b >= 2:
                        sp.wait_ge(smp_kT, 2 * (b - 1))
                    for j in range(PAGES):
                        page = sp.value_load(ptab[0:1, b * PAGES + j:b * PAGES + j + 1], min_val=0,
                                             max_val=cache_k.shape[1] - 1)
                        sp.dma_start(kraw[:, b % 2, j, :],
                                     cache_k[0, bass.ds(page, 1)].rearrange("a p h n -> (a p) (h n)"))\
                            .then_inc(kpage_in[b % 2], 16)
                        if b == 0 and j == 0:
                            sp.wait_ge(att_masked, N2)
                        if b4 == 0 and j == 0 and g:
                            sp.wait_ge(smp_values, 4 * g)
                        sp.dma_start(vpage[:, b4, j, :],
                                     cache_v[0, bass.ds(page, 1)].rearrange("a p h n -> (a p) (h n)"))\
                            .then_inc(vpage_in, 16)

        def pe_samples(pe):
            pe.wait_ge(att_put, LAST)
            pe.wait_ge(att_left, N2)
            pe.wait_ge(att_right, wide[N2])
            for g in range(2):
                S = PS[4 + g]
                pe.wait_ge(masks_done, n_sparse + 1)
                pe.matmul(S[:, 0:SC_W], expand[:, g, :], scd[0:SMP, :], start=True, stop=False, skip_group_check=True)
                for b4 in range(4):
                    b = 4 * g + b4
                    pe.wait_ge(kpage_in[b % 2], 16 * PAGES * (b // 2 + 1))
                    for j in range(PAGES):
                        n = PAGES * b + j
                        if n >= 2:
                            pe.wait_ge(smp_kput, n - 1)
                        for q in range(4):
                            mm = pe.transpose(PS[n % 2][:, q * P:(q + 1) * P], kraw[:, b % 2, j, q * P:(q + 1) * P], ident)
                        mm.then_inc(smp_kT, 1)
                    pe.wait_ge(smp_kput, PAGES * (b + 1))
                    o = S[32 * b4:32 * b4 + 32]
                    for q in range(4):
                        pe.matmul(o[:, 0:PAST], qbd[:, q, b, :], kpT[:, b % 2, q, :], start=False, stop=False,
                                  skip_group_check=True, tile_position=(0, 32 * b4))
                    for q in range(4):
                        mm = pe.matmul(o[:, PAST:SC_W], qbd[:, q, b, :], kT[:, q, SEQ:T], start=False, stop=(q == 3),
                                       skip_group_check=True, tile_position=(0, 32 * b4))
                    mm.then_inc(smp_scores, 1)
                pe.wait_ge(smp_norm, g + 1)
                if g:
                    pe.wait_ge(smp_put, g)
                for j in range(PAGES):
                    pe.transpose(PS[2][:, j * P:(j + 1) * P], prob_s[:, j * P:(j + 1) * P], ident)
                pe.transpose(PS[2][0:SMP, PAGES * P:3 * P], prob_s[:, PAST:SC_W], ident).then_inc(smp_turned, 1)
                pe.wait_ge(smp_put, g + 1)
                pe.wait_ge(vpage_in, 16 * PAGES * 4 * (g + 1))
                for b4 in range(4):
                    for q in range(4):
                        o = PS[6 + g][:, (4 * b4 + q) * SMP:(4 * b4 + q + 1) * SMP]
                        cols, hp = slice(32 * b4, 32 * b4 + 32), slice(q * P, (q + 1) * P)
                        for j in range(PAGES):
                            pe.matmul(o, vpage[:, b4, j, hp], probT_s[:, j, cols], start=(j == 0), stop=False)
                        mm = pe.matmul(o, v_tm[0:SMP, LAST, hp], probT_s[0:SMP, 2, cols], start=False, stop=True)
                    mm.then_inc(smp_values, 1)

        def act_samples(act):
            act.wait_ge(att_turned, turned_before[N2])
            for g in range(2):
                for b4 in range(4):
                    b = 4 * g + b4
                    for j in range(PAGES):
                        act.wait_ge(smp_kT, PAGES * b + j + 1)
                        if b >= 2:
                            act.wait_ge(smp_scores, b - 1)
                        act.activation(kpT[:, b % 2, :, j * P:(j + 1) * P],
                                       PS[(PAGES * b + j) % 2][:, :].rearrange("p (q n) -> p q n", q=4), ACT.Copy)\
                            .then_inc(smp_kput, 1)
                act.wait_ge(smp_mask, g + 1)
                act.activation(prob_s, PS[4 + g][:, 0:SC_W], ACT.Exp, bias=negmax[:, 2:3], scale=float(AD ** -0.5),
                               accum_out=negmax[:, 3:4]).then_inc(smp_exp, 1)
                act.wait_ge(smp_turned, g + 1)
                if g:
                    act.wait_ge(smp_values, 4 * g)
                act.activation(probT_s[:, 0:2, :], PS[2][:, 0:2 * P].rearrange("p (j n) -> p j n", j=2), ACT.Copy)
                act.activation(probT_s[0:SMP, 2, :], PS[2][0:SMP, 2 * P:3 * P], ACT.Copy).then_inc(smp_put, 1)

        def dve_samples(dve):
            for g in range(2):
                dve.wait_ge(smp_scores, 4 * (g + 1))
                if g:
                    dve.wait_ge(smp_exp, g)
                dve.tensor_reduce(m8[:, 0:1], PS[4 + g][:, 0:SC_W], mybir.AxisListType.X, ALU.max).then_inc(smp_step, 1)
                dve.wait_ge(smp_step, 3 * g + 1)
                dve.tensor_scalar(negmax[:, 2:3], m8[:, 0:1], -(AD ** -0.5), None, ALU.mult).then_inc(smp_mask, 1)
                dve.wait_ge(smp_exp, g + 1)
                dve.reciprocal(m8[:, 1:2], negmax[:, 3:4]).then_inc(smp_step, 1)
                dve.wait_ge(smp_step, 3 * g + 2)
                dve.tensor_scalar(prob_s, prob_s, m8[:, 1:2], None, ALU.mult).then_inc(smp_norm, 1)
                dve.wait_ge(smp_values, 4 * (g + 1))
                for h in range(AH):
                    lo = 64 * (h % 2)
                    src = PS[6 + g][lo:lo + 64, :].rearrange("p (b q n) -> p b q n", b=4, q=4)
                    c = dve.tensor_copy(qT[lo:lo + 64, h // 2, SEQ + 16 * g:SEQ + 16 * g + 16]
                                        .rearrange("p (b t) -> p b t", b=4), src[:, :, h // 2, NT * h:NT * h + NT])
                c.then_inc(smp_step, 1)
            dve.wait_ge(smp_step, 6)

        CK = TILES
        top[0] = work1
        qg = take(T)
        st = take(2 * P).rearrange("p (s n) -> p s n", s=2)
        kw = take(2 * P).rearrange("p (s n) -> p s n", s=2)
        hden = take(P)
        hinv = take(P)
        state = take(2 * 2 * P).rearrange("p (s n) -> p s n", s=2)
        c_smp = take(2 * NB * P).rearrange("p (s b n) -> p s b n", s=2, b=NB)
        kw_smp = take(NB * P).rearrange("p (b n) -> p b n", b=NB)
        acol = take(CK * MH).rearrange("p (c h) -> p c h", h=MH)
        qn = take(SMP)
        n_all = take(NB * MH + MH)
        m_prev = take(LAST + NB)
        n_rows = take(P)
        n_out = take(P)
        one_col = take(1)
        lf, ig = gates[0:MH, 1, :], gates[0:MH, 0, :]
        b_row, m_row, a_row, g_row = (score_flat[0:MH, r * T:(r + 1) * T] for r in range(4))
        e_row = kiT[0:MH, :]
        bb, gb, eb, wt = (kT[:, r, :] for r in range(4))

        m_in, nst_in = sem("m_in"), sem("nst_in")
        c_in = [sem(f"c_in{s}") for s in range(2)]
        row_step, row_act = sem("row_step"), sem("row_act")
        a_turned, a_put = sem("a_turned"), sem("a_put")
        n_turned, n_put = sem("n_turned"), sem("n_put")
        bc_filled, bc_freed = sem("bc_filled"), sem("bc_freed")
        wt_arg, wt_exp, qg_done, qn_done = sem("wt_arg"), sem("wt_exp"), sem("qg_done"), sem("qn_done")
        st_ps, st_done, kw_done = sem("st_ps"), sem("st_done"), sem("kw_done")
        nd_ps, cs_ps, cs_done, h_done = sem("nd_ps"), sem("cs_ps"), sem("cs_done"), sem("h_done")
        h_step, gated = sem("h_step"), sem("gated")
        c_stored = [sem(f"c_stored{s}") for s in range(2)]
        cp_stored = sem("cp_stored")
        m_stored = sem("m_stored")
        n_final, n_back, n_out_put, n_stored = sem("n_final"), sem("n_back"), sem("n_out_put"), sem("n_stored")

        def sp_mlstm(sp):
            sp.wait_ge(mp_zero, 1)
            sp.dma_start(m_prev[0:MH, LAST:LAST + NB], state_m[0].rearrange("b h -> h b"),
                         allow_slow_non_contiguous=True).then_inc(m_in, 16)
            sp.dma_start(n_rows[0:NB * MH, :], state_n[0].rearrange("b h d -> (b h) d")).then_inc(nst_in, 16)

            def load_c(h):
                sp.dma_start(c_smp[:, h % 2, :, :], state_C[0, :, h].rearrange("b d e -> d b e"))\
                    .then_inc(c_in[h % 2], 16)

            load_c(0)
            load_c(1)
            sp.wait_ge(row_step, 3 + NB)
            sp.dma_start(m_prompt[0, 0, :].rearrange("(h n) -> h n", n=1), m_row[:, SEQ - 1:SEQ]).then_inc(m_stored, 16)
            sp.dma_start(m_sample[0].rearrange("b h -> h b"),
                         m_row[:, SEQ:T].rearrange("h (b t) -> h b t", b=NB)[:, :, NT - 1],
                         allow_slow_non_contiguous=True).then_inc(m_stored, 16)
            for h in range(MH):
                sp.wait_ge(cs_done, CK * h + LAST)
                sp.dma_start(C_prompt[0, 0, h], state[:, 0, 0:P]).then_inc(cp_stored, 16)
                sp.wait_ge(cs_done, CK * h + CK)
                sp.dma_start(C_sample[0, :, h].rearrange("b d e -> d b e"), c_smp[:, h % 2, :, :])\
                    .then_inc(c_stored[h % 2], 16)
                if h + 2 < MH:
                    sp.wait_ge(c_stored[h % 2], 16)
                    load_c(h + 2)
            sp.wait_ge(n_out_put, 1)
            sp.dma_start(n_sample[0].rearrange("b h d -> (b h) d"), n_out[0:NB * MH, :]).then_inc(n_stored, 16)
            sp.dma_start(n_prompt[0, 0], n_out[NB * MH:NB * MH + MH, :]).then_inc(n_stored, 16)
            sp.wait_ge(n_stored, 32)
            sp.wait_ge(m_stored, 32)
            sp.wait_ge(cp_stored, 16 * MH)
            for s in range(2):
                sp.wait_ge(c_stored[s], 32)

        def dve_rows(dve):
            dve.wait_ge(smp_values, 8)
            dve.wait_ge(smp_scores, 8)
            dve.memset(m_prev[0:MH, 0:1], 0.0)
            dve.memset(one_col, 1.0).then_inc(mp_zero, 1)
            dve.scalar_tensor_tensor(out=a_row, in0=lf, scalar=-1.0, in1=lf, op0=ALU.mult, op1=ALU.max)\
                .then_inc(row_step, 1)
            dve.wait_ge(row_act, 1)
            dve.scalar_tensor_tensor(out=lf, in0=lf, scalar=0.0, in1=g_row, op0=ALU.min, op1=ALU.subtract)\
                .then_inc(row_step, 1)
            dve.wait_ge(row_step, 2)
            dve.tensor_tensor_scan(b_row, not_first, lf, 0.0, ALU.mult, ALU.add)
            dve.tensor_tensor_scan(m_row[:, 0:SEQ], lf[:, 0:SEQ], ig[:, 0:SEQ], 0.0, ALU.add, ALU.max)\
                .then_inc(row_step, 1)
            dve.wait_ge(m_in, 16)
            for b in range(NB):
                c = slice(SEQ + NT * b, SEQ + NT * b + NT)
                dve.tensor_tensor_scan(m_row[:, c], lf[:, c], ig[:, c], m_prev[0:MH, LAST + b:LAST + b + 1],
                                       ALU.add, ALU.max).then_inc(row_step, 1)
            step = 3 + NB
            dve.wait_ge(row_step, step)
            dve.tensor_copy(m_prev[0:MH, 1:LAST],
                            m_row[:, 0:SEQ].rearrange("h (c t) -> h c t", t=P)[:, 0:LAST - 1, P - 1])
            dve.tensor_tensor(a_row, ig, b_row, ALU.subtract).then_inc(row_step, 1)
            dve.wait_ge(row_step, step + 1)
            dve.tensor_tensor(b_row, b_row, m_row, ALU.subtract).then_inc(row_step, 1)
            dve.wait_ge(row_step, step + 2)
            dve.tensor_tensor(g_row[:, 0:SEQ].rearrange("h (c t) -> h c t", t=P),
                              b_row[:, 0:SEQ].rearrange("h (c t) -> h c t", t=P),
                              m_prev[0:MH, 0:LAST].unsqueeze(2).to_broadcast([MH, LAST, P]), ALU.add)
            dve.tensor_tensor(g_row[:, SEQ:T].rearrange("h (c t) -> h c t", t=NT),
                              b_row[:, SEQ:T].rearrange("h (c t) -> h c t", t=NT),
                              m_prev[0:MH, LAST:LAST + NB].unsqueeze(2).to_broadcast([MH, NB, NT]), ALU.add)\
                .then_inc(row_step, 1)

        ROWS_DONE = 3 + NB + 3

        def act_rows(act):
            act.wait_ge(row_step, 1)
            act.activation(e_row, a_row, ACT.Exp, scale=-1.0).then_inc(e_tmp, 1)
            act.wait_ge(e_tmp, 1)
            act.activation(g_row, e_row, ACT.Ln, bias=one_col[0:MH, :]).then_inc(row_act, 1)
            act.wait_ge(row_step, ROWS_DONE)
            act.activation(g_row, g_row, ACT.Exp)
            act.activation(e_row, m_row, ACT.Exp, scale=-1.0).then_inc(row_act, 1)
            act.wait_ge(a_turned, 1)
            act.activation(acol[:, 0:LAST, :], PS[3][:, 0:LAST * MH].rearrange("p (c h) -> p c h", h=MH), ACT.Copy)
            act.activation(acol[0:SMP, LAST, :], PS[3][0:SMP, LAST * MH:CK * MH], ACT.Copy)
            act.activation(n_all[:, 0:NB * MH], PS[3][:, 64:64 + NB * MH], ACT.Copy).then_inc(a_put, 1)

        def pe_rows(pe):
            pe.wait_ge(row_step, ROWS_DONE)
            pe.wait_ge(nst_in, 16)
            for c in range(CK):
                pe.transpose(PS[3][0:rows(c), c * MH:(c + 1) * MH], a_row[:, tile_cols(c)], ident[0:MH, 0:MH])
            pe.transpose(PS[3][:, 64:64 + NB * MH], n_rows[0:NB * MH, :], ident[0:NB * MH, 0:NB * MH])\
                .then_inc(a_turned, 1)
            pe.wait_ge(a_put, 1)
            pe.wait_ge(row_act, 2)

        def pe_mlstm(pe):
            def scores(q):
                h, c = divmod(q, CK)
                r = rows(c)
                if q:
                    pe.wait_ge(st_done, q)
                    pe.wait_ge(kw_done, q)
                pe.matmul(PS[3][0:r, 0:r], mkT[:, h, tile_cols(c)], mixT[:, h, tile_cols(c)], start=True, stop=True)
                pe.transpose(PS[4][0:r, 0:P], mkT[:, h, tile_cols(c)], ident).then_inc(st_ps, 1)

            def outputs(q):
                h, c = divmod(q, CK)
                r = rows(c)
                hs = slice(h * P, (h + 1) * P)
                ND = PS[5 + q % 2]
                w = st[0:r, q % 2, 0:r]
                pe.wait_ge(st_done, q + 1)
                pe.wait_ge(kw_done, q + 1)
                pe.wait_ge(qg_done, h + 1)
                if q >= 2:
                    pe.wait_ge(h_done, q - 1)
                if q:
                    pe.wait_ge(cs_done, q)
                qc = qg[:, tile_cols(c)]
                if c < LAST:
                    pe.matmul(ND[:, 0:P], mv_tm[:, c, hs], w, start=True, stop=(c == 0))
                    if c:
                        pe.matmul(ND[:, 0:P], state[:, c % 2, 0:P], qc, start=False, stop=True)
                    mm = pe.matmul(ND[:, P:2 * P], ones, w, start=True, stop=(c == 0))
                    if c:
                        mm = pe.matmul(ND[:, P:2 * P], state[:, c % 2, P:2 * P], qc, start=False, stop=True)
                    mm.then_inc(nd_ps, 1)
                    pe.matmul(PS[7][:, 0:P], kw[:, q % 2, :], mv_tm[:, c, hs], start=True, stop=True)
                    pe.matmul(PS[7][:, P:2 * P], kw[:, q % 2, :], ones, start=True, stop=True).then_inc(cs_ps, 1)
                else:
                    pe.wait_ge(c_in[h % 2], 16 * (h // 2 + 1))
                    pe.wait_ge(qn_done, h + 1)
                    pe.matmul(ND[:, 0:SMP], mv_tm[0:SMP, c, hs], w, start=True, stop=False, skip_group_check=True)
                    for b in range(NB):
                        pe.matmul(ND[:, NT * b:NT * b + NT], c_smp[:, h % 2, b, :], qc[:, NT * b:NT * b + NT],
                                  start=False, stop=True, skip_group_check=True)
                    pe.matmul(ND[:, P:P + SMP], ones[0:SMP, :], w, start=True, stop=False)
                    pe.matmul(ND[:, P:P + SMP], ones, qn, start=False, stop=True)
                    for b in range(NB):
                        mm = pe.matmul(ND[:, 2 * P + b:2 * P + b + 1], kw_smp[0:SMP, b, :], ones[0:SMP, 0:1],
                                       start=True, stop=True)
                    mm.then_inc(nd_ps, 1)
                    for b in range(NB):
                        mm = pe.matmul(PS[7 if b < 4 else 2][:, (b % 4) * P:(b % 4 + 1) * P], kw_smp[0:SMP, b, :],
                                       mv_tm[0:SMP, c, hs], start=True, stop=True)
                    mm.then_inc(cs_ps, 1)

            pe.wait_ge(mv_loaded, 16 * TILES)
            for h in range(MH):
                for n in range(9):
                    N = 9 * h + n
                    if N >= 2:
                        pe.wait_ge(bc_freed, N - 1)
                    row = (b_row, g_row, e_row)[n // 3]
                    c = n % 3
                    pe.matmul(PS[N % 2][:, 0:CH], head_row[:, h, :], row[:, c * CH:(c + 1) * CH], start=True, stop=True)\
                        .then_inc(bc_filled, 1)
                scores(CK * h)
                for c in range(CK):
                    if c + 1 < CK:
                        scores(CK * h + c + 1)
                    outputs(CK * h + c)
            pe.wait_ge(n_final, 2 * MH)
            pe.transpose(PS[0][0:NB * MH + MH, 0:P], n_all, ident).then_inc(n_back, 1)

        def act_mlstm(act):
            for h in range(MH):
                if h:
                    act.wait_ge(h_done, CK * h)
                    act.wait_ge(cs_done, CK * h)
                    act.wait_ge(qg_done, h)
                for n in range(9):
                    act.wait_ge(bc_filled, 9 * h + n + 1)
                    c = n % 3
                    act.activation((bb, gb, eb)[n // 3][:, c * CH:(c + 1) * CH], PS[(9 * h + n) % 2][:, 0:CH], ACT.Copy)\
                        .then_inc(bc_freed, 1)
                act.wait_ge(wt_arg, h + 1)
                for c in range(CK):
                    r = rows(c)
                    e = act.activation(wt[0:r, tile_cols(c)], wt[0:r, tile_cols(c)], ACT.Exp, bias=acol[0:r, c, h:h + 1])
                e.then_inc(wt_exp, 1)
                act.wait_ge(wt_exp, h + 1)
                for c in range(CK):
                    q = CK * h + c
                    r = rows(c)
                    act.wait_ge(st_ps, q + 1)
                    if c < LAST:
                        if q >= 2:
                            act.wait_ge(cs_ps, q - 1)
                        act.activation(kw[:, q % 2, :], PS[4][:, 0:P], ACT.Copy, scale=wt[:, (c + 1) * P - 1:(c + 1) * P])\
                            .then_inc(kw_done, 1)
                    else:
                        if h:
                            act.wait_ge(cs_ps, q)
                        for b in range(NB):
                            t = SEQ + NT * b + NT - 1
                            e = act.activation(kw_smp[0:SMP, b, :], PS[4][0:SMP, 0:P], ACT.Copy, scale=wt[0:SMP, t:t + 1])
                        e.then_inc(kw_done, 1)
            act.wait_ge(n_back, 1)
            act.activation(n_out[0:NB * MH + MH, :], PS[0][0:NB * MH + MH, 0:P], ACT.Copy).then_inc(n_out_put, 1)

        def pool_mlstm(pool):
            for h in range(MH):
                pool.wait_ge(bc_freed, 9 * h + 6)
                if h:
                    pool.wait_ge(nd_ps, CK * h)
                    pool.wait_ge(gated, h)
                pool.tensor_tensor(qg, mixT[:, h, :], gb, ALU.mult).then_inc(qg_done, 1)
                pool.wait_ge(qg_done, h + 1)
                if h == 0:
                    pool.wait_ge(a_put, 1)
                pool.tensor_tensor(qn.rearrange("p (b t) -> p b t", b=NB),
                                   qg[:, SEQ:T].rearrange("p (b t) -> p b t", b=NB),
                                   n_all[:, h:NB * MH:MH].unsqueeze(2).to_broadcast([P, NB, NT]), ALU.mult)\
                    .then_inc(qn_done, 1)
                pool.wait_ge(h_done, CK * (h + 1))
                pool.tensor_tensor(mixT[:, h, :], mixT[:, h, :], moT[:, h, :], ALU.mult).then_inc(gated, 1)

        def dve_mlstm(dve):
            steps = 0
            for h in range(MH):
                dve.wait_ge(bc_freed, 9 * h + 3)
                if h:
                    dve.wait_ge(kw_done, CK * h)
                dve.tensor_tensor(wt[:, 0:SEQ].rearrange("p (c t) -> p c t", t=P),
                                  bb[:, 0:SEQ].rearrange("p (c t) -> p c t", t=P),
                                  causal_t.unsqueeze(1).to_broadcast([P, LAST, P]), ALU.add)
                dve.tensor_tensor(wt[0:SMP, SEQ:T], bb[0:SMP, SEQ:T], new_mask_t, ALU.add).then_inc(wt_arg, 1)
                dve.wait_ge(bc_freed, 9 * h + 9)
                for c in range(CK):
                    q = CK * h + c
                    r = rows(c)
                    cols = tile_cols(c)
                    dve.wait_ge(st_ps, q + 1)
                    dve.wait_ge(wt_exp, h + 1)
                    if q >= 2:
                        dve.wait_ge(nd_ps, q - 1)
                    dve.tensor_tensor(st[0:r, q % 2, 0:r], PS[3][0:r, 0:r], wt[0:r, cols], ALU.mult)\
                        .then_inc(st_done, 1)
                    dve.wait_ge(nd_ps, q + 1)
                    ND = PS[5 + q % 2]
                    if steps:
                        dve.wait_ge(h_done, q)
                    dve.scalar_tensor_tensor(out=hden[:, 0:r], in0=ND[:, P:P + r], scalar=-1.0, in1=eb[:, cols],
                                             op0=ALU.mult, op1=ALU.max).then_inc(h_step, 1)
                    dve.wait_ge(h_step, 3 * steps + 1)
                    dve.tensor_tensor(hden[:, 0:r], ND[:, P:P + r], hden[:, 0:r], ALU.max).then_inc(h_step, 1)
                    dve.wait_ge(h_step, 3 * steps + 2)
                    dve.reciprocal(hinv[:, 0:r], hden[:, 0:r]).then_inc(h_step, 1)
                    dve.wait_ge(h_step, 3 * steps + 3)
                    steps += 1
                    if c == LAST:
                        n_h = n_all[:, h:NB * MH:MH]
                        g_last = gb[:, SEQ:T].rearrange("p (b t) -> p b t", b=NB)[:, :, NT - 1]
                        dve.wait_ge(qn_done, h + 1)
                        dve.tensor_tensor(n_h, n_h, g_last, ALU.mult).then_inc(n_final, 1)
                        dve.wait_ge(n_final, 2 * h + 1)
                        dve.tensor_tensor(n_h, n_h, ND[:, 2 * P:2 * P + NB], ALU.add).then_inc(n_final, 1)
                    dve.tensor_tensor(mixT[:, h, cols], ND[:, 0:r], hinv[:, 0:r], ALU.mult).then_inc(h_done, 1)
                    dve.wait_ge(cs_ps, q + 1)
                    if c == 0:
                        dve.tensor_copy(state[:, 1, :], PS[7][:, 0:2 * P]).then_inc(cs_done, 1)
                    elif c < LAST:
                        dve.wait_ge(cs_done, q)
                        if c == 1 and h:
                            dve.wait_ge(cp_stored, 16 * h)
                        u = dve.scalar_tensor_tensor(out=state[:, (c + 1) % 2, :], in0=state[:, c % 2, :],
                                                     scalar=gb[:, (c + 1) * P - 1:(c + 1) * P], in1=PS[7][:, 0:2 * P],
                                                     op0=ALU.mult, op1=ALU.add)
                        u.then_inc(cs_done, 1)
                        if c == LAST - 1:
                            dve.wait_ge(cs_done, q + 1)
                            dve.tensor_copy(n_all[:, NB * MH + h:NB * MH + h + 1], state[:, 0, P:P + 1])
                    else:
                        for b in range(NB):
                            t = SEQ + NT * b + NT - 1
                            u = dve.scalar_tensor_tensor(
                                out=c_smp[:, h % 2, b, :], in0=c_smp[:, h % 2, b, :], scalar=gb[:, t:t + 1],
                                in1=PS[7 if b < 4 else 2][:, (b % 4) * P:(b % 4 + 1) * P], op0=ALU.mult, op1=ALU.add)
                        u.then_inc(cs_done, 1)
        e_tmp, mp_zero = sem("e_tmp"), sem("mp_zero")

        F32R = mybir.dt.float32r
        XS0, GS0, WD0, WS0, HS0 = ARENA - 2 * KD * T, 12808, 21000, 23048, 27144
        xs = put("x_split", XS0, 2 * KD * T, F32R).rearrange("p (s k t) -> p s k t", s=2, k=KD)
        gs = put("gate_up_split", GS0, 8 * KD * P, F32R).rearrange("p (u s w k n) -> p u s w k n", u=2, s=2, w=2, k=KD)
        ws = put("weight_split", WS0, 4 * KD * P, F32R)
        hs = put("hidden_split", HS0, 4 * 2 * T, F32R).rearrange("p (m s t) -> p m s t", m=4, s=2)
        y_acc = put("y_acc", 768, KD * T).rearrange("p (k t) -> p k t", t=T)
        graw = put("gate_up", 9216, 2 * KD * P).rearrange("p (w k n) -> p w k n", w=2, k=KD)
        silu = put("silu", 11264, 2 * CH).rearrange("p (s n) -> p s n", s=2)
        hidden = put("hidden", 11968, CH)
        stats = put("stats", 12320, TILES * 12).rearrange("p (i n) -> p i n", n=12)
        moments = put("moments", 12432, TILES * 2).rearrange("p (i n) -> p i n", n=2)
        rstd = put("rstd", 12456, TILES)
        x_tm = put("x_tm", GS0, TILES * D).rearrange("p (i n) -> p i n", n=D)
        wdraw = put("down_weight", WD0, 2 * D).rearrange("p (k n) -> p k n", k=2)
        oraw = put("out_weight", HS0, 2 * KD * P).rearrange("p (s k n) -> p s k n", s=2, k=KD)
        o_y = put("out_y", HS0 + 2048, 2 * T).rearrange("p (s t) -> p s t", s=2)
        gain, bias_ = (put(f"norm_{n}", HS0 + 4160 + r * D, D) for r, n in enumerate(("gain", "bias")))
        os_ = ws.rearrange("p (u s k n) -> p u s k n", u=2, s=2, k=KD)
        wds = ws.rearrange("p (s k n) -> p s k n", s=2, k=2)
        norms = {}
        for name in ("first", "second"):
            norms[name] = {s: sem(f"{name}_{s}") for s in
                           ("gb_in", "in_place", "stat", "var_in", "std", "centred", "normed", "nT", "nput")}
        x_back = sem("x_back")
        mix_hi, mix_lo = sem("mix_hi"), sem("mix_lo")
        o_in = [sem("o_in0"), sem("o_in1")]
        o_hi, o_lo, y_ps, y_put, turned, added = (sem(s) for s in ("o_hi", "o_lo", "y_ps", "y_put", "turned", "added"))
        g_in, g_hi, g_lo = sem("g_in"), sem("g_hi"), sem("g_lo")
        wd_in, wd_hi, wd_lo = sem("wd_in"), sem("wd_hi"), sem("wd_lo")
        gu_ps, silu_done, h_made, h_step, h_hi2, h_lo2 = (sem(s) for s in (
            "gu_ps", "silu_done", "h_made", "hid_step", "h_hi", "h_lo"))
        d_ps, d_added = sem("d_ps"), sem("d_added")
        x1_lo = sem("x1_lo")
        y_stored = sem("y_stored")
        MD = D // P
        GROUPS = MF // 2
        PARTS = [(0, 0), (0, 1), (1, 0)]

        def sp_out(sp):
            sp.wait_ge(gated, MH)
            src = w_out[0].rearrange("(k p) n -> p k n", p=P)

            def load(j):
                for u in range(2):
                    sp.wait_ge(o_lo, j * 2 + (u + 1))
                    sp.dma_start(oraw[:, u], src[:, :, bass.ds(j * (2 * P) + u * P, P)]).then_inc(o_in[u], 16)

            load(0)
            sp_x_back(sp)
            with sp.Fori(1, MD // 2) as j:
                load(j)

        def sp_x_back(sp):
            sp.wait_ge(mix_lo, KD)
            for i in range(TILES):
                src = x_prompt[0, i * P:(i + 1) * P, :] if i < LAST else x_sample.rearrange("b t d -> (b t) d")
                sp.dma_start(x_tm[0:rows(i), i, :], src).then_inc(x_back, 16)
            sp.dma_start(gain, ln1_g[0].partition_broadcast(P)).then_inc(norms["first"]["gb_in"], 16)
            sp.dma_start(bias_, ln1_b[0].partition_broadcast(P)).then_inc(norms["first"]["gb_in"], 16)

        def pe_out(pe):
            pe.sem_inc(y_ps, 6)
            pe.sem_inc(turned, 6)

            def product(j, u, first=False):
                pe.wait_ge(o_lo, j * 2 + (2 + u + 1))
                for c in range(3):
                    pe.wait_ge(y_put, j * 6 + (3 * u + c + 1))
                    for k in range(KD):
                        if first and c == 0:
                            pe.wait_ge(mix_lo, k + 1)
                        for a, b in PARTS:
                            mm = pe.matmul(PS[3 * u + c][:, 0:CH], os_[:, u, a, k, :], xs[:, b, k, c * CH:(c + 1) * CH],
                                           start=(k == 0 and (a, b) == PARTS[0]),
                                           stop=(k == KD - 1 and (a, b) == PARTS[-1]))
                    mm.then_inc(y_ps, 1)

            def turn(j, u):
                pe.wait_ge(y_put, j * 6 + (6 + 3 * u + 3))
                for g in range(3):
                    pe.wait_ge(added, j * 6 + (3 * u + g + 1))
                    for i in range(4 * g, min(4 * g + 4, TILES)):
                        mm = pe.transpose(PS[6 + (3 * u + g) % 2][0:rows(i), (i % 4) * P:(i % 4 + 1) * P],
                                          o_y[:, u, tile_cols(i)], ident)
                    mm.then_inc(turned, 1)

            product(0, 0, True)
            with pe.Fori(0, MD // 2 - 1) as j:
                product(j, 1)
                turn(j, 0)
                product(j + 1, 0)
                turn(j, 1)
            product(MD // 2 - 1, 1)
            turn(MD // 2 - 1, 0)
            turn(MD // 2 - 1, 1)

        def act_out(act):
            act.sem_inc(y_put, 6)

            def high(j, u):
                act.wait_ge(o_in[u], j * 16 + 16)
                act.wait_ge(y_ps, j * 6 + (3 * u + 3))
                act.activation(os_[:, u, 0], oraw[:, u], ACT.Copy).then_inc(o_hi, 1)

            def empty(j, u):
                for c in range(3):
                    act.wait_ge(y_ps, j * 6 + (6 + 3 * u + c + 1))
                    if c == 0:
                        act.wait_ge(turned, j * 6 + (3 * u + 3))
                    act.activation(o_y[:, u, c * CH:(c + 1) * CH], PS[3 * u + c][:, 0:CH], ACT.Copy).then_inc(y_put, 1)

            act.wait_ge(gated, MH)
            high(0, 0)
            for k in range(KD):
                act.activation(xs[:, 0, k, :], mixT[:, k, :], ACT.Copy).then_inc(mix_hi, 1)
            with act.Fori(0, MD // 2 - 1) as j:
                high(j, 1)
                empty(j, 0)
                high(j + 1, 0)
                empty(j, 1)
            high(MD // 2 - 1, 1)
            empty(MD // 2 - 1, 0)
            empty(MD // 2 - 1, 1)

        def dve_out(dve):
            dve.sem_inc(added, 2)
            dve.sem_inc(o_lo, 2)

            def low(j, u):
                dve.wait_ge(o_hi, j * 2 + (u + 1))
                dve.tensor_tensor(os_[:, u, 1], oraw[:, u], os_[:, u, 0].bitcast(F32), ALU.subtract).then_inc(o_lo, 1)

            def add(j, u):
                for g in range(3):
                    bank = PS[6 + (3 * u + g) % 2]
                    dve.wait_ge(turned, j * 6 + (6 + 3 * u + g + 1))
                    if g < 2:
                        x = x_tm[:, 4 * g:4 * g + 4, bass.ds(j * (2 * P) + u * P, P)]
                        y = bank[:, :].rearrange("p (i n) -> p i n", i=4)
                    else:
                        x = x_tm[0:SMP, LAST, bass.ds(j * (2 * P) + u * P, P)]
                        y = bank[0:SMP, 0:P]
                    dve.scalar_tensor_tensor(out=x, in0=x, scalar=float(ALPHA), in1=y, op0=ALU.mult, op1=ALU.add)\
                        .then_inc(added, 1)

            low(0, 0)
            for k in range(KD):
                dve.wait_ge(mix_hi, k + 1)
                dve.tensor_tensor(xs[:, 1, k, :], mixT[:, k, :], xs[:, 0, k, :].bitcast(F32), ALU.subtract)\
                    .then_inc(mix_lo, 1)
            low(0, 1)
            dve.wait_ge(x_back, 16 * TILES)
            with dve.Fori(0, MD // 2 - 1) as j:
                add(j, 0)
                low(j + 1, 0)
                add(j, 1)
                low(j + 1, 1)
            add(MD // 2 - 1, 0)
            add(MD // 2 - 1, 1)

        def dve_norm(dve, nm, ready):
            dve.memset(moments, 1.0).then_inc(nm["stat"], 1)
            dve.wait_ge(nm["stat"], 1)
            for i in range(TILES):
                r = rows(i)
                ready(i)
                for c in range(2):
                    s = dve.bn_stats(stats[0:r, i, 6 * c:6 * c + 6], x_tm[0:r, i, 512 * c:512 * c + 512])
                s.then_inc(nm["stat"], 1)
            dve.wait_ge(nm["stat"], 1 + TILES)
            for i in range(TILES):
                r = rows(i)
                s = dve.bn_aggr(moments[0:r, i, :], stats[0:r, i, :])
            s.then_inc(nm["stat"], 1)
            dve.wait_ge(nm["stat"], 2 + TILES)
            dve.tensor_scalar(rstd, moments[:, :, 1], float(EPS), None, ALU.add).then_inc(nm["var_in"], 1)
            dve.wait_ge(nm["std"], 1)
            dve.reciprocal(rstd, rstd).then_inc(nm["stat"], 1)
            dve.wait_ge(nm["stat"], 3 + TILES)
            dve.wait_ge(nm["gb_in"], 32)
            for i in range(TILES + 1):
                if i < TILES:
                    r = rows(i)
                    x = x_tm[0:r, i, :]
                    dve.tensor_scalar(x, x, moments[0:r, i, 0:1], rstd[0:r, i:i + 1], ALU.subtract, ALU.mult)\
                        .then_inc(nm["stat"], 1)
                if i:
                    r = rows(i - 1)
                    x = x_tm[0:r, i - 1, :]
                    dve.wait_ge(nm["stat"], 3 + TILES + i)
                    dve.tensor_tensor(x, x, gain[0:r, :], ALU.mult).then_inc(nm["centred"], 1)

        def act_std(act, nm):
            act.wait_ge(nm["var_in"], 1)
            act.activation(rstd, rstd, ACT.Sqrt).then_inc(nm["std"], 1)

        def pool_norm(pool, nm):
            for i in range(TILES):
                r = rows(i)
                pool.wait_ge(nm["centred"], i + 1)
                x = x_tm[0:r, i, :]
                pool.tensor_tensor(x, x, bias_[0:r, :], ALU.add).then_inc(nm["normed"], 1)

        def pe_x1(pe):
            nm = norms["first"]
            for i in range(TILES):
                r = rows(i)
                pe.wait_ge(nm["normed"], i + 1)
                for g in range(2):
                    n = 2 * i + g
                    if n >= 4:
                        pe.wait_ge(nm["nput"], 2 * (n - 3))
                        pe.wait_ge(x1_lo, n - 3)
                    for k in range(4):
                        mm = pe.transpose(PS[n % 4][:, k * P:k * P + r], x_tm[0:r, i, (4 * g + k) * P:(4 * g + k + 1) * P],
                                          ident[0:r, 0:r])
                    mm.then_inc(nm["nT"], 1)

        def act_x1(act):
            nm = norms["first"]
            for n in range(2 * TILES):
                i, g = divmod(n, 2)
                act.wait_ge(nm["nT"], n + 1)
                src = PS[n % 4][:, :].rearrange("p (k n) -> p k n", k=4)[:, :, 0:rows(i)]
                act.activation(xs[:, 0, 4 * g:4 * g + 4, tile_cols(i)], src, ACT.Copy).then_inc(nm["nput"], 1)
                act.activation(y_acc[:, 4 * g:4 * g + 4, tile_cols(i)], src, ACT.Copy, scale=float(ALPHA))\
                    .then_inc(nm["nput"], 1)

        def dve_x1(dve):
            nm = norms["first"]
            for n in range(2 * TILES):
                i, g = divmod(n, 2)
                dve.wait_ge(nm["nput"], 2 * n + 2)
                src = PS[n % 4][:, :].rearrange("p (k n) -> p k n", k=4)[:, :, 0:rows(i)]
                dve.tensor_tensor(xs[:, 1, 4 * g:4 * g + 4, tile_cols(i)], src,
                                  xs[:, 0, 4 * g:4 * g + 4, tile_cols(i)].bitcast(F32), ALU.subtract).then_inc(x1_lo, 1)

        def sp_ffn(sp):
            wg = w_gate[0].rearrange("(k p) n -> p k n", p=P)
            wu = w_up[0].rearrange("(k p) n -> p k n", p=P)
            wd = w_down[0].rearrange("(m p) n -> p m n", p=P)

            def gate(g, u):
                sp.wait_ge(g_lo, g * 2 + (u + 1))
                for w, src in ((0, wg), (1, wu)):
                    sp.dma_start(graw[:, w], src[:, :, bass.ds(g * (2 * P) + u * P, P)]).then_inc(g_in, 16)

            gate(0, 0)
            sp.wait_ge(x1_lo, 2 * TILES)
            with sp.Fori(0, GROUPS - 1) as g:
                gate(g, 1)
                sp.wait_ge(wd_lo, g + 1)
                sp.dma_start(wdraw, wd[:, bass.ds(g * 2, 2), :]).then_inc(wd_in, 16)
                gate(g + 1, 0)
            gate(GROUPS - 1, 1)
            sp.wait_ge(wd_lo, GROUPS)
            sp.dma_start(wdraw, wd[:, 2 * (GROUPS - 1):2 * GROUPS, :]).then_inc(wd_in, 16)

        def pe_ffn(pe):
            pe.wait_ge(norms["first"]["nput"], 4 * TILES)
            pe.wait_ge(x1_lo, 2 * TILES)

            def gate(g, u):
                pe.wait_ge(g_lo, g * 2 + (u + 2))
                for c in range(3):
                    pe.wait_ge(h_made, g * 6 + (3 * u + c + 1))
                    for w in range(2):
                        for k in range(KD):
                            for a, b in PARTS:
                                mm = pe.matmul(PS[2 * c + w][:, 0:CH], gs[:, u, a, w, k, :],
                                               xs[:, b, k, c * CH:(c + 1) * CH],
                                               start=(k == 0 and (a, b) == PARTS[0]),
                                               stop=(k == KD - 1 and (a, b) == PARTS[-1]))
                    mm.then_inc(gu_ps, 1)

            def down(g, s):
                pe.wait_ge(wd_lo, g + 2)
                pe.wait_ge(h_lo2, g * 6 + 6)
                for d in range(MD):
                    for c in range(3):
                        n = 3 * d + c
                        pe.wait_ge(d_added, g * (3 * MD) + (n + 1))
                        for k in range(2):
                            for a, b in PARTS:
                                mm = pe.matmul(PS[6 + n % 2][:, 0:CH], wds[:, a, k, d * P:(d + 1) * P],
                                               hs[:, 2 * s + k, b, c * CH:(c + 1) * CH],
                                               start=(k == 0 and (a, b) == PARTS[0]),
                                               stop=(k == 1 and (a, b) == PARTS[-1]))
                        mm.then_inc(d_ps, 1)

            def body(g, s):
                gate(g, 0)
                down(g - 1, 1 - s)
                gate(g, 1)

            gate(0, 0)
            gate(0, 1)
            with pe.Fori(0, (GROUPS - 3) // 2) as j:
                body(j * 2 + 1, 1)
                body(j * 2 + 2, 0)
            body(GROUPS - 2, 1)
            body(GROUPS - 1, 0)
            down(GROUPS - 1, 0)

        def act_ffn(act):
            def high(g, u):
                act.wait_ge(g_in, g * 64 + (32 * u + 32))
                act.wait_ge(gu_ps, g * 6 + (3 * u + 3))
                act.activation(gs[:, u, 0], graw, ACT.Copy).then_inc(g_hi, 1)

            def gates_(g, u):
                for c in range(3):
                    n = 3 * u + c
                    act.wait_ge(gu_ps, g * 6 + (6 + n + 1))
                    act.wait_ge(h_made, g * 6 + (n + 2))
                    act.activation(silu[:, n % 2, :], PS[2 * c][:, 0:CH], ACT.Silu).then_inc(silu_done, 1)

            def high_down(g):
                act.wait_ge(wd_in, g * 16 + 16)
                act.wait_ge(d_ps, g * (3 * MD) + 3 * MD)
                act.activation(wds[:, 0], wdraw, ACT.Copy).then_inc(wd_hi, 1)

            def body(g, last=False):
                high(g, 1)
                gates_(g, 0)
                if not last:
                    high(g + 1, 0)
                high_down(g)
                gates_(g, 1)

            act.wait_ge(x1_lo, 2 * TILES)
            high(0, 0)
            with act.Fori(0, GROUPS - 1) as g:
                body(g)
            body(GROUPS - 1, True)

        def dve_ffn(dve):
            def low(g, u):
                dve.wait_ge(g_hi, g * 2 + (u + 1))
                dve.tensor_tensor(gs[:, u, 1], graw, gs[:, u, 0].bitcast(F32), ALU.subtract).then_inc(g_lo, 1)

            def low_down(g):
                dve.wait_ge(wd_hi, g + 1)
                dve.tensor_tensor(wds[:, 1], wdraw, wds[:, 0].bitcast(F32), ALU.subtract).then_inc(wd_lo, 1)

            def hide(g, u, s):
                for c in range(3):
                    n = 3 * u + c
                    slot, cols = 2 * s + u, slice(c * CH, (c + 1) * CH)
                    dve.wait_ge(silu_done, g * 6 + (n + 1))
                    dve.wait_ge(h_lo2, g * 6 + n) if not (isinstance(g, int) and g * 6 + n == 0) else None
                    dve.tensor_tensor(hidden, silu[:, n % 2, :], PS[2 * c + 1][:, 0:CH], ALU.mult).then_inc(h_made, 1)
                    dve.wait_ge(h_made, g * 6 + (3 + n + 1))
                    dve.tensor_copy(hs[:, slot, 0, cols], hidden).then_inc(h_hi2, 1)
                    dve.wait_ge(h_hi2, g * 6 + (n + 1))
                    dve.tensor_tensor(hs[:, slot, 1, cols], hidden, hs[:, slot, 0, cols].bitcast(F32), ALU.subtract)\
                        .then_inc(h_lo2, 1)

            def add(g):
                for d in range(MD):
                    for c in range(3):
                        n = 3 * d + c
                        y = y_acc[:, d, c * CH:(c + 1) * CH]
                        dve.wait_ge(d_ps, g * (3 * MD) + (3 * MD + n + 1))
                        dve.tensor_tensor(y, y, PS[6 + n % 2][:, 0:CH], ALU.add).then_inc(d_added, 1)

            def body(g, s, last=False):
                low(g, 1)
                hide(g, 0, s)
                if not last:
                    low(g + 1, 0)
                add(g - 1)
                low_down(g)
                hide(g, 1, s)

            low(0, 0)
            low(0, 1)
            hide(0, 0, 0)
            low(1, 0)
            low_down(0)
            hide(0, 1, 0)
            with dve.Fori(0, (GROUPS - 3) // 2) as j:
                body(j * 2 + 1, 1)
                body(j * 2 + 2, 0)
            body(GROUPS - 2, 1)
            body(GROUPS - 1, 0, True)
            add(GROUPS - 1)

        def pe_y(pe):
            nm = norms["second"]
            pe.wait_ge(d_added, 2 + 3 * MD * GROUPS)
            for n in range(2 * TILES):
                i, g = divmod(n, 2)
                if n >= 4:
                    pe.wait_ge(nm["nput"], n - 3)
                for k in range(4):
                    mm = pe.transpose(PS[n % 4][0:rows(i), k * P:(k + 1) * P], y_acc[:, 4 * g + k, tile_cols(i)], ident)
                mm.then_inc(nm["nT"], 1)

        def act_y(act):
            nm = norms["second"]
            for n in range(2 * TILES):
                i, g = divmod(n, 2)
                act.wait_ge(nm["nT"], n + 1)
                act.activation(x_tm[0:rows(i), i, 512 * g:512 * g + 512], PS[n % 4][0:rows(i), :], ACT.Copy)\
                    .then_inc(nm["nput"], 1)

        def sp_phase5(sp):
            sp_out(sp)
            sp_ffn(sp)
            nm = norms["second"]
            sp.wait_ge(h_lo2, 6 * GROUPS)
            sp.wait_ge(d_ps, 3 * MD * (GROUPS + 1))
            sp.dma_start(gain, ln2_g[0].partition_broadcast(P)).then_inc(nm["gb_in"], 16)
            sp.dma_start(bias_, ln2_b[0].partition_broadcast(P)).then_inc(nm["gb_in"], 16)
            for i in range(TILES):
                sp.wait_ge(nm["normed"], i + 1)
                dst = y_prompt[0, i * P:(i + 1) * P, :] if i < LAST else y_sample.rearrange("b t d -> (b t) d")
                sp.dma_start(dst, x_tm[0:rows(i), i, :]).then_inc(y_stored, 16)
            sp.wait_ge(y_stored, 16 * TILES)

        def pe_phase5(pe):
            pe.wait_ge(gated, MH)
            pe.sem_inc(gu_ps, 6)
            pe.sem_inc(d_ps, 3 * MD)
            pe_out(pe)
            pe_x1(pe)
            pe_ffn(pe)
            pe_y(pe)

        def act_phase5(act):
            act_out(act)
            act_std(act, norms["first"])
            act_x1(act)
            act_ffn(act)
            act_y(act)
            act_std(act, norms["second"])

        def dve_phase5(dve):
            dve.sem_inc(h_made, 3)
            dve.sem_inc(d_added, 2)
            dve.sem_inc(g_lo, 1)
            dve.sem_inc(wd_lo, 1)
            dve_out(dve)
            dve_norm(dve, norms["first"], lambda i: dve.wait_ge(added, 2 + 3 * MD))
            dve_x1(dve)
            dve_ffn(dve)
            dve_norm(dve, norms["second"], lambda i: dve.wait_ge(norms["second"]["nput"], 2 * i + 2))

        def sp_rest(sp):
            sp_attention(sp)
            sp_samples(sp)
            sp_mlstm(sp)
            sp_phase5(sp)

        def pe_rest(pe):
            pe_attention(pe)
            pe_samples(pe)
            pe_rows(pe)
            pe_mlstm(pe)
            pe_phase5(pe)

        def act_rest(act):
            act_attention(act)
            act_samples(act)
            act_rows(act)
            act_mlstm(act)
            act_phase5(act)

        def pool_rest(pool):
            pool_mlstm(pool)
            pool_norm(pool, norms["first"])
            pool_norm(pool, norms["second"])

        def dve_rest(dve):
            dve_attention(dve)
            dve_samples(dve)
            dve_rows(dve)
            dve_mlstm(dve)
            dve_phase5(dve)

        block = ctx.enter_context(nc.Block())

        @block.sync
        def _(sp):
            sp.dma_start(sq, c_square).then_inc(square_in, 16)

            def load_x(i):
                if i >= 3:
                    sp.wait_ge(filled, pos["xT", i - 3, 1] + 1)
                src = x_prompt[0, i * P:(i + 1) * P, :] if i < LAST else x_sample.rearrange("b t d -> (b t) d")
                sp.dma_start(xin[0:rows(i), i % 3, :], src).then_inc(x_in[i % 3], 16)

            def load_w(g):
                s = big.index(g)
                if s >= 2:
                    before = max(n for n, j in enumerate(jobs) if j[0] in ("tm", "fm") and j[1] == big[s - 2])
                    sp.wait_ge(filled, before + 1)
                src = w_in[0, :, col[g]:col[g] + 512].rearrange("(k p) n -> p k n", p=P)
                for k in range(0, KD, 4):
                    sp.dma_start(wslot[:, s % 2, k:k + 4, :], src[:, k:k + 4, :]).then_inc(w_in_s[s % 2], 16)

            for i in range(3):
                load_x(i)
            load_w("iq")
            for i in range(3, TILES):
                load_x(i)
            sp.dma_start(rope, c_rope).then_inc(const_in, 16)
            sp.dma_start(small, c_small).then_inc(const_in, 16)
            sp.dma_start(crow[0:MH, :], c_rows).then_inc(const_in, 16)
            sp.dma_start(ptab[:, :], page_table.rearrange("(a b) n -> a (b n)", a=1)).then_inc(const_in, 16)
            sp.dma_start(gate_b[0:MH, :], b_gate[0, :].rearrange("(w h) -> h w", w=2),
                         allow_slow_non_contiguous=True).then_inc(const_in, 16)
            win = w_in[0].rearrange("(k p) n -> p k n", p=P)
            sp.dma_start(wsm[:, :, 0:NSM], win[:, :, IK:IK + NSM]).then_inc(wsm_in, 16)
            sp.dma_start(wsm[:, :, NSM:80], win[:, :, MI:MI + 8]).then_inc(wsm_in, 16)
            load_w("ak")
            sp.wait_ge(const_in, 16 * 5)
            with sp.Fori(0, NB * PAGES) as j:
                page = sp.value_load(ptab[0:1, bass.ds(j, 1)], min_val=0, max_val=cache_kidx.shape[1] - 1)
                for twin in range(2):
                    sp.dma_start(mkT_flat[:, bass.ds(j * P + twin * IDX_D, IDX_D)],
                                 cache_kidx[0, bass.ds(page, 1)].rearrange("a p n -> (a p) n")).then_inc(kix_in, 16)

            def store(g, i):
                j = ("tm", g, i)
                s = stage_no[j] % STG
                if g in ("ak", "ik"):
                    sp.wait_ge(roped, rope_no[j] + 1)
                else:
                    sp.wait_ge(freed, pos[j] + 1)
                smp, prm, w = dict(ak=(k_sample, k_prompt, AW), av=(v_sample, v_prompt, AW),
                                   ik=(kidx_sample, kidx_prompt, IDX_D), mv=(None, None, 512))[g]
                if g == "mv":
                    dst = mv_dram[i * P:i * P + rows(i), :]
                elif i == LAST:
                    dst = smp[0].rearrange("b t h n -> (b t) (h n)") if g != "ik" else smp[0].rearrange("b t n -> (b t) n")
                else:
                    dst = prm[0, 0, i * P:(i + 1) * P]
                    if g != "ik":
                        dst = dst.rearrange("t h n -> t (h n)")
                sp.dma_start(dst, stage[0:rows(i), s, 0:w]).then_inc(stored[s], 16)

            for i in range(TILES):
                store("ik", i)
            sp.dma_start(iw_dram, iw[0:SMP, LAST, :]).then_inc(wcol_in, 16)
            sp.wait_ge(wcol_in, 16)
            for b in range(NB):
                sp.dma_start(wcol[32 * (b % 4):32 * (b % 4) + 32, b // 4:b // 4 + 1],
                             iw_dram[NT * b:NT * b + NT, :].rearrange("t h -> h t"),
                             allow_slow_non_contiguous=True).then_inc(wcol_in, 16)
            for i in range(TILES):
                store("ak", i)
            load_w("aq")
            load_w("av")
            for i in range(TILES):
                store("av", i)
            load_w("mv")
            load_w("mk")
            for i in range(TILES):
                store("mv", i)
            load_w("mq")
            load_w("mo")
            for s in range(STG):
                sp.wait_ge(stored[s], 16 * seen[s])
            sp_rest(sp)

        @block.tensor
        def _(pe):
            pe.wait_ge(square_in, 16)
            for n, job in enumerate(jobs):
                kind = job[0]
                bank = PS[n % RING]
                if n >= RING:
                    pe.wait_ge(freed, n - RING + 1)
                if kind == "xT":
                    _, i, j = job
                    r = rows(i)
                    if j == 0:
                        pe.wait_ge(x_in[i % 3], 16 * (i // 3 + 1))
                    for k in range(4):
                        mm = pe.transpose(bank[:, k * P:k * P + r], xin[0:r, i % 3, (4 * j + k) * P:(4 * j + k + 1) * P],
                                          ident[0:r, 0:r])
                elif kind == "tm":
                    _, g, i = job
                    if g == "ik":
                        pe.wait_ge(wsm_in, 32)
                        w, wd = wsm, NSM
                    else:
                        s = big.index(g)
                        pe.wait_ge(w_in_s[s % 2], 32 * (s // 2 + 1))
                        w, wd = wslot[:, s % 2], 512
                    pe.wait_ge(freed, pos["xT", i, 1] + 1)
                    for k in range(KD):
                        mm = pe.matmul(bank[0:rows(i), 0:wd], xT[:, k, tile_cols(i)], w[:, k, 0:wd],
                                       start=(k == 0), stop=(k == KD - 1))
                elif kind == "tr":
                    _, g, i = job
                    r = rows(i)
                    pe.wait_ge(roped, rope_no["tm", g, i] + 1)
                    s = stage_no["tm", g, i] % STG
                    for k in range(1 if g == "ik" else 4):
                        mm = pe.transpose(bank[:, k * P:k * P + r], stage[0:r, s, k * P:(k + 1) * P], ident[0:r, 0:r])
                elif kind == "idx":
                    _, i, h, c = job
                    wd = min(512, widths[i] - 512 * c)
                    if h == 0 and c == 0:
                        pe.wait_ge(freed, pos["tr", "ik", i] + 1)
                    lo = 64 * (h % 2)
                    mm = pe.matmul(bank[:, 0:wd], iqT[lo:lo + 64, h // 2, tile_cols(i)],
                                   kiT[lo:lo + 64, 512 * c:512 * c + wd], start=True, stop=True)
                elif kind == "kxT":
                    _, q = job
                    if q == 0:
                        pe.wait_ge(kix_in, 2 * 16 * NB * PAGES)
                    for j in range(4):
                        mm = pe.transpose(bank[:, j * P:(j + 1) * P], kix[:, 4 * q + j, :], ident)
                elif kind == "idxd":
                    _, g = job
                    pe.wait_ge(freed, pos["kxT", 3] + 1)
                    for b4 in range(4):
                        b = 4 * g + b4
                        o = bank[32 * b4:32 * b4 + 32]
                        for q in range(4):
                            mm = pe.matmul(o[:, 0:PAST], qbd[:, q, b, :],
                                           kixT[:, PAGES * b:PAGES * b + PAGES, :].rearrange("p j n -> p (j n)"),
                                           start=(q == 0), stop=(q == 3), tile_position=(0, 32 * b4))
                        for q in range(4):
                            mm = pe.matmul(o[:, PAST:SC_W], qbd[:, q, b, :], kiT[:, SEQ:T],
                                           start=(q == 0), stop=(q == 3), tile_position=(0, 32 * b4))
                elif kind == "scd":
                    pe.wait_ge(freed, pos["idxd", 1] + 1)
                    pe.wait_ge(wsel_done, 2)
                    for g in range(2):
                        mm = pe.matmul(bank[0:SMP, 0:SC_W], wsel[:, g, :], relud[:, g, :], start=(g == 0), stop=(g == 1))
                elif kind == "fm":
                    _, g, m, c = job
                    s = big.index(g)
                    pe.wait_ge(w_in_s[s % 2], 32 * (s // 2 + 1))
                    for k in range(KD):
                        mm = pe.matmul(bank[:, 0:CH], wslot[:, s % 2, k, m * P:(m + 1) * P],
                                       xT[:, k, c * CH:(c + 1) * CH], start=(k == 0), stop=(k == KD - 1))
                elif kind == "gate":
                    _, w, c = job
                    for k in range(KD):
                        mm = pe.matmul(bank[0:MH, 0:CH], wsm[:, k, NSM + 4 * w:NSM + 4 * w + 4],
                                       xT[:, k, c * CH:(c + 1) * CH], start=(k == 0), stop=(k == KD - 1))
                mm.then_inc(filled, 1)
            pe_rest(pe)

        @block.scalar
        def _(act):
            for n, job in enumerate(jobs):
                kind = job[0]
                bank = PS[n % RING]
                if kind == "tm":
                    _, g, i = job
                    s = stage_no[job]
                    if s >= STG:
                        last = staged[s - STG]
                        if last[1] in ("iq", "ik", "ak", "aq"):
                            act.wait_ge(filled, pos["tr", last[1], last[2]] + 1)
                        if last in store_no:
                            act.wait_ge(stored[s % STG], 16 * store_no[last])
                if kind == "idx" and idx_no[job] >= 4:
                    act.wait_ge(scored, idx_no[job] - 3)
                act.wait_ge(filled, n + 1)
                if kind == "xT":
                    _, i, j = job
                    out = act.activation(xT[:, 4 * j:4 * j + 4, tile_cols(i)],
                                         bank[:, :].rearrange("p (k n) -> p k n", k=4)[:, :, 0:rows(i)], ACT.Copy)
                elif kind == "tm":
                    _, g, i = job
                    r, st = rows(i), stage[:, stage_no[job] % STG, :]
                    if g == "ik":
                        act.activation(iw[0:r, i, :], bank[0:r, IDX_D:NSM], ACT.Copy,
                                       scale=float(AH ** -0.5 * IDX_D ** -0.5))
                        act.activation(st[0:r, IDX_D:2 * IDX_D], bank[0:r, 0:IDX_D], ACT.Copy)
                        out = act.activation(st[0:r, 0:IDX_D], bank[0:r, 0:IDX_D], ACT.Copy)
                    else:
                        out = act.activation(st[0:r, :], bank[0:r, :], ACT.Copy)
                elif kind == "tr":
                    _, g, i = job
                    r = rows(i)
                    if g == "ik":
                        out = act.activation(kiT[:, tile_cols(i)], bank[:, 0:r], ACT.Copy)
                    else:
                        dst = turned_into[g]
                        if i == LAST and g in ("iq", "aq"):
                            act.wait_ge(zeroed, 1)
                            if g == "aq":
                                act.wait_ge(filled, pos["idxd", 1] + 1)
                            for h in range(AH):
                                lo = 64 * (h % 2)
                                act.activation(
                                    qbd[lo:lo + 64, h // 2, :, NT * h:NT * h + NT],
                                    bank[lo:lo + 64, (h // 2) * P:(h // 2) * P + SMP].rearrange("p (b t) -> p b t", b=NB),
                                    ACT.Copy)
                        out = act.activation(dst[:, :, tile_cols(i)],
                                             bank[:, :].rearrange("p (k n) -> p k n", k=4)[:, :, 0:r], ACT.Copy)
                elif kind == "idx":
                    _, i, h, c = job
                    wd = min(512, widths[i] - 512 * c)
                    out = act.activation(relu[:, idx_no[job] % 4, 0:wd], bank[:, 0:wd], ACT.Relu)
                elif kind == "kxT":
                    _, q = job
                    out = act.activation(kixT[:, 4 * q:4 * q + 4, :],
                                         bank[:, :].rearrange("p (k n) -> p k n", k=4), ACT.Copy)
                elif kind == "idxd":
                    if job[1] == 0:
                        act.wait_ge(scored, len(idx_jobs))
                    out = act.activation(relud[:, job[1], :], bank[:, 0:SC_W], ACT.Relu)
                elif kind == "scd":
                    out = act.activation(scd[0:SMP, :], bank[0:SMP, 0:SC_W], ACT.Copy)
                elif kind == "fm":
                    _, g, m, c = job
                    cols = slice(c * CH, (c + 1) * CH)
                    if g == "mq":
                        out = act.activation(mixT[:, m, cols], bank[:, 0:CH], ACT.Copy)
                    elif g == "mk":
                        out = act.activation(mkT[:, m, cols], bank[:, 0:CH], ACT.Copy, scale=float(P ** -0.5))
                    else:
                        out = act.activation(moT[:, m, cols], bank[:, 0:CH], ACT.Sigmoid)
                elif kind == "gate":
                    _, w, c = job
                    if w == 0 and c == 0:
                        act.wait_ge(const_in, 16 * 5)
                    out = act.activation(gates[0:MH, w, c * CH:(c + 1) * CH], bank[0:MH, 0:CH], ACT.Identity,
                                         bias=gate_b[0:MH, w:w + 1])
                out.then_inc(freed, 1)
            act_rest(act)

        @block.gpsimd
        def _(pool):
            pool.memset(qbd, 0.0).then_inc(zeroed, 1)
            pool.wait_ge(const_in, 16 * 5)
            steps = 0

            def rope_tile(job):
                nonlocal steps
                _, g, i = job
                r, hn = rows(i), 2 if g == "ik" else AH
                s = stage[0:r, stage_no[job] % STG, 0:hn * AD].rearrange("p (h n) -> p h n", h=hn)
                t = ropet[0:r, 0:hn * 32].rearrange("p (h n) -> p h n", h=hn)
                cos = rope[0:r, i, 0, :].unsqueeze(1).to_broadcast([r, hn, 16])
                sin = rope[0:r, i, 1, :].unsqueeze(1).to_broadcast([r, hn, 16])
                pool.wait_ge(freed, pos[job] + 1)
                if steps:
                    pool.wait_ge(roped, steps)
                pool.tensor_tensor(t[:, :, 0:16], s[:, :, 0:16], cos, ALU.mult)
                pool.tensor_tensor(t[:, :, 16:24], s[:, :, 8:16], sin[:, :, 0:8], ALU.mult)
                pool.tensor_tensor(t[:, :, 24:32], s[:, :, 0:8], sin[:, :, 8:16], ALU.mult).then_inc(rope_step, 1)
                pool.wait_ge(rope_step, steps + 1)
                pool.tensor_tensor(s[:, :, 0:16], t[:, :, 0:16], t[:, :, 16:32], ALU.add).then_inc(roped, 1)
                steps += 1

            for job in rope_jobs:
                rope_tile(job)
                if job == ("tm", "ik", LAST):
                    pool.wait_ge(wcol_in, 16 * (NB + 1))
                    for g in range(2):
                        pool.tensor_scalar(wsel[:, g, :], wsel_mask[:, g, :], wcol[:, g:g + 1], None, ALU.mult)\
                            .then_inc(wsel_done, 1)
            pool_rest(pool)

        @block.vector
        def _(dve):
            dve.wait_ge(square_in, 16)
            dve.wait_ge(const_in, 16 * 5)
            for job in idx_jobs:
                _, i, h, c = job
                r = idx_no[job]
                wd = min(512, widths[i] - 512 * c)
                cols = slice(512 * c, 512 * c + wd)
                dve.wait_ge(freed, pos[job] + 1)
                src = relu[:, r % 4, 0:wd]
                w = iw[:, i, h:h + 1]
                if h == 0:
                    dve.tensor_scalar(score[i][:, cols], src, w, None, ALU.mult).then_inc(scored, 1)
                else:
                    dve.wait_ge(scored, idx_no["idx", i, h - 1, c] + 1)
                    dve.scalar_tensor_tensor(out=score[i][:, cols], in0=src, scalar=w, in1=score[i][:, cols],
                                             op0=ALU.mult, op1=ALU.add).then_inc(scored, 1)
                if h == AH - 1 and 512 * c + wd == widths[i]:
                    dve.wait_ge(scored, r + 1)
                    diag = score[i][:, widths[i] - P:widths[i]]
                    dve.tensor_tensor(diag, diag, causal, ALU.add).then_inc(causal_done, 1)
            step = 0
            for a in range(FIRST_SPARSE, TILES - 1, 2):
                if step == 0:
                    dve.wait_ge(causal_done, n_sparse)
                with dve.Fori(0, TOPK // 8) as rnd:
                    for u in range(2):
                        dve.max(m8[:, 8 * u:8 * u + 8], score[a + u]).then_inc(topk_step, 1)
                    for u in range(2):
                        dve.wait_ge(topk_step, rnd * 4 + (step + 1 + u))
                        dve.sem_inc(topk_turn, 1)
                        dve.match_replace(score[a + u], m8[:, 8 * u:8 * u + 8], score[a + u], TAKEN)\
                            .then_inc(topk_step, 1)
                    dve.wait_ge(topk_step, rnd * 4 + (step + 4))
                step += 4 * (TOPK // 8)
            for i in range(FIRST_SPARSE, TILES - 1):
                dve.tensor_scalar(score[i], score[i], -2e38, NEG, ALU.is_gt, ALU.mult).then_inc(masks_done, 1)
            dve.wait_ge(freed, pos["scd",] + 1)
            sd, m8d = scd[0:SMP, :], m8[0:SMP, 16:24]
            dve.memset(m8[0:SMP, 24:32], TAKEN).then_inc(topk_step, 1)
            dve.tensor_tensor(sd[:, PAST:SC_W], sd[:, PAST:SC_W], new_mask, ALU.add).then_inc(topk_step, 1)
            step += 2
            dve.wait_ge(topk_step, step)
            with dve.Fori(0, TOPK_S // 8) as rnd:
                dve.max(m8d, sd).then_inc(topk_step, 1)
                dve.wait_ge(topk_step, rnd * 2 + (step + 1))
                dve.sem_inc(topk_turn, 1)
                dve.match_replace(sd, m8d, sd, TAKEN).then_inc(topk_step, 1)
                dve.wait_ge(topk_step, rnd * 2 + (step + 2))
            step += 2 * (TOPK_S // 8)
            dve.max(m8d, sd).then_inc(topk_step, 1)
            dve.wait_ge(topk_step, step + 1)
            dve.tensor_copy(m8[0:SMP, 24:25], m8d[:, 0:1]).then_inc(topk_step, 1)
            dve.wait_ge(topk_step, step + 2)
            dve.match_replace(sd, m8[0:SMP, 24:32], sd, TAKEN).then_inc(topk_step, 1)
            dve.wait_ge(topk_step, step + 3)
            dve.tensor_scalar(sd, sd, -2e38, NEG, ALU.is_gt, ALU.mult).then_inc(masks_done, 1)
            dve_rest(dve)


_INS = ['x_prompt', 'x_sample', 'cache_k', 'cache_v', 'cache_kidx', 'state_C', 'state_n', 'state_m', 'page_table',
        'w_in', 'b_gate', 'w_out', 'ln1_g', 'ln1_b', 'w_gate', 'w_up', 'w_down', 'ln2_g', 'ln2_b']
_OUTS = [(1, SEQ, D), (NB, NT, D), (1, 1, SEQ, AH, AD), (1, 1, SEQ, AH, AD), (1, 1, SEQ, IDX_D),
         (1, 1, MH, P, P), (1, 1, MH, P), (1, 1, MH),
         (1, NB, NT, AH, AD), (1, NB, NT, AH, AD), (1, NB, NT, IDX_D), (1, NB, MH, P, P), (1, NB, MH, P), (1, NB, MH)]
_SCRATCH = [(T, 512), (SMP, AH)]


def shape_constants():
    import numpy as np
    f = np.float32
    r = np.arange(P)
    square = np.zeros((P, 6, P), f)
    square[:, 0] = np.eye(P)
    square[:, 1] = np.where(r[None, :] <= r[:, None], 0, NEG)
    square[:, 2] = np.where(r[:, None] <= r[None, :], 0, NEG)
    square[:, 3] = 1
    bt = np.arange(SMP)
    for g in range(2):
        square[bt, 4 + g] = ((bt // NT)[:, None] == 4 * g + (r // 32)[None, :]) & ((bt % NT)[:, None] == (r % NT)[None, :])
    half = AD // 4 // 2
    pos = np.zeros((TILES, P), f)
    pos[:LAST] = np.arange(SEQ).reshape(LAST, P)
    pos[LAST] = PAST + r % NT
    inv = f(500000.0) ** (-(np.arange(half, dtype=f) / f(half)))
    ang = pos[:, :, None] * inv
    cos, sin = np.cos(ang), np.sin(ang)
    rope = np.stack([np.concatenate([cos, cos], -1), np.concatenate([-sin, sin], -1)], 2)
    small = np.zeros((P, 64 + 2 * SMP), f)
    small[:, 0:64] = square[0:SMP, 4:6].transpose(2, 1, 0).reshape(P, 64)
    own = ((bt // NT)[:, None] == (bt // NT)[None, :]) & (bt[None, :] <= bt[:, None])
    small[0:SMP, 64:96] = np.where(own, 0, NEG)
    small[0:SMP, 96:128] = np.where(own.T, 0, NEG)
    first = np.ones(T, f)
    first[0:SEQ:P] = 0
    first[SEQ:T:NT] = 0
    rows_ = np.concatenate([np.tile(first, (MH, 1)), np.repeat(np.eye(MH, dtype=f), P, axis=1)], 1)
    return [square.reshape(P, -1), np.ascontiguousarray(rope.transpose(1, 0, 2, 3)).reshape(P, -1), small,
            rows_.astype(f)]


def kernel(**inputs):
    import numpy as _np
    import concourse.bacc as _bacc
    from concourse import mybir as _mybir
    from concourse.bass_utils import run_bass_kernel_spmd as _run

    nc = _bacc.Bacc("TRN2", target_bir_lowering=False, num_devices=1)
    arrays, args = {}, []
    given = [(name, _np.ascontiguousarray(inputs[name])) for name in _INS]
    given += [(f"shape_constant_{n}", _np.ascontiguousarray(a)) for n, a in enumerate(shape_constants())]
    for name, a in given:
        arrays[f"in_{name}_dram"] = a
        args.append(nc.dram_tensor(f"in_{name}_dram", a.shape, _mybir.dt.from_np(a.dtype), kind="ExternalInput").ap())
    for i, shape in enumerate(_OUTS):
        args.append(nc.dram_tensor(f"out_{i}_dram", shape, F32, kind="ExternalOutput").ap())
    for i, shape in enumerate(_SCRATCH):
        args.append(nc.dram_tensor(f"scratch_{i}_dram", shape, F32, kind="Internal").ap())
    build(nc, *args)
    r = _run(nc, [arrays], core_ids=[0])
    return tuple(r.results[0][f"out_{i}_dram"] for i in range(len(_OUTS)))
```

```python
import concourse.bass as bass
from concourse import mybir
from contextlib import ExitStack

F32 = mybir.dt.float32
F32R = mybir.dt.float32r
I32 = mybir.dt.int32
ALU = mybir.AluOpType
ACT = mybir.ActivationFunctionType

P = 128
D = 1024
KD = D // P
SEQ = 1024
NB, NT = 8, 4
SMP = NB * NT
T = SEQ + SMP
TILES = SEQ // P + 1
LAST = TILES - 1
CH = T // 3
MH = 4
AH, AD = 8, 64
AW = AH * AD
PAGES = 2
PAST = PAGES * P
SC_W = PAST + SMP
TOPK, TOPK_S = 256, (PAST + NT) // 4
FF = 2816
MF = FF // P
ALPHA = 2 ** 0.25
EPS = 1e-5
NEG = -1e30
TAKEN = -3e38
MQ, MK, MV, MO, MI, AQ, AK, AV, IQ, IK = 0, 512, 1024, 1536, 2048, 2056, 2568, 3080, 3592, 4104
IDX_D = 64
NSM = IDX_D + AH
RING = 6
ARENA = 52600
STG, FST, HALF = 8, 6, 256
FIRST_SPARSE = TOPK // P


def rows(i):
    return SMP if i == LAST else P


def build(nc, x_prompt, x_sample, cache_k, cache_v, cache_kidx, state_C, state_n, state_m, page_table,
          w_in, b_gate, w_out, ln1_g, ln1_b, w_gate, w_up, w_down, ln2_g, ln2_b,
          c_square, c_rope, c_small, c_rows,
          y_prompt, y_sample, k_prompt, v_prompt, kidx_prompt, C_prompt, n_prompt, m_prompt,
          k_sample, v_sample, kidx_sample, C_sample, n_sample, m_sample,
          mv_dram, iw_dram, fm_dram):
    ctx = ExitStack()
    with ctx:
        def sem(name):
            return ctx.enter_context(nc.semaphore(name))

        arena_base = -(-nc.sbuf_base // 32) * 32
        ctx.enter_context(nc.sbuf_tensor("arena", [P, ARENA], F32))
        top = [0]

        def put(name, word, n, dt=F32):
            return nc.alloc_sbuf_tensor_at(name, [P, n], dt, offset=arena_base + 4 * word)[:, :]

        def take(n, name="buffer"):
            word = -(-top[0] // 8) * 8
            top[0] = word + n
            assert top[0] <= ARENA, top[0]
            return put(name, word, n)

        sq = take(6 * P, "square").rearrange("p (c n) -> p c n", n=P)
        ident, causal, causal_t, ones = (sq[:, c, :] for c in range(4))
        expand = sq[0:SMP, 4:6, :]
        rope = take(TILES * 32, "rope").rearrange("p (i c n) -> p i c n", c=2, n=16)
        small = take(64 + SMP * 2, "small")
        wsel_mask = small[:, 0:64].rearrange("p (g n) -> p g n", g=2)
        new_mask, new_mask_t = small[0:SMP, 64:96], small[0:SMP, 96:128]
        crow = take(T + MH * P, "rows_const")
        not_first = crow[0:MH, 0:T]
        head_row = crow[0:MH, T:T + MH * P].rearrange("q (h n) -> q h n", h=MH)
        iw = take(TILES * AH, "index_weights").rearrange("p (i h) -> p i h", h=AH)
        wcol = take(2, "sample_index_weights")
        wsel = take(2 * SMP, "sample_index_select").rearrange("p (g n) -> p g n", g=2)
        gate_b = take(2, "gate_bias")
        ptab = ctx.enter_context(nc.sbuf_tensor("ptab", [1, NB * PAGES], I32))
        m8 = take(32, "eight_largest")
        scd = take(SC_W, "sample_scores")
        qbd = take(NB * 4 * SMP, "sample_queries").rearrange("p (q b n) -> p q b n", q=4, b=NB)
        gates = take(2 * T, "gates").rearrange("p (w t) -> p w t", w=2)
        mixT = take(8 * T, "mixT").rearrange("p (k t) -> p k t", t=T)
        mixT_at = top[0] - 8 * T
        qT = mixT[:, 4:8, :]
        kT_flat = take(4 * T, "kT")
        kT_at = top[0] - 4 * T
        kT = kT_flat.rearrange("p (k t) -> p k t", t=T)
        mkT_flat = take(4 * T, "mkT")
        mkT_at = top[0] - 4 * T
        mkT = mkT_flat.rearrange("p (k t) -> p k t", t=T)
        iqT = take(4 * T, "iqT").rearrange("p (k t) -> p k t", t=T)
        iqT_at = top[0] - 4 * T
        moT = iqT
        kiT = take(T, "kiT")
        kiT_at = top[0] - T
        widths = [(i + 1) * P for i in range(TILES - 1)]
        score_flat = take(sum(widths[FIRST_SPARSE:]), "scores")
        score_at = top[0] - sum(widths[FIRST_SPARSE:])
        score, at = {}, 0
        for i in range(FIRST_SPARSE, TILES - 1):
            score[i] = score_flat[:, at:at + widths[i]]
            at += widths[i]
        stage_flat = take(STG * HALF, "stage")
        stage_at = top[0] - STG * HALF
        stage = stage_flat.rearrange("p (s n) -> p s n", s=STG)
        ropet = take(AH // 2 * 32, "rope_products")
        work0 = -(-top[0] // 8) * 8
        top[0] = work0
        PARTS = [(0, 0), (0, 1), (1, 0)]
        XS0 = (ARENA - 2 * KD * T) // 8 * 8
        assert work0 + 16 * KD <= XS0
        xs1 = put("xT_split", XS0, 2 * KD * T, F32R).rearrange("p (s k t) -> p s k t", s=2, k=KD)
        wsplit = [put(f"w_split{u}", at, 2 * KD * HALF, F32R).rearrange("p (s k n) -> p s k n", s=2, k=KD)
                  for u, at in enumerate((mixT_at, mkT_at))]
        wraw = [put(f"w_unit{u}", at, KD * HALF).rearrange("p (k n) -> p k n", k=KD)
                for u, at in enumerate((kT_at + 2048, iqT_at))]
        wsm = put("w_small", kT_at, KD * 80).rearrange("p (k n) -> p k n", k=KD)
        wsm_s = put("w_small_split", kT_at + KD * 80, 2 * KD * NSM, F32R).rearrange("p (s k n) -> p s k n", s=2, k=KD)
        wgate_s = put("w_gates_split", work0, 2 * KD * 8, F32R).rearrange("p (s k n) -> p s k n", s=2, k=KD)
        fstage = put("feature_stage", iqT_at + 2048, FST * CH).rearrange("p (s n) -> p s n", s=FST)
        xin = score_flat[:, 0:3 * D].rearrange("p (s n) -> p s n", s=3)
        kix = put("index_pages", mixT_at + 4 * T, 2048).rearrange("p (j n) -> p j n", n=P)
        kix_flat = kix.rearrange("p j n -> p (j n)")
        kixT = put("index_pages_turned", mixT_at + 4 * T + 2048, 2048).rearrange("p (j n) -> p j n", n=P)
        relu = kT_flat[:, 0:4 * 512].rearrange("p (s n) -> p s n", s=4)
        relud = relu[:, 0:2, 0:SC_W]
        top[0] = work0
        v_tm = take(TILES * AW, "v").rearrange("p (i n) -> p i n", n=AW)
        mv_tm = take(TILES * 512, "mv").rearrange("p (i n) -> p i n", n=512)
        work1 = top[0]

        PS = [ctx.enter_context(nc.psum_tensor(f"bank{i}", [P, 512], F32)) for i in range(8)]

        square_in = sem("square_in")
        const_in = sem("const_in")
        x_in = [sem(f"x_in{s}") for s in range(3)]
        x_low = sem("x_low")
        w_in_s, w_hi, w_lo = sem("w_in"), sem("w_hi"), sem("w_lo")
        wsm_in, wsm_hi, wsm_lo = sem("wsm_in"), sem("wsm_hi"), sem("wsm_lo")
        fstored = [sem(f"fstored{s}") for s in range(FST)]
        kix_in = sem("kix_in")
        wcol_in = sem("wcol_in")
        filled, freed = sem("filled"), sem("freed")
        roped, rope_step = sem("roped"), sem("rope_step")
        stored = [sem(f"stored{s}") for s in range(STG)]
        scored = sem("scored")
        causal_done = sem("causal_done")
        topk_step, topk_turn = sem("topk_step"), sem("topk_turn")
        zeroed = sem("zeroed")
        wsel_done = sem("wsel_done")
        masks_done = sem("masks_done")

        big = ["iq", "ak", "aq", "av", "mv", "mk", "mq", "mo"]
        col = dict(iq=IQ, ak=AK, aq=AQ, av=AV, mv=MV, mk=MK, mq=MQ, mo=MO)
        units = [(g, u) for g in big for u in range(2)]
        unit_no = {unit: n for n, unit in enumerate(units)}
        def tm_jobs(g, u, turned):
            out = []
            for i in range(TILES):
                out.append(("tm", g, u, i))
                if turned and i >= 2:
                    out.append(("tr", g, u, i - 2))
            return out + ([("tr", g, u, TILES - 2), ("tr", g, u, TILES - 1)] if turned else [])

        jobs, first_unit = [], tm_jobs("iq", 0, True)
        for i in range(TILES):
            jobs += [("xT", i, 0), ("xT", i, 1)]
            if i >= 2:
                jobs += first_unit[:2]
                first_unit = first_unit[2:]
        jobs += first_unit + tm_jobs("iq", 1, True)
        jobs += [("ikf", c) for c in range(3)] + tm_jobs("ik", 0, True)
        for i in range(FIRST_SPARSE, TILES - 1):
            jobs += [("idx", i, h, c) for h in range(AH) for c in range(-(-widths[i] // 512))]
        jobs += [("kxT", q) for q in range(4)] + [("idxd", g) for g in range(2)] + [("scd",)]
        for g in ("ak", "aq", "av", "mv"):
            jobs += tm_jobs(g, 0, g in ("ak", "aq")) + tm_jobs(g, 1, g in ("ak", "aq"))
        jobs += [("gate", w, c) for w in range(2) for c in range(3)]
        for g in ("mk", "mq", "mo"):
            jobs += [("fm", g, m, c) for m in range(4) for c in range(3)]
        pos = {job: n for n, job in enumerate(jobs)}
        fm_no = {job: n for n, job in enumerate(j for j in jobs if j[0] == "fm")}
        unit_end = {}
        for n, j in enumerate(jobs):
            if j[0] == "tm" and j[1] != "ik":
                unit_end[unit_no[j[1], j[2]]] = n
            elif j[0] == "fm":
                unit_end[unit_no[j[1], j[2] // 2]] = n
        staged = [j for j in jobs if j[0] == "tm"]
        stage_no = {j: s for s, j in enumerate(staged)}
        rope_jobs = [j for j in staged if j[1] in ("iq", "ik", "ak", "aq")]
        rope_no = {j: r for r, j in enumerate(rope_jobs)}
        store_jobs = [j for j in staged if j[1] in ("ik", "ak", "av", "mv")]
        store_no, seen = {}, [0] * STG
        for j in store_jobs:
            seen[stage_no[j] % STG] += 1
            store_no[j] = seen[stage_no[j] % STG]
        idx_jobs = [j for j in jobs if j[0] == "idx"]
        idx_no = {j: r for r, j in enumerate(idx_jobs)}
        turned_into = dict(iq=iqT, ik=kiT, ak=kT, aq=qT)

        def tile_cols(i):
            return slice(i * P, i * P + rows(i))

        n_sparse = LAST - FIRST_SPARSE
        top[0] = work1
        masked = take(2 * SEQ, "attention_weights").rearrange("p (s n) -> p s n", s=2)
        probT = take(2 * SEQ, "attention_weights_turned").rearrange("p (s j n) -> p s j n", s=2, j=LAST)
        att_out = take(2 * AW, "attention_out").rearrange("p (s n) -> p s n", s=2)
        kraw_at = top[0]
        kraw = take(2 * PAGES * AW, "key_pages").rearrange("p (s j n) -> p s j n", s=2, j=PAGES)
        prob_s = take(SC_W, "sample_weights")
        probT_s = take(3 * P, "sample_weights_turned").rearrange("p (j n) -> p j n", n=P)
        negmax = take(4, "negative_maxima")
        rowsum = take(2 * AH, "row_sums").rearrange("p (s h) -> p s h", s=2)
        rinv = take(2 * AH, "row_sums_inverted").rearrange("p (s h) -> p s h", s=2)
        vpage = [flat[:, 0:4 * PAGES * AW].rearrange("p (b j n) -> p b j n", b=4, j=PAGES)
                 for flat in (score_flat, kT_flat)]
        kpT = masked.rearrange("p s n -> p (s n)")[:, 0:2 * 4 * PAST].rearrange("p (s q n) -> p s q n", s=2, q=4)
        kT_new = put("kT_new", stage_at + 1568, 4 * SMP).rearrange("p (q n) -> p q n", q=4)
        dense01 = stage_flat[:, 0:3 * P]

        steps2 = [(i, h) for i in reversed(range(LAST)) for h in range(AH)]
        order = {i: LAST - 1 - i for i in range(LAST)}
        N2 = len(steps2)
        wide = [0] * (N2 + 1)
        for n, (i, h) in enumerate(steps2):
            wide[n + 1] = wide[n] + (widths[i] > 512)

        WIDE = sum(widths[i] > 512 for i, h in steps2)
        schedule, t = [], 0
        for n in range(N2 + 1):
            while n == WIDE and t < n:
                schedule.append(("turn", t))
                t += 1
            if n < N2:
                schedule.append(("scores", n))
            while t <= (n - (1 if n < WIDE else 3) if n < N2 else N2 + 1):
                schedule.append(("turn", t))
                t += 1

        def steps_before(n):
            return n - 1 if n < WIDE else max(n - 3, WIDE)

        def scores_bank(n, c):
            return PS[2 * (n % 2) + c] if n < WIDE else PS[n % 4]

        def weights_slot(n):
            return masked[:, n % 2, :] if n < WIDE else \
                masked.rearrange("p s n -> p (s n)")[:, 512 * (n % 4):512 * (n % 4) + 512]

        def mask_of(i):
            if i >= FIRST_SPARSE:
                return score[i]
            return dense01[:, 0:P] if i == 0 else dense01[:, P:3 * P]

        v_loaded = sem("v_loaded")
        dense_ready = sem("dense_ready")
        att_scores, att_masked, att_exp = sem("att_scores"), sem("att_masked"), sem("att_exp")
        att_turned, att_left, att_right = sem("att_turned"), sem("att_left"), sem("att_right")
        att_values, att_scaled, att_oT, att_put = sem("att_values"), sem("att_scaled"), sem("att_oT"), sem("att_put")
        neg_step = sem("neg_step")
        turned_before = [0] * (N2 + 1)
        for n, (i, h) in enumerate(steps2):
            turned_before[n + 1] = turned_before[n] + 1 + (widths[i] > 512)

        def pe_attention(pe):
            pe.wait_ge(freed, len(jobs))

            def scores(n):
                i, h = steps2[n]
                lo = 64 * (h % 2)
                if n >= 2:
                    pe.wait_ge(att_masked, steps_before(n))
                for c in range(-(-widths[i] // 512)):
                    wd = min(512, widths[i] - 512 * c)
                    mm = pe.matmul(scores_bank(n, c)[:, 0:wd], qT[lo:lo + 64, h // 2, tile_cols(i)],
                                   kT[lo:lo + 64, h // 2, 512 * c:512 * c + wd], start=True, stop=True)
                mm.then_inc(att_scores, 1)

            def turn(n):
                i, h = steps2[n]
                pe.wait_ge(att_exp, n + 1)
                for c in range(-(-widths[i] // 512)):
                    if c == 0 and n >= 1:
                        pe.wait_ge(att_left, n)
                    if c == 1 and wide[n] >= 1:
                        pe.wait_ge(att_right, wide[n])
                    for j in range(4 * c, min(4 * c + 4, i + 1)):
                        mm = pe.transpose(PS[4 + c][:, (j % 4) * P:(j % 4 + 1) * P],
                                          weights_slot(n)[:, j * P:(j + 1) * P], ident)
                    mm.then_inc(att_turned, 1)

            def values(n):
                i, h = steps2[n]
                if n == 0:
                    pe.wait_ge(v_loaded, 16 * TILES)
                pe.wait_ge(att_left, n + 1)
                if wide[n + 1] > wide[n]:
                    pe.wait_ge(att_right, wide[n + 1])
                if h == 0 and order[i]:
                    pe.wait_ge(att_scaled, order[i])
                for j in range(i + 1):
                    mm = pe.matmul(PS[6][:, h * AD:(h + 1) * AD], probT[:, n % 2, j, :],
                                   v_tm[:, j, h * AD:(h + 1) * AD], start=(j == 0), stop=(j == i))
                mm.then_inc(att_values, 1)

            def out_turn(i):
                o = order[i]
                pe.wait_ge(att_scaled, o + 1)
                if o:
                    pe.wait_ge(att_put, o)
                for k in range(4):
                    mm = pe.transpose(PS[7][:, k * P:(k + 1) * P], att_out[:, o % 2, k * P:(k + 1) * P], ident)
                mm.then_inc(att_oT, 1)

            for what, n in schedule:
                if what == "scores":
                    scores(n)
                    continue
                if n < N2:
                    turn(n)
                if n >= 2 and steps2[n - 2][1] == AH - 1:
                    out_turn(steps2[n - 2][0])
                if 1 <= n <= N2:
                    values(n - 1)

        def dve_attention(dve):
            for s in range(STG):
                dve.wait_ge(stored[s], 16 * seen[s])
            dve.memset(dense01[:, P:2 * P], 0.0).then_inc(dense_ready, 1)
            dve.tensor_copy(dense01[:, 0:P], causal).then_inc(dense_ready, 1)
            dve.tensor_copy(dense01[:, 2 * P:3 * P], causal).then_inc(dense_ready, 1)
            dve.tensor_copy(kT_new, kT[:, :, SEQ:T]).then_inc(dense_ready, 1)
            dve.wait_ge(dense_ready, 4)
            dve.wait_ge(masks_done, n_sparse + 1)
            for what, n in schedule:
                if what == "scores":
                    i, h = steps2[n]
                    dve.wait_ge(att_scores, n + 1)
                    if n >= 2:
                        dve.wait_ge(att_turned, turned_before[steps_before(n)])
                        dve.wait_ge(att_exp, n - 1)
                    nc_ = -(-widths[i] // 512)
                    for c in range(nc_):
                        wd = min(512, widths[i] - 512 * c)
                        dve.tensor_tensor_reduce(weights_slot(n)[:, 512 * c:512 * c + wd], scores_bank(n, c)[:, 0:wd],
                                                 mask_of(i)[:, 512 * c:512 * c + wd], 1.0, -3e38, ALU.add, ALU.max,
                                                 m8[:, c:c + 1]).then_inc(neg_step, 1)
                    base = sum(-(-widths[a] // 512) + 1 for a, _ in steps2[:n])
                    dve.wait_ge(neg_step, base + nc_)
                    if nc_ == 2:
                        dve.scalar_tensor_tensor(out=m8[:, 2:3], in0=m8[:, 0:1], scalar=1.0, in1=m8[:, 1:2],
                                                 op0=ALU.mult, op1=ALU.max).then_inc(neg_step, 1)
                    else:
                        dve.tensor_copy(m8[:, 2:3], m8[:, 0:1]).then_inc(neg_step, 1)
                    dve.wait_ge(neg_step, base + nc_ + 1)
                    dve.tensor_scalar(negmax[:, n % 2:n % 2 + 1], m8[:, 2:3], -(AD ** -0.5), None, ALU.mult)\
                        .then_inc(att_masked, 1)
                    continue
                if n < N2 and wide[n + 1] > wide[n]:
                    i, h = steps2[n]
                    dve.wait_ge(att_turned, turned_before[n + 1])
                    if n >= 2:
                        dve.wait_ge(att_values, n - 1)
                    dve.tensor_copy(probT[:, n % 2, 4:i + 1, :],
                                    PS[5][:, 0:(i - 3) * P].rearrange("p (j n) -> p j n", n=P)).then_inc(att_right, 1)
                if 1 <= n <= N2 and steps2[n - 1][1] == AH - 1:
                    o = order[steps2[n - 1][0]]
                    dve.wait_ge(att_values, n)
                    dve.reciprocal(rinv[:, o % 2, :], rowsum[:, o % 2, :]).then_inc(dense_ready, 1)
                    dve.wait_ge(dense_ready, 5 + o)
                    if o >= 2:
                        dve.wait_ge(att_oT, o - 1)
                    dve.tensor_tensor(att_out[:, o % 2, :].rearrange("p (h n) -> p h n", h=AH),
                                      PS[6][:, :].rearrange("p (h n) -> p h n", h=AH),
                                      rinv[:, o % 2, :].unsqueeze(2).to_broadcast([P, AH, AD]), ALU.mult)\
                        .then_inc(att_scaled, 1)

        def act_attention(act):
            for what, n in schedule:
                if what == "scores":
                    i, h = steps2[n]
                    act.wait_ge(att_masked, n + 1)
                    o = order[i]
                    if h == 0 and o >= 2:
                        act.wait_ge(att_scaled, o - 1)
                    x = weights_slot(n)[:, 0:widths[i]]
                    act.activation(x, x, ACT.Exp, bias=negmax[:, n % 2:n % 2 + 1], scale=float(AD ** -0.5),
                                   accum_out=rowsum[:, o % 2, h:h + 1]).then_inc(att_exp, 1)
                    continue
                if n < N2:
                    i, h = steps2[n]
                    k = min(4, i + 1)
                    act.wait_ge(att_turned, turned_before[n] + 1)
                    if n >= 2:
                        act.wait_ge(att_values, n - 1)
                    act.activation(probT[:, n % 2, 0:k, :],
                                   PS[4][:, 0:k * P].rearrange("p (j n) -> p j n", n=P), ACT.Copy).then_inc(att_left, 1)
                if n >= 2 and steps2[n - 2][1] == AH - 1:
                    i = steps2[n - 2][0]
                    act.wait_ge(att_oT, order[i] + 1)
                    act.activation(qT[:, :, tile_cols(i)], PS[7][:, :].rearrange("p (k n) -> p k n", k=4), ACT.Copy)\
                        .then_inc(att_put, 1)

        def sp_attention(sp):
            sp.wait_ge(filled, len(jobs))
            for i in range(TILES):
                r = rows(i)
                src = v_prompt[0, 0, i * P:(i + 1) * P].rearrange("t h n -> t (h n)") if i < LAST else \
                    v_sample[0].rearrange("b t h n -> (b t) (h n)")
                sp.dma_start(v_tm[0:r, i, :], src).then_inc(v_loaded, 16)
            sp.dma_start(m_prev[0:MH, LAST:LAST + NB], state_m[0].rearrange("b h -> h b"),
                         allow_slow_non_contiguous=True).then_inc(m_in, 16)
            for i in range(TILES):
                sp.dma_start(mv_tm[0:rows(i), i, :], mv_dram[i * P:i * P + rows(i), :]).then_inc(mv_loaded, 16)
            for n, dst in enumerate((mkT, mixT[:, 0:4, :], moT)):
                sp.dma_start(dst, fm_dram[n].rearrange("m p t -> p m t")).then_inc(fm_loaded, 16)

        kpage_in = [sem(f"kpage_in{s}") for s in range(2)]
        vpage_in = [sem(f"vpage_in{g}") for g in range(2)]
        mv_loaded, fm_loaded = sem("mv_loaded"), sem("fm_loaded")
        smp_kT, smp_kput = sem("smp_kT"), sem("smp_kput")
        smp_mask, smp_scores, smp_exp, smp_norm = sem("smp_mask"), sem("smp_scores"), sem("smp_exp"), sem("smp_norm")
        smp_turned, smp_put, smp_values, smp_out = sem("smp_turned"), sem("smp_put"), sem("smp_values"), sem("smp_out")
        smp_step = sem("smp_step")

        def load_page(sp, cache, b, j, dst, done):
            page = sp.value_load(ptab[0:1, b * PAGES + j:b * PAGES + j + 1], min_val=0, max_val=cache.shape[1] - 1)
            sp.dma_start(dst, cache[0, bass.ds(page, 1)].rearrange("a p h n -> (a p) (h n)")).then_inc(done, 16)

        def load_keys(sp, b):
            if b >= 2:
                sp.wait_ge(smp_kT, 2 * (b - 1))
            for j in range(PAGES):
                load_page(sp, cache_k, b, j, kraw[:, b % 2, j, :], kpage_in[b % 2])

        def sp_samples(sp):
            for b in (3, 2, 1, 0, 4, 5, 6, 7):
                if b < 4:
                    i = min(i for i in score if sum(widths[FIRST_SPARSE:i + 1]) > b * PAGES * AW)
                    sp.wait_ge(att_masked, AH * (order[i] + 1))
                elif b == 4:
                    sp.wait_ge(att_scores, N2)
                for j in range(PAGES):
                    load_page(sp, cache_v, b, j, vpage[b // 4][:, b % 4, j, :], vpage_in[b // 4])
                if b >= 4:
                    load_keys(sp, b - 2)
            load_keys(sp, NB - 2)
            load_keys(sp, NB - 1)

        def pe_samples(pe):
            pe.wait_ge(att_masked, N2)
            pe.wait_ge(att_left, N2)
            pe.wait_ge(att_right, wide[N2])
            pe.wait_ge(att_put, LAST)
            for g in range(2):
                S = PS[4 + g]
                pe.wait_ge(masks_done, n_sparse + 1)
                pe.matmul(S[:, 0:SC_W], expand[:, g, :], scd[0:SMP, :], start=True, stop=False, skip_group_check=True)
                for b4 in range(4):
                    b = 4 * g + b4
                    pe.wait_ge(kpage_in[b % 2], 16 * PAGES * (b // 2 + 1))
                    for j in range(PAGES):
                        n = PAGES * b + j
                        if n >= 2:
                            pe.wait_ge(smp_kput, n - 1)
                        for q in range(4):
                            mm = pe.transpose(PS[n % 2][:, q * P:(q + 1) * P], kraw[:, b % 2, j, q * P:(q + 1) * P], ident)
                        mm.then_inc(smp_kT, 1)
                    pe.wait_ge(smp_kput, PAGES * (b + 1))
                    o = S[32 * b4:32 * b4 + 32]
                    for q in range(4):
                        pe.matmul(o[:, 0:PAST], qbd[:, q, b, :], kpT[:, b % 2, q, :], start=False, stop=False,
                                  skip_group_check=True, tile_position=(0, 32 * b4))
                    for q in range(4):
                        mm = pe.matmul(o[:, PAST:SC_W], qbd[:, q, b, :], kT_new[:, q, :], start=False, stop=(q == 3),
                                       skip_group_check=True, tile_position=(0, 32 * b4))
                    mm.then_inc(smp_scores, 1)
                pe.wait_ge(smp_norm, g + 1)
                if g:
                    pe.wait_ge(smp_put, g)
                for j in range(PAGES):
                    pe.transpose(PS[2][:, j * P:(j + 1) * P], prob_s[:, j * P:(j + 1) * P], ident)
                pe.transpose(PS[2][0:SMP, PAGES * P:3 * P], prob_s[:, PAST:SC_W], ident).then_inc(smp_turned, 1)
                pe.wait_ge(smp_put, g + 1)
                pe.wait_ge(vpage_in[g], 16 * PAGES * 4)
                for b4 in range(4):
                    for q in range(4):
                        o = PS[6 + g][:, (4 * b4 + q) * SMP:(4 * b4 + q + 1) * SMP]
                        cols, hp = slice(32 * b4, 32 * b4 + 32), slice(q * P, (q + 1) * P)
                        for j in range(PAGES):
                            pe.matmul(o, vpage[g][:, b4, j, hp], probT_s[:, j, cols], start=(j == 0), stop=False)
                        mm = pe.matmul(o, v_tm[0:SMP, LAST, hp], probT_s[0:SMP, 2, cols], start=False, stop=True)
                    mm.then_inc(smp_values, 1)

        def act_samples(act):
            act.wait_ge(att_turned, turned_before[N2])
            for g in range(2):
                for b4 in range(4):
                    b = 4 * g + b4
                    for j in range(PAGES):
                        act.wait_ge(smp_kT, PAGES * b + j + 1)
                        if b >= 2:
                            act.wait_ge(smp_scores, b - 1)
                        act.activation(kpT[:, b % 2, :, j * P:(j + 1) * P],
                                       PS[(PAGES * b + j) % 2][:, :].rearrange("p (q n) -> p q n", q=4), ACT.Copy)\
                            .then_inc(smp_kput, 1)
                act.wait_ge(smp_mask, g + 1)
                act.activation(prob_s, PS[4 + g][:, 0:SC_W], ACT.Exp, bias=negmax[:, 2:3], scale=float(AD ** -0.5),
                               accum_out=negmax[:, 3:4]).then_inc(smp_exp, 1)
                act.wait_ge(smp_turned, g + 1)
                if g:
                    act.wait_ge(smp_values, 4 * g)
                act.activation(probT_s[:, 0:2, :], PS[2][:, 0:2 * P].rearrange("p (j n) -> p j n", j=2), ACT.Copy)
                act.activation(probT_s[0:SMP, 2, :], PS[2][0:SMP, 2 * P:3 * P], ACT.Copy).then_inc(smp_put, 1)

        def dve_samples(dve):
            for g in range(2):
                dve.wait_ge(smp_scores, 4 * (g + 1))
                if g:
                    dve.wait_ge(smp_exp, g)
                dve.tensor_reduce(m8[:, 0:1], PS[4 + g][:, 0:SC_W], mybir.AxisListType.X, ALU.max).then_inc(smp_step, 1)
                dve.wait_ge(smp_step, 3 * g + 1)
                dve.tensor_scalar(negmax[:, 2:3], m8[:, 0:1], -(AD ** -0.5), None, ALU.mult).then_inc(smp_mask, 1)
                dve.wait_ge(smp_exp, g + 1)
                dve.reciprocal(m8[:, 1:2], negmax[:, 3:4]).then_inc(smp_step, 1)
                dve.wait_ge(smp_step, 3 * g + 2)
                dve.tensor_scalar(prob_s, prob_s, m8[:, 1:2], None, ALU.mult).then_inc(smp_norm, 1)
                dve.wait_ge(smp_values, 4 * (g + 1))
                for h in range(AH):
                    lo = 64 * (h % 2)
                    src = PS[6 + g][lo:lo + 64, :].rearrange("p (b q n) -> p b q n", b=4, q=4)
                    c = dve.tensor_copy(qT[lo:lo + 64, h // 2, SEQ + 16 * g:SEQ + 16 * g + 16]
                                        .rearrange("p (b t) -> p b t", b=4), src[:, :, h // 2, NT * h:NT * h + NT])
                c.then_inc(smp_step, 1)
            dve.wait_ge(smp_step, 6)

        CK = TILES
        top[0] = work1
        qg = take(2 * T, "mq_scaled").rearrange("p (s t) -> p s t", s=2)
        state = take(LAST * 2 * P, "state").rearrange("p (c n) -> p c n", c=LAST)
        hden = take(2 * 4 * P, "denominator").rearrange("p (s n) -> p s n", s=2)
        hnum = take(2 * 4 * P, "numerator").rearrange("p (s n) -> p s n", s=2)
        sets = []
        for word in (kT_at, work0):
            sets.append([put(f"spread_{word}_{r}", word + r * T, T) for r in range(3)])
        st = put("weighted_scores", kT_at + 3 * T, T)
        c_smp = put("c_sample", score_at, 2 * NB * P).rearrange("p (s b n) -> p s b n", s=2, b=NB)
        kw = put("mk_weighted", score_at + 2048, LAST * P).rearrange("p (c n) -> p c n", c=LAST)
        kw_smp = put("mk_weighted_sample", score_at + 3072, NB * P).rearrange("p (b n) -> p b n", b=NB)
        top[0] = work0 + 3 * T
        acol = take(CK * MH, "a_columns").rearrange("p (c h) -> p c h", h=MH)
        qn = take(SMP, "q_times_n")
        n_all = take(NB * MH + MH, "n_columns")
        n_rows = take(P, "n_rows_in")
        n_out = put("n_rows_out", mkT_at, P)
        assert top[0] <= work0 + LAST * AW
        a_row, g_row = gates[0:MH, 0, :], gates[0:MH, 1, :]
        lf, ig = g_row, a_row
        b_row = put("b_row", kiT_at, T)[0:MH, :]
        m_row = put("m_row", stage_at + 512, T)[0:MH, :]
        m_prev = put("m_before", stage_at + 1696 + 16, LAST + NB)
        log_one = put("log_one", stage_at + 1736, 1)

        m_in, nst_in = sem("m_in"), sem("nst_in")
        c_in = [sem(f"c_in{s}") for s in range(2)]
        row_step, row_act = sem("row_step"), sem("row_act")
        mp_zero = sem("mp_zero")
        a_turned, a_put = sem("a_turned"), sem("a_put")
        bc_filled, bc_freed = sem("bc_filled"), sem("bc_freed")
        wt_arg, wt_exp, qg_done, qn_done = sem("wt_arg"), sem("wt_exp"), sem("qg_done"), sem("qn_done")
        st_ps, st_done, kw_done = sem("st_ps"), sem("st_done"), sem("kw_done")
        nd_ps, u_ps, cs_done, h_done = sem("nd_ps"), sem("u_ps"), sem("cs_done"), sem("h_done")
        cs_step, h_step, gated = sem("cs_step"), sem("h_step"), sem("gated")
        den_taken, num_taken, inverted = sem("den_taken"), sem("num_taken"), sem("inverted")
        c_stored = [sem(f"c_stored{s}") for s in range(2)]
        cp_stored, m_stored = sem("cp_stored"), sem("m_stored")
        n_final, n_back, n_out_put, n_stored = sem("n_final"), sem("n_back"), sem("n_out_put"), sem("n_stored")
        ROWS_DONE = 3 + NB + 3

        def sp_rows(sp):
            sp.wait_ge(row_step, 3 + NB)
            sp.dma_start(m_prompt[0, 0, :].rearrange("(h n) -> h n", n=1), m_row[:, SEQ - 1:SEQ]).then_inc(m_stored, 16)
            sp.dma_start(m_sample[0].rearrange("b h -> h b"),
                         m_row[:, SEQ:T].rearrange("h (b t) -> h b t", b=NB)[:, :, NT - 1],
                         allow_slow_non_contiguous=True).then_inc(m_stored, 16)

        def sp_mlstm(sp):
            sp.wait_ge(smp_values, 4)

            def load_c(h):
                sp.dma_start(c_smp[:, h % 2, :, :], state_C[0, :, h].rearrange("b d e -> d b e"))\
                    .then_inc(c_in[h % 2], 16)

            sp.dma_start(n_rows[0:NB * MH, :], state_n[0].rearrange("b h d -> (b h) d")).then_inc(nst_in, 16)
            load_c(0)
            load_c(1)
            for h in range(MH):
                sp.wait_ge(cs_done, 6 * h + 4)
                sp.dma_start(C_prompt[0, 0, h], state[:, LAST - 1, 0:P]).then_inc(cp_stored, 16)
                sp.wait_ge(cs_done, 6 * h + 6)
                sp.dma_start(C_sample[0, :, h].rearrange("b d e -> d b e"), c_smp[:, h % 2, :, :])\
                    .then_inc(c_stored[h % 2], 16)
                if h + 2 < MH:
                    sp.wait_ge(c_stored[h % 2], 16)
                    load_c(h + 2)
            sp.wait_ge(n_out_put, 1)
            sp.dma_start(n_sample[0].rearrange("b h d -> (b h) d"), n_out[0:NB * MH, :]).then_inc(n_stored, 16)
            sp.dma_start(n_prompt[0, 0], n_out[NB * MH:NB * MH + MH, :]).then_inc(n_stored, 16)

        def sp_mlstm_end(sp):
            sp.wait_ge(n_stored, 32)
            sp.wait_ge(m_stored, 32)
            sp.wait_ge(cp_stored, 16 * MH)
            for s in range(2):
                sp.wait_ge(c_stored[s], 32)

        def dve_rows(dve):
            dve.wait_ge(freed, pos["gate", 1, 2] + 1)
            for s in range(STG):
                dve.wait_ge(stored[s], 16 * seen[s])
            dve.memset(m_prev[0:MH, 0:1], 0.0)
            dve.memset(log_one, 1.0).then_inc(mp_zero, 1)
            dve.scalar_tensor_tensor(out=b_row, in0=lf, scalar=-1.0, in1=lf, op0=ALU.mult, op1=ALU.max)\
                .then_inc(row_step, 1)
            dve.wait_ge(row_act, 2)
            dve.scalar_tensor_tensor(out=lf, in0=lf, scalar=0.0, in1=b_row, op0=ALU.min, op1=ALU.subtract)\
                .then_inc(row_step, 1)
            dve.wait_ge(row_step, 2)
            dve.tensor_tensor_scan(b_row, not_first, lf, 0.0, ALU.mult, ALU.add)
            dve.tensor_tensor_scan(m_row[:, 0:SEQ], lf[:, 0:SEQ], ig[:, 0:SEQ], 0.0, ALU.add, ALU.max)\
                .then_inc(row_step, 1)
            dve.wait_ge(m_in, 16)
            for b in range(NB):
                c = slice(SEQ + NT * b, SEQ + NT * b + NT)
                dve.tensor_tensor_scan(m_row[:, c], lf[:, c], ig[:, c], m_prev[0:MH, LAST + b:LAST + b + 1],
                                       ALU.add, ALU.max).then_inc(row_step, 1)
            step = 3 + NB
            dve.wait_ge(row_step, step)
            dve.tensor_copy(m_prev[0:MH, 1:LAST],
                            m_row[:, 0:SEQ].rearrange("h (c t) -> h c t", t=P)[:, 0:LAST - 1, P - 1])
            dve.tensor_tensor(a_row, ig, b_row, ALU.subtract).then_inc(row_step, 1)
            dve.wait_ge(row_step, step + 1)
            dve.tensor_tensor(b_row, b_row, m_row, ALU.subtract).then_inc(row_step, 1)
            dve.wait_ge(row_step, step + 2)
            dve.tensor_tensor(g_row[:, 0:SEQ].rearrange("h (c t) -> h c t", t=P),
                              b_row[:, 0:SEQ].rearrange("h (c t) -> h c t", t=P),
                              m_prev[0:MH, 0:LAST].unsqueeze(2).to_broadcast([MH, LAST, P]), ALU.add)
            dve.tensor_tensor(g_row[:, SEQ:T].rearrange("h (c t) -> h c t", t=NT),
                              b_row[:, SEQ:T].rearrange("h (c t) -> h c t", t=NT),
                              m_prev[0:MH, LAST:LAST + NB].unsqueeze(2).to_broadcast([MH, NB, NT]), ALU.add)\
                .then_inc(row_step, 1)

        def act_rows(act):
            act.wait_ge(row_step, 1)
            act.activation(m_row, b_row, ACT.Exp, scale=-1.0).then_inc(row_act, 1)
            act.wait_ge(row_act, 1)
            act.activation(b_row, m_row, ACT.Ln, bias=log_one[0:MH, :]).then_inc(row_act, 1)

        def act_columns(act):
            act.wait_ge(a_turned, 1)
            act.activation(acol[:, 0:LAST, :], PS[3][:, 0:LAST * MH].rearrange("p (c h) -> p c h", h=MH), ACT.Copy)
            act.activation(acol[0:SMP, LAST, :], PS[3][0:SMP, LAST * MH:CK * MH], ACT.Copy)
            act.activation(n_all[:, 0:NB * MH], PS[3][:, 64:64 + NB * MH], ACT.Copy).then_inc(a_put, 1)

        def pe_columns(pe):
            pe.wait_ge(smp_kput, NB * PAGES)
            pe.wait_ge(smp_exp, 2)
            pe.wait_ge(smp_put, 2)
            pe.wait_ge(smp_step, 6)
            pe.wait_ge(row_step, ROWS_DONE)
            pe.wait_ge(nst_in, 16)
            for c in range(CK):
                pe.transpose(PS[3][0:rows(c), c * MH:(c + 1) * MH], a_row[:, tile_cols(c)], ident[0:MH, 0:MH])
            pe.transpose(PS[3][:, 64:64 + NB * MH], n_rows[0:NB * MH, :], ident[0:NB * MH, 0:NB * MH])\
                .then_inc(a_turned, 1)
            pe.wait_ge(a_put, 1)

        def pe_mlstm(pe):
            def spread(h, part):
                for c in range(3):
                    n = 9 * h + 3 * part + c
                    if n >= 2:
                        pe.wait_ge(bc_freed, n - 1)
                    pe.matmul(PS[n % 2][:, 0:CH], head_row[:, h, :], (b_row, g_row, m_row)[part][:, c * CH:(c + 1) * CH],
                              start=True, stop=True).then_inc(bc_filled, 1)

            def scores(h, s):
                w = 3 * h + s
                if w:
                    pe.wait_ge(st_done, w)
                    pe.wait_ge(kw_done, w)
                for i, c in enumerate(range(4 * s, min(4 * s + 4, CK))):
                    r = rows(c)
                    pe.matmul(PS[2][0:r, i * P:i * P + r], mkT[:, h, tile_cols(c)], mixT[:, h, tile_cols(c)],
                              start=True, stop=True)
                    mm = pe.transpose(PS[3][0:r, i * P:(i + 1) * P], mkT[:, h, tile_cols(c)], ident)
                mm.then_inc(st_ps, 1)

            def updates(h, s):
                pe.wait_ge(kw_done, 3 * h + s + 1)
                hs_ = slice(h * P, (h + 1) * P)
                for i in range(2):
                    ub = 6 * h + 2 * s + i
                    if ub >= 2:
                        pe.wait_ge(cs_done, ub - 1)
                    bank = PS[4 + ub % 2]
                    if s < 2:
                        for e in range(2):
                            c = 4 * s + 2 * i + e
                            pe.matmul(bank[:, 2 * e * P:(2 * e + 1) * P], kw[:, c, :], mv_tm[:, c, hs_], start=True, stop=True)
                            mm = pe.matmul(bank[:, (2 * e + 1) * P:(2 * e + 2) * P], kw[:, c, :], ones, start=True, stop=True)
                    else:
                        for b in range(4):
                            mm = pe.matmul(bank[:, b * P:(b + 1) * P], kw_smp[0:SMP, 4 * i + b, :], mv_tm[0:SMP, LAST, hs_],
                                           start=True, stop=True)
                    mm.then_inc(u_ps, 1)

            def outputs(h, s):
                w = 3 * h + s
                hs_ = slice(h * P, (h + 1) * P)
                num, den = PS[6], PS[7]
                pe.wait_ge(st_done, w + 1)
                pe.wait_ge(qg_done, h + 1)
                if w:
                    pe.wait_ge(den_taken, w)
                    pe.wait_ge(num_taken, w)
                if s < 2:
                    pe.wait_ge(cs_done, 6 * h + 2 * s + 2)
                    pe.matmul(den[:, 0:4 * P], ones, st[:, 4 * s * P:(4 * s + 4) * P], start=True, stop=False,
                              skip_group_check=True)
                    for i in range(4):
                        c = 4 * s + i
                        o, q = slice(i * P, (i + 1) * P), qg[:, h % 2, tile_cols(c)]
                        pe.matmul(num[:, o], mv_tm[:, c, hs_], st[:, tile_cols(c)], start=True, stop=(c == 0),
                                  skip_group_check=True)
                        if c:
                            pe.matmul(num[:, o], state[:, c - 1, 0:P], q, start=False, stop=True, skip_group_check=True)
                            mm = pe.matmul(den[:, o], state[:, c - 1, P:2 * P], q, start=False, stop=(i == 3),
                                           skip_group_check=True)
                else:
                    pe.wait_ge(c_in[h % 2], 16 * (h // 2 + 1))
                    pe.wait_ge(qn_done, h + 1)
                    pe.wait_ge(kw_done, w + 1)
                    pe.matmul(num[:, 0:SMP], mv_tm[0:SMP, LAST, hs_], st[0:SMP, SEQ:T], start=True, stop=False,
                              skip_group_check=True)
                    for b in range(NB):
                        c = SEQ + NT * b
                        pe.matmul(num[:, NT * b:NT * b + NT], c_smp[:, h % 2, b, :], qg[:, h % 2, c:c + NT],
                                  start=False, stop=True, skip_group_check=True)
                    pe.matmul(den[:, 0:SMP], ones[0:SMP, :], st[0:SMP, SEQ:T], start=True, stop=False)
                    pe.matmul(den[:, 0:SMP], ones, qn, start=False, stop=True)
                    for b in range(NB):
                        mm = pe.matmul(den[:, P + b:P + b + 1], kw_smp[0:SMP, b, :], ones[0:SMP, 0:1], start=True, stop=True)
                mm.then_inc(nd_ps, 1)

            pe.wait_ge(mv_loaded, 16 * TILES)
            pe.wait_ge(fm_loaded, 16 * 3)
            for part in range(3):
                spread(0, part)
            scores(0, 0)
            for h in range(MH):
                more = h + 1 < MH
                if more:
                    spread(h + 1, 0)
                scores(h, 1)
                updates(h, 0)
                if more:
                    spread(h + 1, 1)
                outputs(h, 0)
                scores(h, 2)
                updates(h, 1)
                if more:
                    spread(h + 1, 2)
                outputs(h, 1)
                if more:
                    scores(h + 1, 0)
                outputs(h, 2)
                updates(h, 2)
            pe.wait_ge(n_final, 2 * MH)
            pe.wait_ge(cs_done, 6 * MH)
            pe.transpose(PS[0][0:NB * MH + MH, 0:P], n_all, ident).then_inc(n_back, 1)

        def act_mlstm(act):
            def spread(h, part):
                if h >= 2 and part == 0:
                    act.wait_ge(h_done, 3 * (h - 1))
                    act.wait_ge(cs_done, 6 * (h - 1))
                    act.wait_ge(qg_done, h - 1)
                for c in range(3):
                    n = 9 * h + 3 * part + c
                    act.wait_ge(bc_filled, n + 1)
                    act.activation(sets[h % 2][part][:, c * CH:(c + 1) * CH], PS[n % 2][:, 0:CH],
                                   (ACT.Copy, ACT.Exp, ACT.Exp)[part], scale=(1.0, 1.0, -1.0)[part]).then_inc(bc_freed, 1)

            def weights(h):
                wt = sets[h % 2][0]
                act.wait_ge(wt_arg, h + 1)
                for c in range(CK):
                    r = rows(c)
                    e = act.activation(wt[0:r, tile_cols(c)], wt[0:r, tile_cols(c)], ACT.Exp, bias=acol[0:r, c, h:h + 1])
                e.then_inc(wt_exp, 1)
                act.wait_ge(wt_exp, h + 1)

            def keys(h, s):
                wt, w = sets[h % 2][0], 3 * h + s
                act.wait_ge(st_ps, w + 1)
                if h:
                    act.wait_ge(u_ps, 6 * (h - 1) + 2 * s + 2)
                    act.wait_ge(nd_ps, 3 * h)
                if s < 2:
                    for i in range(4):
                        c = 4 * s + i
                        e = act.activation(kw[:, c, :], PS[3][:, i * P:(i + 1) * P], ACT.Copy,
                                           scale=wt[:, (c + 1) * P - 1:(c + 1) * P])
                else:
                    for b in range(NB):
                        t = SEQ + NT * b + NT - 1
                        e = act.activation(kw_smp[0:SMP, b, :], PS[3][0:SMP, 0:P], ACT.Copy, scale=wt[0:SMP, t:t + 1])
                e.then_inc(kw_done, 1)

            def take_num(h, s):
                w = 3 * h + s
                act.wait_ge(nd_ps, w + 1)
                if w >= 2:
                    act.wait_ge(h_done, w - 1)
                n = 4 * P if s < 2 else SMP
                act.activation(hnum[:, w % 2, 0:n], PS[6][:, 0:n], ACT.Copy).then_inc(num_taken, 1)

            act.wait_ge(smp_values, NB)
            for part in range(3):
                spread(0, part)
            weights(0)
            for h in range(MH):
                for s in range(3):
                    keys(h, s)
                    if h + 1 < MH:
                        spread(h + 1, s)
                    if s:
                        take_num(h, s - 1)
                if h + 1 < MH:
                    weights(h + 1)
                take_num(h, 2)
            act.wait_ge(n_back, 1)
            act.activation(n_out[0:NB * MH + MH, :], PS[0][0:NB * MH + MH, 0:P], ACT.Copy).then_inc(n_out_put, 1)

        def pool_mlstm(pool):
            pool.wait_ge(fm_loaded, 16 * 3)
            def scale_queries(h):
                pool.wait_ge(bc_freed, 9 * h + 6)
                if h >= 2:
                    pool.wait_ge(nd_ps, 3 * (h - 1))
                pool.tensor_tensor(qg[:, h % 2, :], mixT[:, h, :], sets[h % 2][1], ALU.mult).then_inc(qg_done, 1)

            def queries_by_n(h):
                pool.wait_ge(qg_done, h + 1)
                if h == 0:
                    pool.wait_ge(a_put, 1)
                else:
                    pool.wait_ge(nd_ps, 3 * h)
                pool.tensor_tensor(qn.rearrange("p (b t) -> p b t", b=NB),
                                   qg[:, h % 2, SEQ:T].rearrange("p (b t) -> p b t", b=NB),
                                   n_all[:, h:NB * MH:MH].unsqueeze(2).to_broadcast([P, NB, NT]), ALU.mult)\
                    .then_inc(qn_done, 1)

            def divide(h, s):
                w = 3 * h + s
                n, cols = (4 * P, slice(4 * s * P, (4 * s + 4) * P)) if s < 2 else (SMP, slice(SEQ, T))
                pool.wait_ge(inverted, w + 1)
                pool.wait_ge(num_taken, w + 1)
                pool.wait_ge(qg_done, h + 1)
                pool.tensor_tensor(mixT[:, h, cols], hnum[:, w % 2, 0:n], hden[:, w % 2, 0:n], ALU.mult)\
                    .then_inc(h_done, 1)

            scale_queries(0)
            queries_by_n(0)
            for h in range(MH):
                divide(h, 0)
                if h + 1 < MH:
                    scale_queries(h + 1)
                divide(h, 1)
                divide(h, 2)
                if h + 1 < MH:
                    queries_by_n(h + 1)
                gate_out(pool, h)

        def gate_out(pool, h):
            pool.wait_ge(h_done, 3 * (h + 1))
            pool.tensor_tensor(mixT[:, h, :], mixT[:, h, :], moT[:, h, :], ALU.mult).then_inc(gated, 1)

        def dve_mlstm(dve):
            def argument(h):
                wt = sets[h % 2][0]
                dve.wait_ge(bc_freed, 9 * h + 3)
                dve.tensor_tensor(wt[:, 0:SEQ].rearrange("p (c t) -> p c t", t=P),
                                  wt[:, 0:SEQ].rearrange("p (c t) -> p c t", t=P),
                                  causal_t.unsqueeze(1).to_broadcast([P, LAST, P]), ALU.add)
                dve.tensor_tensor(wt[0:SMP, SEQ:T], wt[0:SMP, SEQ:T], new_mask_t, ALU.add).then_inc(wt_arg, 1)

            def weigh(h, s):
                w = 3 * h + s
                dve.wait_ge(st_ps, w + 1)
                dve.wait_ge(wt_exp, h + 1)
                if w >= 3:
                    dve.wait_ge(nd_ps, w - 2)
                r, cols = (P, slice(4 * s * P, (4 * s + 4) * P)) if s < 2 else (SMP, slice(SEQ, T))
                dve.tensor_tensor(st[0:r, cols], PS[2][0:r, 0:cols.stop - cols.start], sets[h % 2][0][0:r, cols], ALU.mult)\
                    .then_inc(st_done, 1)

            def carry(h, s):
                gb = sets[h % 2][1]
                for i in range(2):
                    ub = 6 * h + 2 * s + i
                    dve.wait_ge(u_ps, ub + 1)
                    bank = PS[4 + ub % 2]
                    if s < 2:
                        for e in range(2):
                            c = 4 * s + 2 * i + e
                            if c == 0:
                                if h:
                                    dve.wait_ge(nd_ps, 3 * h)
                                    dve.wait_ge(cp_stored, 16 * h)
                                u = dve.tensor_copy(state[:, 0, :], bank[:, 0:2 * P])
                            else:
                                dve.wait_ge(cs_step, LAST * h + c)
                                u = dve.scalar_tensor_tensor(
                                    out=state[:, c, :], in0=state[:, c - 1, :], scalar=gb[:, (c + 1) * P - 1:(c + 1) * P],
                                    in1=bank[:, 2 * e * P:(2 * e + 2) * P], op0=ALU.mult, op1=ALU.add)
                            u.then_inc(cs_step, 1)
                        dve.wait_ge(cs_step, LAST * h + 4 * s + 2 * i + 2)
                        u = dve.tensor_copy(n_all[:, NB * MH + h:NB * MH + h + 1], state[:, c, P:P + 1])
                    else:
                        for b in range(4):
                            t = SEQ + NT * (4 * i + b) + NT - 1
                            x = c_smp[:, h % 2, 4 * i + b, :]
                            u = dve.scalar_tensor_tensor(out=x, in0=x, scalar=gb[:, t:t + 1],
                                                         in1=bank[:, b * P:(b + 1) * P], op0=ALU.mult, op1=ALU.add)
                    u.then_inc(cs_done, 1)

            def denominator(h, s):
                w = 3 * h + s
                em = sets[h % 2][2]
                n, cols = (4 * P, slice(4 * s * P, (4 * s + 4) * P)) if s < 2 else (SMP, slice(SEQ, T))
                dve.wait_ge(nd_ps, w + 1)
                dve.wait_ge(bc_freed, 9 * h + 9)
                if w >= 2:
                    dve.wait_ge(h_done, w - 1)
                den = hden[:, w % 2, 0:n]
                dve.scalar_tensor_tensor(out=den, in0=PS[7][:, 0:n], scalar=-1.0, in1=em[:, cols],
                                         op0=ALU.mult, op1=ALU.max).then_inc(h_step, 1)
                if s == 2:
                    n_h = n_all[:, h:NB * MH:MH]
                    g_last = sets[h % 2][1][:, SEQ:T].rearrange("p (b t) -> p b t", b=NB)[:, :, NT - 1]
                    dve.wait_ge(qn_done, h + 1)
                    dve.tensor_tensor(n_h, n_h, g_last, ALU.mult).then_inc(n_final, 1)
                    dve.wait_ge(n_final, 2 * h + 1)
                    dve.tensor_tensor(n_h, n_h, PS[7][:, P:P + NB], ALU.add).then_inc(n_final, 1)
                dve.wait_ge(h_step, w + 1)
                dve.tensor_tensor(den, PS[7][:, 0:n], den, ALU.max).then_inc(den_taken, 1)
                dve.wait_ge(den_taken, w + 1)
                dve.reciprocal(den, den).then_inc(inverted, 1)

            argument(0)
            for h in range(MH):
                weigh(h, 0)
                weigh(h, 1)
                carry(h, 0)
                denominator(h, 0)
                weigh(h, 2)
                carry(h, 1)
                denominator(h, 1)
                if h + 1 < MH:
                    argument(h + 1)
                denominator(h, 2)
                carry(h, 2)

        GS0, WD0, WS0, HS0 = 12808, 21000, 23048, 27144
        xs = put("x_split", XS0, 2 * KD * T, F32R).rearrange("p (s k t) -> p s k t", s=2, k=KD)
        gs = put("gate_up_split", GS0, 8 * KD * P, F32R).rearrange("p (u s w k n) -> p u s w k n", u=2, s=2, w=2, k=KD)
        ws = put("weight_split", WS0, 4 * KD * P, F32R)
        hs = put("hidden_split", HS0, 4 * 2 * T, F32R).rearrange("p (m s t) -> p m s t", m=4, s=2)
        y_acc = put("y_acc", 768, KD * T).rearrange("p (k t) -> p k t", t=T)
        graw = put("gate_up", 9216, 2 * KD * P).rearrange("p (w k n) -> p w k n", w=2, k=KD)
        silu = put("silu", 11264, 2 * CH).rearrange("p (s n) -> p s n", s=2)
        hidden = put("hidden", 11968, CH)
        stats = put("stats", 12320, TILES * 48).rearrange("p (i n) -> p i n", n=48)
        moments = put("moments", 12752, TILES * 2).rearrange("p (i n) -> p i n", n=2)
        rstd = put("rstd", 12776, TILES)
        gain_col, bias_col = put("gain_columns", 12792, KD), put("bias_columns", 12800, KD)
        x_tm = put("x_tm", GS0 + 4 * KD * P, TILES * D).rearrange("p (i n) -> p i n", n=D)
        y_tm = put("y_tm", GS0, TILES * D).rearrange("p (i n) -> p i n", n=D)
        wdraw = put("down_weight", WD0, 2 * D).rearrange("p (k n) -> p k n", k=2)
        os_ = put("out_weight_split", HS0, 4 * KD * P, F32R).rearrange("p (u s k n) -> p u s k n", u=2, s=2, k=KD)
        oraw = put("out_weight", HS0 + 4096, 2 * KD * P).rearrange("p (s k n) -> p s k n", s=2, k=KD)
        o_y = put("out_y", HS0 + 6144, 2 * T).rearrange("p (s t) -> p s t", s=2)
        gain, bias_ = (put(f"norm_{n}", HS0 + 4 * T + r * D, D) for r, n in enumerate(("gain", "bias")))
        wds = ws.rearrange("p (s k n) -> p s k n", s=2, k=2)
        norms = {}
        for name in ("first", "second"):
            norms[name] = {s: sem(f"{name}_{s}") for s in
                           ("gb_in", "stat", "var_in", "std", "shift", "centred", "gained", "normed", "nT", "nput")}
        x_back = sem("x_back")
        mix_hi, mix_lo = sem("mix_hi"), sem("mix_lo")
        o_in = [sem("o_in0"), sem("o_in1")]
        o_hi, o_lo, y_ps, y_put, turned, added = (sem(s) for s in ("o_hi", "o_lo", "y_ps", "y_put", "turned", "added"))
        g_in, g_hi, g_lo = sem("g_in"), sem("g_hi"), sem("g_lo")
        wd_in, wd_hi, wd_lo = sem("wd_in"), sem("wd_hi"), sem("wd_lo")
        gu_ps, silu_done, h_made, h_step, h_hi2, h_lo2 = (sem(s) for s in (
            "gu_ps", "silu_done", "h_made", "hid_step", "h_hi", "h_lo"))
        d_ps, d_added = sem("d_ps"), sem("d_added")
        col_stat = sem("column_stat")
        x1_hi, x1_lo, x1_scaled = sem("x1_hi"), sem("x1_lo"), sem("x1_scaled")
        y_stored = sem("y_stored")
        MD = D // P
        GROUPS = MF // 2

        def sp_out(sp):
            sp.wait_ge(gated, MH)
            src = w_out[0].rearrange("(k p) n -> p k n", p=P)

            def load(j):
                for u in range(2):
                    sp.wait_ge(o_lo, j * 2 + (u + 1))
                    sp.dma_start(oraw[:, u], src[:, :, bass.ds(j * (2 * P) + u * P, P)]).then_inc(o_in[u], 16)

            load(0)
            sp_x_back(sp)
            with sp.Fori(1, MD // 2) as j:
                load(j)

        def sp_x_back(sp):
            sp.wait_ge(mix_lo, KD)
            for i in range(TILES):
                src = x_prompt[0, i * P:(i + 1) * P, :] if i < LAST else x_sample.rearrange("b t d -> (b t) d")
                sp.dma_start(x_tm[0:rows(i), i, :], src).then_inc(x_back, 16)
            for dst, src in ((gain_col, ln1_g), (bias_col, ln1_b)):
                sp.dma_start(dst, src[0].rearrange("(k p) -> p k", p=P), allow_slow_non_contiguous=True)\
                    .then_inc(norms["first"]["gb_in"], 16)

        def pe_out(pe):
            pe.sem_inc(y_ps, 6)
            pe.sem_inc(turned, 6)

            def product(j, u, first=False):
                pe.wait_ge(o_lo, j * 2 + (2 + u + 1))
                for c in range(3):
                    pe.wait_ge(y_put, j * 6 + (3 * u + c + 1))
                    for k in range(KD):
                        if first and c == 0:
                            pe.wait_ge(mix_lo, k + 1)
                        for a, b in PARTS:
                            mm = pe.matmul(PS[3 * u + c][:, 0:CH], os_[:, u, a, k, :], xs[:, b, k, c * CH:(c + 1) * CH],
                                           start=(k == 0 and (a, b) == PARTS[0]),
                                           stop=(k == KD - 1 and (a, b) == PARTS[-1]))
                    mm.then_inc(y_ps, 1)

            def turn(j, u):
                pe.wait_ge(y_put, j * 6 + (6 + 3 * u + 3))
                for g in range(3):
                    pe.wait_ge(added, j * 6 + (3 * u + g + 1))
                    for i in range(4 * g, min(4 * g + 4, TILES)):
                        mm = pe.transpose(PS[6 + (3 * u + g) % 2][0:rows(i), (i % 4) * P:(i % 4 + 1) * P],
                                          o_y[:, u, tile_cols(i)], ident)
                    mm.then_inc(turned, 1)

            product(0, 0, True)
            with pe.Fori(0, MD // 2 - 1) as j:
                product(j, 1)
                turn(j, 0)
                product(j + 1, 0)
                turn(j, 1)
            product(MD // 2 - 1, 1)
            turn(MD // 2 - 1, 0)
            turn(MD // 2 - 1, 1)

        def act_out(act):
            act.sem_inc(y_put, 6)

            def high(j, u):
                act.wait_ge(o_in[u], j * 16 + 16)
                act.wait_ge(y_ps, j * 6 + (3 * u + 3))
                act.activation(os_[:, u, 0], oraw[:, u], ACT.Copy).then_inc(o_hi, 1)

            def empty(j, u):
                for c in range(3):
                    act.wait_ge(y_ps, j * 6 + (6 + 3 * u + c + 1))
                    if c == 0:
                        act.wait_ge(turned, j * 6 + (3 * u + 3))
                    act.activation(o_y[:, u, c * CH:(c + 1) * CH], PS[3 * u + c][:, 0:CH], ACT.Copy).then_inc(y_put, 1)

            act.wait_ge(gated, MH)
            act.wait_ge(cp_stored, 16 * MH)
            for k in range(KD):
                if k == KD - 2:
                    high(0, 0)
                act.activation(xs[:, 0, k, :], mixT[:, k, :], ACT.Copy).then_inc(mix_hi, 1)
            with act.Fori(0, MD // 2 - 1) as j:
                high(j, 1)
                empty(j, 0)
                high(j + 1, 0)
                empty(j, 1)
            high(MD // 2 - 1, 1)
            empty(MD // 2 - 1, 0)
            empty(MD // 2 - 1, 1)

        def dve_out(dve):
            dve.sem_inc(added, 2)
            dve.sem_inc(o_lo, 2)

            def low(j, u):
                dve.wait_ge(o_hi, j * 2 + (u + 1))
                dve.tensor_tensor(os_[:, u, 1], oraw[:, u], os_[:, u, 0].bitcast(F32), ALU.subtract).then_inc(o_lo, 1)

            def add(j, u):
                for g in range(3):
                    bank = PS[6 + (3 * u + g) % 2]
                    dve.wait_ge(turned, j * 6 + (6 + 3 * u + g + 1))
                    if g < 2:
                        x = x_tm[:, 4 * g:4 * g + 4, bass.ds(j * (2 * P) + u * P, P)]
                        y = bank[:, :].rearrange("p (i n) -> p i n", i=4)
                    else:
                        x = x_tm[0:SMP, LAST, bass.ds(j * (2 * P) + u * P, P)]
                        y = bank[0:SMP, 0:P]
                    dve.scalar_tensor_tensor(out=x, in0=x, scalar=float(ALPHA), in1=y, op0=ALU.mult, op1=ALU.add)\
                        .then_inc(added, 1)

            def stat(j, u):
                for g in range(3):
                    dve.wait_ge(added, j * 6 + (2 + 3 * u + g + 1))
                    for i in range(4 * g, min(4 * g + 4, TILES)):
                        s = dve.bn_stats(stats[0:rows(i), i, bass.ds(j * 12 + 6 * u, 6)],
                                         x_tm[0:rows(i), i, bass.ds(j * (2 * P) + u * P, P)])
                s.then_inc(col_stat, 1)

            for k in range(KD):
                if k == KD - 2:
                    low(0, 0)
                dve.wait_ge(mix_hi, k + 1)
                dve.tensor_tensor(xs[:, 1, k, :], mixT[:, k, :], xs[:, 0, k, :].bitcast(F32), ALU.subtract)\
                    .then_inc(mix_lo, 1)
            low(0, 1)
            dve.wait_ge(x_back, 16 * TILES)
            with dve.Fori(0, MD // 2 - 1) as j:
                add(j, 0)
                low(j + 1, 0)
                stat(j, 0)
                add(j, 1)
                low(j + 1, 1)
                stat(j, 1)
            add(MD // 2 - 1, 0)
            stat(MD // 2 - 1, 0)
            add(MD // 2 - 1, 1)
            stat(MD // 2 - 1, 1)

        NEEDS = [-(-(c + 1) * CH // P) for c in range(3)]

        def dve_x1(dve):
            nm = norms["first"]
            dve.memset(moments, 1.0).then_inc(nm["stat"], 1)
            dve.wait_ge(nm["stat"], 1)
            dve.wait_ge(col_stat, MD)
            for i in range(TILES):
                r = rows(i)
                s = dve.bn_aggr(moments[0:r, i, :], stats[0:r, i, :])
            s.then_inc(nm["stat"], 1)
            dve.wait_ge(nm["stat"], 2)
            dve.tensor_scalar(rstd, moments[:, :, 1], float(EPS), None, ALU.add).then_inc(nm["var_in"], 1)
            dve.wait_ge(nm["std"], 1)
            dve.reciprocal(rstd, rstd).then_inc(nm["stat"], 1)
            dve.wait_ge(nm["stat"], 3)
            for i in range(TILES + 2):
                if i < TILES:
                    r = rows(i)
                    x = x_tm[0:r, i, :]
                    dve.tensor_scalar(x, x, moments[0:r, i, 0:1], rstd[0:r, i:i + 1], ALU.subtract, ALU.mult)\
                        .then_inc(nm["centred"], 1)
                if i >= 2:
                    for g in range(2):
                        n = 2 * (i - 2) + g
                        dve.wait_ge(nm["nput"], n + 1)
                        x = y_acc[:, 4 * g:4 * g + 4, tile_cols(i - 2)]
                        hi, lo = (xs[:, s, 4 * g:4 * g + 4, tile_cols(i - 2)] for s in range(2))
                        dve.tensor_copy(hi, x).then_inc(x1_hi, 1)
                        dve.wait_ge(x1_hi, n + 1)
                        dve.tensor_tensor(lo, x, hi.bitcast(F32), ALU.subtract).then_inc(x1_lo, 1)

        def act_std(act, nm):
            act.wait_ge(nm["var_in"], 1)
            act.activation(rstd, rstd, ACT.Sqrt).then_inc(nm["std"], 1)

        def pe_x1(pe, n):
            nm = norms["first"]
            i, g = divmod(n, 2)
            r = rows(i)
            pe.wait_ge(nm["centred"], i + 1)
            if n >= 2:
                pe.wait_ge(nm["nput"], n - 1)
            for k in range(4):
                mm = pe.transpose(PS[6 + n % 2][:, k * P:k * P + r], x_tm[0:r, i, (4 * g + k) * P:(4 * g + k + 1) * P],
                                  ident[0:r, 0:r])
            mm.then_inc(nm["nT"], 1)

        def act_x1(act):
            nm = norms["first"]
            act.wait_ge(nm["gb_in"], 32)
            for n in range(2 * TILES):
                i, g = divmod(n, 2)
                act.wait_ge(nm["nT"], n + 1)
                for k in range(4):
                    m = 4 * g + k
                    a = act.activation(y_acc[:, m, tile_cols(i)], PS[6 + n % 2][:, k * P:k * P + rows(i)], ACT.Identity,
                                       bias=bias_col[:, m:m + 1], scale=gain_col[:, m:m + 1])
                a.then_inc(nm["nput"], 1)

        def sp_ffn(sp):
            wg = w_gate[0].rearrange("(k p) n -> p k n", p=P)
            wu = w_up[0].rearrange("(k p) n -> p k n", p=P)
            wd = w_down[0].rearrange("(m p) n -> p m n", p=P)

            def gate(g, u):
                sp.wait_ge(g_lo, g * 2 + (u + 1))
                for w, src in ((0, wg), (1, wu)):
                    sp.dma_start(graw[:, w], src[:, :, bass.ds(g * (2 * P) + u * P, P)]).then_inc(g_in, 16)

            gate(0, 0)
            sp.wait_ge(norms["first"]["nput"], 2 * TILES)
            with sp.Fori(0, GROUPS - 1) as g:
                gate(g, 1)
                sp.wait_ge(wd_lo, g + 1)
                sp.dma_start(wdraw, wd[:, bass.ds(g * 2, 2), :]).then_inc(wd_in, 16)
                gate(g + 1, 0)
            gate(GROUPS - 1, 1)
            sp.wait_ge(wd_lo, GROUPS)
            sp.dma_start(wdraw, wd[:, 2 * (GROUPS - 1):2 * GROUPS, :]).then_inc(wd_in, 16)

        def pe_down(pe, g, s, n, d, c):
            pe.wait_ge(d_added, g * (3 * MD) + (n + 1))
            for k in range(2):
                for a, b in PARTS:
                    mm = pe.matmul(PS[6 + n % 2][:, 0:CH], wds[:, a, k, d * P:(d + 1) * P],
                                   hs[:, 2 * s + k, b, c * CH:(c + 1) * CH],
                                   start=(k == 0 and (a, b) == PARTS[0]), stop=(k == 1 and (a, b) == PARTS[-1]))
            mm.then_inc(d_ps, 1)

        def dve_add(dve, g, n, d, c):
            y = y_acc[:, d, c * CH:(c + 1) * CH]
            dve.wait_ge(d_ps, g * (3 * MD) + (3 * MD + n + 1))
            dve.tensor_tensor(y, y, PS[6 + n % 2][:, 0:CH], ALU.add).then_inc(d_added, 1)

        def pe_ffn(pe):
            def gate(g, u, first=False):
                pe.wait_ge(g_lo, g * 2 + (u + 2))
                for c in range(3):
                    ahead = []
                    if first:
                        for n in range(2 * NEEDS[0] if c == 0 else 0):
                            pe_x1(pe, n)
                        pe.wait_ge(x1_lo, 2 * NEEDS[c])
                        ahead = list(range(2 * NEEDS[c], 2 * NEEDS[c + 1])) if c < 2 else []
                    pe.wait_ge(h_made, g * 6 + (3 * u + c + 1))
                    for w in range(2):
                        for k in range(KD):
                            for a, b in PARTS:
                                mm = pe.matmul(PS[2 * c + w][:, 0:CH], gs[:, u, a, w, k, :],
                                               xs[:, b, k, c * CH:(c + 1) * CH],
                                               start=(k == 0 and (a, b) == PARTS[0]),
                                               stop=(k == KD - 1 and (a, b) == PARTS[-1]))
                            if ahead and k % 2:
                                pe_x1(pe, ahead.pop(0))
                    mm.then_inc(gu_ps, 1)

            def down(g, s):
                pe.wait_ge(wd_lo, g + 2)
                pe.wait_ge(h_lo2, g * 6 + 6)
                for d in range(MD):
                    for c in range(3):
                        pe_down(pe, g, s, 3 * d + c, d, c)

            def body(g, s):
                gate(g, 0)
                down(g - 1, 1 - s)
                gate(g, 1)

            gate(0, 0, True)
            gate(0, 1)
            with pe.Fori(0, (GROUPS - 3) // 2) as j:
                body(j * 2 + 1, 1)
                body(j * 2 + 2, 0)
            body(GROUPS - 2, 1)
            body(GROUPS - 1, 0)

        def high(act, g, u):
            act.wait_ge(g_in, g * 64 + (32 * u + 32))
            act.wait_ge(gu_ps, g * 6 + (3 * u + 3))
            act.activation(gs[:, u, 0], graw, ACT.Copy).then_inc(g_hi, 1)

        def act_ffn(act):
            def gates_(g, u):
                for c in range(3):
                    n = 3 * u + c
                    act.wait_ge(gu_ps, g * 6 + (6 + n + 1))
                    act.wait_ge(h_made, g * 6 + (n + 2))
                    act.activation(silu[:, n % 2, :], PS[2 * c][:, 0:CH], ACT.Silu).then_inc(silu_done, 1)

            def high_down(g):
                act.wait_ge(wd_in, g * 16 + 16)
                act.wait_ge(d_ps, g * (3 * MD) + 3 * MD)
                act.activation(wds[:, 0], wdraw, ACT.Copy).then_inc(wd_hi, 1)

            def body(g, last=False):
                high(act, g, 1)
                gates_(g, 0)
                if not last:
                    high(act, g + 1, 0)
                high_down(g)
                gates_(g, 1)

            with act.Fori(0, GROUPS - 1) as g:
                body(g)
            body(GROUPS - 1, True)

        def dve_ffn(dve):
            def hide(g, u, s):
                for c in range(3):
                    n = 3 * u + c
                    slot, cols = 2 * s + u, slice(c * CH, (c + 1) * CH)
                    dve.wait_ge(silu_done, g * 6 + (n + 1))
                    if n or not isinstance(g, int) or g:
                        dve.wait_ge(h_lo2, g * 6 + n)
                    dve.tensor_tensor(hidden, silu[:, n % 2, :], PS[2 * c + 1][:, 0:CH], ALU.mult).then_inc(h_made, 1)
                    dve.wait_ge(h_made, g * 6 + (3 + n + 1))
                    dve.tensor_copy(hs[:, slot, 0, cols], hidden).then_inc(h_hi2, 1)
                    dve.wait_ge(h_hi2, g * 6 + (n + 1))
                    dve.tensor_tensor(hs[:, slot, 1, cols], hidden, hs[:, slot, 0, cols].bitcast(F32), ALU.subtract)\
                        .then_inc(h_lo2, 1)

            def add(g):
                for d in range(MD):
                    for c in range(3):
                        dve_add(dve, g, 3 * d + c, d, c)

            def body(g, s):
                hide(g, 0, s)
                add(g - 1)
                hide(g, 1, s)

            hide(0, 0, 0)
            dve.wait_ge(x1_lo, 2 * TILES)
            dve.tensor_scalar(y_acc, y_acc, float(ALPHA), None, ALU.mult).then_inc(x1_scaled, 1)
            hide(0, 1, 0)
            dve.wait_ge(x1_scaled, 1)
            with dve.Fori(0, (GROUPS - 3) // 2) as j:
                body(j * 2 + 1, 1)
                body(j * 2 + 2, 0)
            body(GROUPS - 2, 1)
            body(GROUPS - 1, 0)

        def pool_ffn(pool):
            def low(g, u):
                pool.wait_ge(g_hi, g * 2 + (u + 1))
                pool.tensor_tensor(gs[:, u, 1], graw, gs[:, u, 0].bitcast(F32), ALU.subtract).then_inc(g_lo, 1)

            def low_down(g):
                pool.wait_ge(wd_hi, g + 1)
                pool.tensor_tensor(wds[:, 1], wdraw, wds[:, 0].bitcast(F32), ALU.subtract).then_inc(wd_lo, 1)

            pool.sem_inc(g_lo, 1)
            pool.sem_inc(wd_lo, 1)
            low(0, 0)
            with pool.Fori(0, GROUPS - 1) as g:
                low(g, 1)
                low(g + 1, 0)
                low_down(g)
            low(GROUPS - 1, 1)
            low_down(GROUPS - 1)

        DONE = [(c + 1) * CH // P for c in range(2)] + [TILES]
        BATCHES = [range(DONE[c - 1] if c else 0, DONE[c]) for c in range(3)]
        LAST_GROUP = GROUPS - 1
        BY_DVE = range(TILES - 2, TILES)
        dve_normed = sem("dve_normed")

        def pe_y(pe):
            nm = norms["second"]
            pe.wait_ge(wd_lo, GROUPS + 1)
            pe.wait_ge(h_lo2, 6 * GROUPS)

            def turn(c):
                pe.wait_ge(d_added, 3 * MD * LAST_GROUP + (2 + MD * (c + 1)))
                for n in range(2 * BATCHES[c].start, 2 * BATCHES[c].stop):
                    i, g = divmod(n, 2)
                    if n >= 4:
                        pe.wait_ge(nm["nput"], n - 3)
                    for k in range(4):
                        mm = pe.transpose(PS[n % 4][0:rows(i), k * P:(k + 1) * P], y_acc[:, 4 * g + k, tile_cols(i)], ident)
                    mm.then_inc(nm["nT"], 1)

            for c in range(3):
                for d in range(MD):
                    pe_down(pe, LAST_GROUP, 0, MD * c + d, d, c)
                    if d == 2 and c:
                        turn(c - 1)
            turn(2)

        def act_y(act):
            nm = norms["second"]

            def centre(tiles):
                act.wait_ge(nm["shift"], tiles.stop)
                for i in tiles:
                    r = rows(i)
                    act.activation(y_tm[0:r, i, :], y_tm[0:r, i, :], ACT.Identity, bias=moments[0:r, i, 0:1],
                                   scale=rstd[0:r, i:i + 1]).then_inc(nm["centred"], 1)

            for c in range(3):
                for n in range(2 * BATCHES[c].start, 2 * BATCHES[c].stop):
                    i, g = divmod(n, 2)
                    act.wait_ge(nm["nT"], n + 1)
                    act.activation(y_tm[0:rows(i), i, 512 * g:512 * g + 512], PS[n % 4][0:rows(i), :], ACT.Copy)\
                        .then_inc(nm["nput"], 1)
                act.wait_ge(nm["var_in"], c + 1)
                t = slice(BATCHES[c].start, BATCHES[c].stop)
                act.activation(rstd[:, t], rstd[:, t], ACT.Sqrt).then_inc(nm["std"], 1)
                centre(BATCHES[c])

        def dve_y(dve):
            nm = norms["second"]
            step = 0
            dve.memset(moments, 1.0).then_inc(nm["stat"], 1)

            def stat(c):
                nonlocal step
                for i in BATCHES[c]:
                    r = rows(i)
                    for g in range(2):
                        dve.wait_ge(nm["nput"], 2 * i + g + 1)
                        s = dve.bn_stats(stats[0:r, i, 6 * g:6 * g + 6], y_tm[0:r, i, 512 * g:512 * g + 512])
                s.then_inc(nm["stat"], 1)
                step += 2 if step == 0 else 1
                dve.wait_ge(nm["stat"], step)
                for i in BATCHES[c]:
                    r = rows(i)
                    s = dve.bn_aggr(moments[0:r, i, :], stats[0:r, i, 0:12])
                s.then_inc(nm["stat"], 1)
                step += 1
                dve.wait_ge(nm["stat"], step)
                t = slice(BATCHES[c].start, BATCHES[c].stop)
                dve.tensor_scalar(rstd[:, t], moments[:, t, 1], float(EPS), None, ALU.add).then_inc(nm["var_in"], 1)
                dve.wait_ge(nm["std"], c + 1)
                dve.reciprocal(rstd[:, t], rstd[:, t]).then_inc(nm["stat"], 1)
                step += 1
                dve.wait_ge(nm["stat"], step)
                for i in BATCHES[c]:
                    dve.scalar_tensor_tensor(out=moments[:, i, 0:1], in0=moments[:, i, 0:1], scalar=-1.0,
                                             in1=rstd[:, i:i + 1], op0=ALU.mult, op1=ALU.mult).then_inc(nm["shift"], 1)

            def scale(c):
                dve.wait_ge(nm["gb_in"], 32)
                for i in BATCHES[c]:
                    y = y_tm[0:rows(i), i, :]
                    dve.wait_ge(nm["centred"], i + 1)
                    dve.tensor_tensor(y, y, gain[0:rows(i), :], ALU.mult).then_inc(nm["gained"], 1)
                    if i in BY_DVE:
                        dve.wait_ge(nm["gained"], i + 1)
                        dve.tensor_tensor(y, y, bias_[0:rows(i), :], ALU.add).then_inc(dve_normed, 1)

            for c in range(3):
                for d in range(MD):
                    dve_add(dve, LAST_GROUP, MD * c + d, d, c)
                    if d == 4 and c:
                        stat(c - 1)
                if c:
                    scale(c - 1)
            stat(2)
            scale(2)

        def pool_y(pool):
            nm = norms["second"]
            for i in range(BY_DVE.start):
                pool.wait_ge(nm["gained"], i + 1)
                y = y_tm[0:rows(i), i, :]
                pool.tensor_tensor(y, y, bias_[0:rows(i), :], ALU.add).then_inc(nm["normed"], 1)

        def sp_phase5(sp):
            sp_out(sp)
            sp_ffn(sp)
            nm = norms["second"]
            sp.wait_ge(d_ps, 3 * MD * GROUPS)
            sp.dma_start(gain, ln2_g[0].partition_broadcast(P)).then_inc(nm["gb_in"], 16)
            sp.dma_start(bias_, ln2_b[0].partition_broadcast(P)).then_inc(nm["gb_in"], 16)
            for i in range(TILES):
                if i in BY_DVE:
                    sp.wait_ge(dve_normed, i - BY_DVE.start + 1)
                else:
                    sp.wait_ge(nm["normed"], i + 1)
                dst = y_prompt[0, i * P:(i + 1) * P, :] if i < LAST else y_sample.rearrange("b t d -> (b t) d")
                sp.dma_start(dst, y_tm[0:rows(i), i, :]).then_inc(y_stored, 16)
            sp.wait_ge(y_stored, 16 * TILES)

        def pe_phase5(pe):
            pe.wait_ge(gated, MH)
            pe.sem_inc(gu_ps, 6)
            pe.sem_inc(d_ps, 3 * MD)
            pe_out(pe)
            pe_ffn(pe)
            pe_y(pe)

        def act_phase5(act):
            act_out(act)
            high(act, 0, 0)
            act_std(act, norms["first"])
            act_x1(act)
            act_ffn(act)
            act_y(act)

        def pool_phase5(pool):
            pool_ffn(pool)
            pool_y(pool)

        def dve_phase5(dve):
            dve.sem_inc(h_made, 3)
            dve.sem_inc(d_added, 2)
            dve_out(dve)
            dve_x1(dve)
            dve_ffn(dve)
            dve_y(dve)
        def sp_rest(sp):
            sp_attention(sp)
            load_keys(sp, 0)
            load_keys(sp, 1)
            sp_samples(sp)
            sp_rows(sp)
            sp_mlstm(sp)
            sp_mlstm_end(sp)
            sp_phase5(sp)

        def pe_rest(pe):
            pe_attention(pe)
            pe_samples(pe)
            pe_columns(pe)
            pe_mlstm(pe)
            pe_phase5(pe)

        def act_rest(act):
            act_attention(act)
            act_rows(act)
            act_samples(act)
            act_columns(act)
            act_mlstm(act)
            act_phase5(act)

        def pool_rest(pool):
            pool_mlstm(pool)
            pool_phase5(pool)

        def dve_rest(dve):
            dve_attention(dve)
            dve_rows(dve)
            dve_samples(dve)
            dve_mlstm(dve)
            dve_phase5(dve)

        block = ctx.enter_context(nc.Block())

        @block.sync
        def _(sp):
            sp.dma_start(sq, c_square).then_inc(square_in, 16)

            def load_x(i):
                if i >= 3:
                    sp.wait_ge(filled, pos["xT", i - 3, 1] + 1)
                src = x_prompt[0, i * P:(i + 1) * P, :] if i < LAST else x_sample.rearrange("b t d -> (b t) d")
                sp.dma_start(xin[0:rows(i), i % 3, :], src).then_inc(x_in[i % 3], 16)

            win = w_in[0].rearrange("(k p) n -> p k n", p=P)

            def load_w(n):
                g, u = units[n]
                if n:
                    sp.wait_ge(w_lo, n)
                if n == 4:
                    sp.wait_ge(filled, pos["scd",] + 1)
                sp.dma_start(wraw[n >= 4], win[:, :, col[g] + HALF * u:col[g] + HALF * (u + 1)]).then_inc(w_in_s, 16)

            for i in range(3):
                load_x(i)
            load_w(0)
            load_x(3)
            sp.dma_start(rope, c_rope).then_inc(const_in, 16)
            sp.dma_start(small, c_small).then_inc(const_in, 16)
            sp.dma_start(crow[0:MH, :], c_rows).then_inc(const_in, 16)
            sp.dma_start(ptab[:, :], page_table.rearrange("(a b) n -> a (b n)", a=1)).then_inc(const_in, 16)
            sp.dma_start(gate_b[0:MH, :], b_gate[0, :].rearrange("(w h) -> h w", w=2),
                         allow_slow_non_contiguous=True).then_inc(const_in, 16)
            for i in range(4, TILES):
                load_x(i)
            sp.dma_start(wsm[:, :, 0:NSM], win[:, :, IK:IK + NSM]).then_inc(wsm_in, 16)
            sp.dma_start(wsm[:, :, NSM:80], win[:, :, MI:MI + 8]).then_inc(wsm_in, 16)
            load_w(1)
            load_w(2)
            sp.wait_ge(const_in, 16 * 5)
            with sp.Fori(0, NB * PAGES) as j:
                page = sp.value_load(ptab[0:1, bass.ds(j, 1)], min_val=0, max_val=cache_kidx.shape[1] - 1)
                for twin in range(2):
                    sp.dma_start(kix_flat[:, bass.ds(j * P + twin * IDX_D, IDX_D)],
                                 cache_kidx[0, bass.ds(page, 1)].rearrange("a p n -> (a p) n")).then_inc(kix_in, 16)

            def store(g, u, i):
                j = ("tm", g, u, i)
                s = stage_no[j] % STG
                if g in ("ak", "ik"):
                    sp.wait_ge(roped, rope_no[j] + 1)
                else:
                    sp.wait_ge(freed, pos[j] + 1)
                smp, prm = dict(ak=(k_sample, k_prompt), av=(v_sample, v_prompt), ik=(kidx_sample, kidx_prompt),
                                mv=(None, None))[g]
                if g == "mv":
                    dst = mv_dram[i * P:i * P + rows(i), :]
                elif i == LAST:
                    dst = smp[0].rearrange("b t h n -> (b t) (h n)") if g != "ik" else smp[0].rearrange("b t n -> (b t) n")
                else:
                    dst = prm[0, 0, i * P:(i + 1) * P]
                    if g != "ik":
                        dst = dst.rearrange("t h n -> t (h n)")
                if g == "ik":
                    w = IDX_D
                else:
                    dst, w = dst[:, HALF * u:HALF * (u + 1)], HALF
                sp.dma_start(dst, stage[0:rows(i), s, 0:w]).then_inc(stored[s], 16)

            def store_all(g, u):
                for i in range(TILES):
                    store(g, u, i)

            load_w(3)
            store_all("ik", 0)
            sp.dma_start(iw_dram, iw[0:SMP, LAST, :]).then_inc(wcol_in, 16)
            sp.wait_ge(wcol_in, 16)
            for b in range(NB):
                sp.dma_start(wcol[32 * (b % 4):32 * (b % 4) + 32, b // 4:b // 4 + 1],
                             iw_dram[NT * b:NT * b + NT, :].rearrange("t h -> h t"),
                             allow_slow_non_contiguous=True).then_inc(wcol_in, 16)
            for n in range(2, len(units)):
                g, u = units[n]
                if 4 <= n + 2 < len(units):
                    load_w(n + 2)
                if g in ("ak", "av", "mv"):
                    store_all(g, u)
                elif g != "aq":
                    for m in range(2 * u, 2 * u + 2):
                        for c in range(3):
                            f = fm_no["fm", g, m, c]
                            sp.wait_ge(freed, pos["fm", g, m, c] + 1)
                            sp.dma_start(fm_dram[("mk", "mq", "mo").index(g), m, :, c * CH:(c + 1) * CH],
                                         fstage[:, f % FST, :]).then_inc(fstored[f % FST], 16)
            for s in range(STG):
                sp.wait_ge(stored[s], 16 * seen[s])
            for s in range(FST):
                sp.wait_ge(fstored[s], 16 * (len(fm_no) // FST))
            sp_rest(sp)

        @block.tensor
        def _(pe):
            pe.wait_ge(square_in, 16)
            for n, job in enumerate(jobs):
                kind = job[0]
                bank = PS[n % RING]
                if n >= RING:
                    pe.wait_ge(freed, n - RING + 1)
                    if jobs[n - RING][0] == "xT":
                        _, i, j = jobs[n - RING]
                        pe.wait_ge(x_low, 2 * i + j + 1)
                if kind == "xT":
                    _, i, j = job
                    r = rows(i)
                    if j == 0:
                        pe.wait_ge(x_in[i % 3], 16 * (i // 3 + 1))
                    for k in range(4):
                        mm = pe.transpose(bank[:, k * P:k * P + r], xin[0:r, i % 3, (4 * j + k) * P:(4 * j + k + 1) * P],
                                          ident[0:r, 0:r])
                elif kind == "tm":
                    _, g, u, i = job
                    if g == "ik":
                        pe.wait_ge(freed, pos["ikf", 2] + 1)
                        mm = pe.transpose(bank[0:rows(i), 0:NSM], kiT[0:NSM, tile_cols(i)], ident[0:NSM, 0:NSM])
                    else:
                        pe.wait_ge(w_lo, unit_no[g, u] + 1)
                        w = wsplit[unit_no[g, u] % 2]
                        pe.wait_ge(x_low, 2 * i + 2)
                        for k in range(KD):
                            for a, b in PARTS:
                                mm = pe.matmul(bank[0:rows(i), 0:HALF], xs1[:, a, k, tile_cols(i)], w[:, b, k, :],
                                               start=(k == 0 and (a, b) == PARTS[0]),
                                               stop=(k == KD - 1 and (a, b) == PARTS[-1]))
                elif kind == "ikf":
                    _, c = job
                    pe.wait_ge(wsm_lo, 2)
                    for k in range(KD):
                        for a, b in PARTS:
                            mm = pe.matmul(bank[0:NSM, 0:CH], wsm_s[:, a, k, :], xs1[:, b, k, c * CH:(c + 1) * CH],
                                           start=(k == 0 and (a, b) == PARTS[0]),
                                           stop=(k == KD - 1 and (a, b) == PARTS[-1]))
                elif kind == "tr":
                    _, g, u, i = job
                    r = rows(i)
                    pe.wait_ge(roped, rope_no["tm", g, u, i] + 1)
                    s = stage_no["tm", g, u, i] % STG
                    for k in range(1 if g == "ik" else 2):
                        mm = pe.transpose(bank[:, k * P:k * P + r], stage[0:r, s, k * P:(k + 1) * P], ident[0:r, 0:r])
                elif kind == "idx":
                    _, i, h, c = job
                    wd = min(512, widths[i] - 512 * c)
                    if h == 0 and c == 0:
                        pe.wait_ge(freed, pos["tr", "ik", 0, i] + 1)
                    lo = 64 * (h % 2)
                    mm = pe.matmul(bank[:, 0:wd], iqT[lo:lo + 64, h // 2, tile_cols(i)],
                                   kiT[lo:lo + 64, 512 * c:512 * c + wd], start=True, stop=True)
                elif kind == "kxT":
                    _, q = job
                    if q == 0:
                        pe.wait_ge(kix_in, 2 * 16 * NB * PAGES)
                    for j in range(4):
                        mm = pe.transpose(bank[:, j * P:(j + 1) * P], kix[:, 4 * q + j, :], ident)
                elif kind == "idxd":
                    _, g = job
                    pe.wait_ge(freed, pos["kxT", 3] + 1)
                    for b4 in range(4):
                        b = 4 * g + b4
                        o = bank[32 * b4:32 * b4 + 32]
                        for q in range(4):
                            mm = pe.matmul(o[:, 0:PAST], qbd[:, q, b, :],
                                           kixT[:, PAGES * b:PAGES * b + PAGES, :].rearrange("p j n -> p (j n)"),
                                           start=(q == 0), stop=(q == 3), tile_position=(0, 32 * b4))
                        for q in range(4):
                            mm = pe.matmul(o[:, PAST:SC_W], qbd[:, q, b, :], kiT[:, SEQ:T],
                                           start=(q == 0), stop=(q == 3), tile_position=(0, 32 * b4))
                elif kind == "scd":
                    pe.wait_ge(freed, pos["idxd", 1] + 1)
                    pe.wait_ge(wsel_done, 2)
                    for g in range(2):
                        mm = pe.matmul(bank[0:SMP, 0:SC_W], wsel[:, g, :], relud[:, g, :], start=(g == 0), stop=(g == 1))
                elif kind == "fm":
                    _, g, m, c = job
                    n_unit = unit_no[g, m // 2]
                    pe.wait_ge(w_lo, n_unit + 1)
                    for k in range(KD):
                        for a, b in PARTS:
                            mm = pe.matmul(bank[:, 0:CH], wsplit[n_unit % 2][:, a, k, (m % 2) * P:(m % 2 + 1) * P],
                                           xs1[:, b, k, c * CH:(c + 1) * CH],
                                           start=(k == 0 and (a, b) == PARTS[0]),
                                           stop=(k == KD - 1 and (a, b) == PARTS[-1]))
                elif kind == "gate":
                    _, w, c = job
                    for k in range(KD):
                        for a, b in PARTS:
                            mm = pe.matmul(bank[0:MH, 0:CH], wgate_s[:, a, k, 4 * w:4 * w + 4],
                                           xs1[:, b, k, c * CH:(c + 1) * CH],
                                           start=(k == 0 and (a, b) == PARTS[0]),
                                           stop=(k == KD - 1 and (a, b) == PARTS[-1]))
                mm.then_inc(filled, 1)
            pe_rest(pe)

        @block.scalar
        def _(act):
            def high(n):
                act.wait_ge(w_in_s, 16 * (n + 1))
                if n >= 2:
                    act.wait_ge(filled, unit_end[n - 2] + 1)
                act.activation(wsplit[n % 2][:, 0], wraw[n >= 4], ACT.Copy).then_inc(w_hi, 1)

            high_before = {6: [0], pos["tm", "iq", 0, 6]: [1]}
            for n in range(2, len(units)):
                high_before.setdefault(unit_end[n - 2] + 1, []).append(n)
            for n, job in enumerate(jobs):
                for unit in high_before.get(n, ()):
                    high(unit)
                    if unit == 1:
                        act.wait_ge(wsm_in, 32)
                        act.activation(wsm_s[:, 0], wsm[:, :, 0:NSM], ACT.Copy).then_inc(wsm_hi, 1)
                        act.activation(wgate_s[:, 0], wsm[:, :, NSM:80], ACT.Copy).then_inc(wsm_hi, 1)
                kind = job[0]
                bank = PS[n % RING]
                if kind == "tm":
                    _, g, u, i = job
                    s = stage_no[job]
                    if s >= STG:
                        last = staged[s - STG]
                        if last[1] in ("iq", "ik", "ak", "aq"):
                            act.wait_ge(filled, pos[("tr",) + last[1:]] + 1)
                        if last in store_no:
                            act.wait_ge(stored[s % STG], 16 * store_no[last])
                if kind == "idx" and idx_no[job] >= 4:
                    act.wait_ge(scored, idx_no[job] - 3)
                act.wait_ge(filled, n + 1)
                if kind == "xT":
                    _, i, j = job
                    out = act.activation(xs1[:, 0, 4 * j:4 * j + 4, tile_cols(i)],
                                         bank[:, :].rearrange("p (k n) -> p k n", k=4)[:, :, 0:rows(i)], ACT.Copy)
                elif kind == "tm":
                    _, g, u, i = job
                    r, st = rows(i), stage[:, stage_no[job] % STG, :]
                    if g == "ik":
                        act.activation(iw[0:r, i, :], bank[0:r, IDX_D:NSM], ACT.Copy,
                                       scale=float(AH ** -0.5 * IDX_D ** -0.5))
                        act.activation(st[0:r, IDX_D:2 * IDX_D], bank[0:r, 0:IDX_D], ACT.Copy)
                        out = act.activation(st[0:r, 0:IDX_D], bank[0:r, 0:IDX_D], ACT.Copy)
                    else:
                        out = act.activation(st[0:r, :], bank[0:r, 0:HALF], ACT.Copy)
                elif kind == "ikf":
                    _, c = job
                    out = act.activation(kiT[0:NSM, c * CH:(c + 1) * CH], bank[0:NSM, 0:CH], ACT.Copy)
                elif kind == "tr":
                    _, g, u, i = job
                    r = rows(i)
                    if g == "ik":
                        out = act.activation(kiT[:, tile_cols(i)], bank[:, 0:r], ACT.Copy)
                    else:
                        if g == "ak":
                            act.wait_ge(w_lo, 4)
                        if g == "aq" and i == 0:
                            act.wait_ge(filled, pos["idxd", 1] + 1)
                        if i == LAST and g in ("iq", "aq"):
                            act.wait_ge(zeroed, 1)
                            for h in range(4 * u, 4 * u + 4):
                                lo, k = 64 * (h % 2), h // 2 - 2 * u
                                act.activation(
                                    qbd[lo:lo + 64, h // 2, :, NT * h:NT * h + NT],
                                    bank[lo:lo + 64, k * P:k * P + SMP].rearrange("p (b t) -> p b t", b=NB), ACT.Copy)
                        out = act.activation(turned_into[g][:, 2 * u:2 * u + 2, tile_cols(i)],
                                             bank[:, 0:HALF].rearrange("p (k n) -> p k n", k=2)[:, :, 0:r], ACT.Copy)
                elif kind == "idx":
                    _, i, h, c = job
                    wd = min(512, widths[i] - 512 * c)
                    out = act.activation(relu[:, idx_no[job] % 4, 0:wd], bank[:, 0:wd], ACT.Relu)
                elif kind == "kxT":
                    _, q = job
                    out = act.activation(kixT[:, 4 * q:4 * q + 4, :],
                                         bank[:, :].rearrange("p (k n) -> p k n", k=4), ACT.Copy)
                elif kind == "idxd":
                    if job[1] == 0:
                        act.wait_ge(scored, len(idx_jobs))
                    out = act.activation(relud[:, job[1], :], bank[:, 0:SC_W], ACT.Relu)
                elif kind == "scd":
                    out = act.activation(scd[0:SMP, :], bank[0:SMP, 0:SC_W], ACT.Copy)
                elif kind == "fm":
                    _, g, m, c = job
                    f = fm_no[job]
                    if f >= FST:
                        act.wait_ge(fstored[f % FST], 16 * (f // FST))
                    out = act.activation(fstage[:, f % FST, :], bank[:, 0:CH],
                                         ACT.Sigmoid if g == "mo" else ACT.Copy,
                                         scale=float(P ** -0.5) if g == "mk" else 1.0)
                elif kind == "gate":
                    _, w, c = job
                    if w == 0 and c == 0:
                        act.wait_ge(const_in, 16 * 5)
                    out = act.activation(gates[0:MH, w, c * CH:(c + 1) * CH], bank[0:MH, 0:CH], ACT.Identity,
                                         bias=gate_b[0:MH, w:w + 1])
                out.then_inc(freed, 1)
            act_rest(act)

        @block.gpsimd
        def _(pool):
            pool.memset(qbd, 0.0).then_inc(zeroed, 1)
            steps = 0

            def rope_tile(job):
                nonlocal steps
                _, g, u, i = job
                r, hn = rows(i), 2 if g == "ik" else AH // 2
                s = stage[0:r, stage_no[job] % STG, 0:hn * AD].rearrange("p (h n) -> p h n", h=hn)
                t = ropet[0:r, 0:hn * 32].rearrange("p (h n) -> p h n", h=hn)
                cos = rope[0:r, i, 0, :].unsqueeze(1).to_broadcast([r, hn, 16])
                sin = rope[0:r, i, 1, :].unsqueeze(1).to_broadcast([r, hn, 16])
                pool.wait_ge(freed, pos[job] + 1)
                if steps:
                    pool.wait_ge(roped, steps)
                pool.tensor_tensor(t[:, :, 0:16], s[:, :, 0:16], cos, ALU.mult)
                pool.tensor_tensor(t[:, :, 16:24], s[:, :, 8:16], sin[:, :, 0:8], ALU.mult)
                pool.tensor_tensor(t[:, :, 24:32], s[:, :, 0:8], sin[:, :, 8:16], ALU.mult).then_inc(rope_step, 1)
                pool.wait_ge(rope_step, steps + 1)
                pool.tensor_tensor(s[:, :, 0:16], t[:, :, 0:16], t[:, :, 16:32], ALU.add).then_inc(roped, 1)
                steps += 1

            def low(n):
                pool.wait_ge(w_hi, n + 1)
                hi, lo = wsplit[n % 2][:, 0], wsplit[n % 2][:, 1]
                pool.tensor_tensor(lo, wraw[n >= 4], hi.bitcast(F32), ALU.subtract).then_inc(w_lo, 1)

            low(0)
            pool.wait_ge(const_in, 16 * 5)
            for i in range(6):
                rope_tile(("tm", "iq", 0, i))
            low(1)
            for part, (w, ws_) in enumerate(((wsm[:, :, 0:NSM], wsm_s), (wsm[:, :, NSM:80], wgate_s))):
                pool.wait_ge(wsm_hi, part + 1)
                pool.tensor_tensor(ws_[:, 1], w, ws_[:, 0].bitcast(F32), ALU.subtract).then_inc(wsm_lo, 1)
            for job in rope_jobs[6:]:
                rope_tile(job)
                if job[3] == LAST and job[1] != "ik":
                    low(unit_no[job[1], job[2]] + 2)
                if job == ("tm", "ik", 0, LAST):
                    pool.wait_ge(wcol_in, 16 * (NB + 1))
                    for g in range(2):
                        pool.tensor_scalar(wsel[:, g, :], wsel_mask[:, g, :], wcol[:, g:g + 1], None, ALU.mult)\
                            .then_inc(wsel_done, 1)
            for n in range(unit_no["aq", 1] + 3, len(units)):
                low(n)
            pool_rest(pool)

        @block.vector
        def _(dve):
            for n in range(2 * TILES):
                i, j = divmod(n, 2)
                job_no = pos["xT", i, j]
                dve.wait_ge(freed, job_no + 1)
                hi, lo = (xs1[:, s, 4 * j:4 * j + 4, tile_cols(i)] for s in range(2))
                dve.tensor_tensor(lo, PS[job_no % RING][:, :].rearrange("p (k n) -> p k n", k=4)[:, :, 0:rows(i)],
                                  hi.bitcast(F32), ALU.subtract).then_inc(x_low, 1)
            dve.wait_ge(square_in, 16)
            dve.wait_ge(const_in, 16 * 5)
            for job in idx_jobs:
                _, i, h, c = job
                r = idx_no[job]
                wd = min(512, widths[i] - 512 * c)
                cols = slice(512 * c, 512 * c + wd)
                dve.wait_ge(freed, pos[job] + 1)
                src = relu[:, r % 4, 0:wd]
                w = iw[:, i, h:h + 1]
                if h == 0:
                    dve.tensor_scalar(score[i][:, cols], src, w, None, ALU.mult).then_inc(scored, 1)
                else:
                    dve.wait_ge(scored, idx_no["idx", i, h - 1, c] + 1)
                    dve.scalar_tensor_tensor(out=score[i][:, cols], in0=src, scalar=w, in1=score[i][:, cols],
                                             op0=ALU.mult, op1=ALU.add).then_inc(scored, 1)
                if h == AH - 1 and 512 * c + wd == widths[i]:
                    dve.wait_ge(scored, r + 1)
                    diag = score[i][:, widths[i] - P:widths[i]]
                    dve.tensor_tensor(diag, diag, causal, ALU.add).then_inc(causal_done, 1)
            dve.wait_ge(causal_done, n_sparse)
            dve.wait_ge(freed, pos["scd",] + 1)
            sd, m8d = scd[0:SMP, :], m8[0:SMP, 24:32]
            dve.tensor_tensor(sd[:, PAST:SC_W], sd[:, PAST:SC_W], new_mask, ALU.add).then_inc(topk_step, 1)
            dve.sem_inc(topk_step, 3)
            step = 4
            dve.wait_ge(topk_step, step)

            def rounds(count, streams):
                nonlocal step
                n = len(streams)
                with dve.Fori(0, count) as rnd:
                    for u, (best, row) in enumerate(streams):
                        dve.wait_ge(topk_step, rnd * (2 * n) + (step + u + 1 - n))
                        dve.sem_inc(topk_turn, 1)
                        dve.max(best, row).then_inc(topk_step, 1)
                    for u, (best, row) in enumerate(streams):
                        dve.wait_ge(topk_step, rnd * (2 * n) + (step + 1 + u))
                        dve.sem_inc(topk_turn, 1)
                        dve.match_replace(row, best, row, TAKEN).then_inc(topk_step, 1)
                step += 2 * n * count

            for a in range(FIRST_SPARSE, TILES - 1, 3):
                streams = [(m8[:, 8 * u:8 * u + 8], score[a + u]) for u in range(3)]
                with_samples = TOPK_S // 8 if a == FIRST_SPARSE else 0
                if with_samples:
                    rounds(with_samples, streams + [(m8d, sd)])
                rounds(TOPK // 8 - with_samples, streams)
            dve.wait_ge(topk_step, step)
            for i in range(FIRST_SPARSE, TILES - 1):
                dve.tensor_scalar(score[i], score[i], -2e38, NEG, ALU.is_gt, ALU.mult).then_inc(masks_done, 1)
            one_more = m8[0:SMP, 0:8]
            dve.memset(one_more, TAKEN).then_inc(topk_step, 1)
            step += 1
            dve.max(m8d, sd).then_inc(topk_step, 1)
            dve.wait_ge(topk_step, step + 1)
            dve.tensor_copy(one_more[:, 0:1], m8d[:, 0:1]).then_inc(topk_step, 1)
            dve.wait_ge(topk_step, step + 2)
            dve.match_replace(sd, one_more, sd, TAKEN).then_inc(topk_step, 1)
            dve.wait_ge(topk_step, step + 3)
            dve.tensor_scalar(sd, sd, -2e38, NEG, ALU.is_gt, ALU.mult).then_inc(masks_done, 1)
            dve_rest(dve)


_INS = ['x_prompt', 'x_sample', 'cache_k', 'cache_v', 'cache_kidx', 'state_C', 'state_n', 'state_m', 'page_table',
        'w_in', 'b_gate', 'w_out', 'ln1_g', 'ln1_b', 'w_gate', 'w_up', 'w_down', 'ln2_g', 'ln2_b']
_OUTS = [(1, SEQ, D), (NB, NT, D), (1, 1, SEQ, AH, AD), (1, 1, SEQ, AH, AD), (1, 1, SEQ, IDX_D),
         (1, 1, MH, P, P), (1, 1, MH, P), (1, 1, MH),
         (1, NB, NT, AH, AD), (1, NB, NT, AH, AD), (1, NB, NT, IDX_D), (1, NB, MH, P, P), (1, NB, MH, P), (1, NB, MH)]
_SCRATCH = [(T, 512), (SMP, AH), (3, MH, P, T)]


def shape_constants():
    import numpy as np
    f = np.float32
    r = np.arange(P)
    square = np.zeros((P, 6, P), f)
    square[:, 0] = np.eye(P)
    square[:, 1] = np.where(r[None, :] <= r[:, None], 0, NEG)
    square[:, 2] = np.where(r[:, None] <= r[None, :], 0, NEG)
    square[:, 3] = 1
    bt = np.arange(SMP)
    for g in range(2):
        square[bt, 4 + g] = ((bt // NT)[:, None] == 4 * g + (r // 32)[None, :]) & ((bt % NT)[:, None] == (r % NT)[None, :])
    half = AD // 4 // 2
    pos = np.zeros((TILES, P), f)
    pos[:LAST] = np.arange(SEQ).reshape(LAST, P)
    pos[LAST] = PAST + r % NT
    inv = f(500000.0) ** (-(np.arange(half, dtype=f) / f(half)))
    ang = pos[:, :, None] * inv
    cos, sin = np.cos(ang), np.sin(ang)
    rope = np.stack([np.concatenate([cos, cos], -1), np.concatenate([-sin, sin], -1)], 2)
    small = np.zeros((P, 64 + 2 * SMP), f)
    small[:, 0:64] = square[0:SMP, 4:6].transpose(2, 1, 0).reshape(P, 64)
    own = ((bt // NT)[:, None] == (bt // NT)[None, :]) & (bt[None, :] <= bt[:, None])
    small[0:SMP, 64:96] = np.where(own, 0, NEG)
    small[0:SMP, 96:128] = np.where(own.T, 0, NEG)
    first = np.ones(T, f)
    first[0:SEQ:P] = 0
    first[SEQ:T:NT] = 0
    rows_ = np.concatenate([np.tile(first, (MH, 1)), np.repeat(np.eye(MH, dtype=f), P, axis=1)], 1)
    return [square.reshape(P, -1), np.ascontiguousarray(rope.transpose(1, 0, 2, 3)).reshape(P, -1), small,
            rows_.astype(f)]


def kernel(**inputs):
    import numpy as _np
    import concourse.bacc as _bacc
    from concourse import mybir as _mybir
    from concourse.bass_utils import run_bass_kernel_spmd as _run

    nc = _bacc.Bacc("TRN2", target_bir_lowering=False, num_devices=1)
    arrays, args = {}, []
    given = [(name, _np.ascontiguousarray(inputs[name])) for name in _INS]
    given += [(f"shape_constant_{n}", _np.ascontiguousarray(a)) for n, a in enumerate(shape_constants())]
    for name, a in given:
        arrays[f"in_{name}_dram"] = a
        args.append(nc.dram_tensor(f"in_{name}_dram", a.shape, _mybir.dt.from_np(a.dtype), kind="ExternalInput").ap())
    for i, shape in enumerate(_OUTS):
        args.append(nc.dram_tensor(f"out_{i}_dram", shape, F32, kind="ExternalOutput").ap())
    for i, shape in enumerate(_SCRATCH):
        args.append(nc.dram_tensor(f"scratch_{i}_dram", shape, F32, kind="Internal").ap())
    build(nc, *args)
    r = _run(nc, [arrays], core_ids=[0])
    return tuple(r.results[0][f"out_{i}_dram"] for i in range(len(_OUTS)))
```
